# Optimizing a Trainium2 kernel written in Bass

```python
import math
import jax, jax.numpy as jnp
from jax import lax
import numpy as np

D_MODEL = 1024
BATCH = 1
SEQ = 1024
DEPTH = 1
DEC_BATCH = 8
DEC_SEQ = 1
PAST_LEN = 1024
PAGE_SIZE = 128

MIX_A = D_MODEL // 2
H_A = 4
HD_A = MIX_A // H_A
MIX_B = D_MODEL - MIX_A
H_B = 4
DK_B = MIX_B // H_B
DV_B = MIX_B // H_B
MIX_W = MIX_A + MIX_B
CONV_W = 4
CONV_DIM = 2 * H_B * DK_B + H_B * DV_B
GDN_CHUNK = 64
Q_BLOCK = 128
D_FF = 4 * D_MODEL
RMS_EPS = 1e-6
L2_EPS = 1e-6
FGATE_BIAS_MEAN = 2.0
COL_SIZES = (MIX_A, MIX_A, MIX_A, H_A, CONV_DIM, MIX_B, H_B, H_B)
IN_DIM = sum(COL_SIZES)

kernel_name = 'hymba_fox_gdn_decode_step'

def rmsnorm(x, w):
    xf = x.astype(jnp.float32)
    y = xf * lax.rsqrt(jnp.mean(xf * xf, axis=-1, keepdims=True) + RMS_EPS)
    return (y * w.astype(jnp.float32)).astype(x.dtype)

def l2norm(x):
    xf = x.astype(jnp.float32)
    return xf * lax.rsqrt(jnp.sum(xf * xf, axis=-1, keepdims=True) + L2_EPS)

def split_cols(p):
    idx = [int(i) for i in np.cumsum(COL_SIZES)[:-1]]
    return jnp.split(p, idx, axis=-1)

def mixer_inputs(x, ln1, w_in, b_f, a_log, dt_bias):
    B, L = x.shape[0], x.shape[1]
    h = rmsnorm(x, ln1)
    qa, ka, va, fa, qkv_b, z, bb, aa = split_cols(h @ w_in)
    q = qa.reshape(B, L, H_A, HD_A)
    k = ka.reshape(B, L, H_A, HD_A)
    v = va.reshape(B, L, H_A, HD_A)
    lf = jax.nn.log_sigmoid((fa + b_f).astype(jnp.float32))
    beta = jax.nn.sigmoid(bb.astype(jnp.float32))
    g = -jnp.exp(a_log.astype(jnp.float32)) * jax.nn.softplus(
        aa.astype(jnp.float32) + dt_bias.astype(jnp.float32))
    return q, k, v, lf, qkv_b, z, beta, g

def fox_attend(q, k, v, dq, dk, q_pos, k_pos):
    s = jnp.einsum('bqhd,bkhd->bhqk', q, k).astype(jnp.float32) * (HD_A ** -0.5)
    bias = jnp.swapaxes(dq, 1, 2)[:, :, :, None] - jnp.swapaxes(dk, 1, 2)[:, :, None, :]
    causal = k_pos[None, :] <= q_pos[:, None]
    s = jnp.where(causal, s + bias, -jnp.inf)
    p = jax.nn.softmax(s, axis=-1)
    return jnp.einsum('bhqk,bkhd->bqhd', p.astype(v.dtype), v)

def fox_prompt(q, k, v, dcum):
    B, L = q.shape[0], q.shape[1]
    nq = L // Q_BLOCK
    qb = jnp.swapaxes(q.reshape(B, nq, Q_BLOCK, H_A, HD_A), 0, 1)
    db = jnp.swapaxes(dcum.reshape(B, nq, Q_BLOCK, H_A), 0, 1)
    starts = jnp.arange(nq, dtype=jnp.int32) * Q_BLOCK
    k_pos = jnp.arange(L, dtype=jnp.int32)

    def block(args):
        qi, di, st = args
        return fox_attend(qi, k, v, di, dcum, st + jnp.arange(Q_BLOCK, dtype=jnp.int32), k_pos)

    o = lax.map(block, (qb, db, starts))
    return jnp.swapaxes(o, 0, 1).reshape(B, L, H_A, HD_A)

def short_conv(xp, w):
    L = xp.shape[1] - (CONV_W - 1)
    acc = xp[:, 0:L] * w[0]
    for i in range(1, CONV_W):
        acc = acc + xp[:, i:i + L] * w[i]
    return jax.nn.silu(acc)

def gdn_qkv(conv_in, w_conv):
    B = conv_in.shape[0]
    c = short_conv(conv_in, w_conv).astype(jnp.float32)
    L = c.shape[1]
    qb, kb, vb = jnp.split(c, [H_B * DK_B, 2 * H_B * DK_B], axis=-1)
    q = l2norm(qb.reshape(B, L, H_B, DK_B))
    k = l2norm(kb.reshape(B, L, H_B, DK_B))
    v = vb.reshape(B, L, H_B, DV_B)
    return q, k, v

def gdn_chunked(q, k, v, g, beta, s0):
    B, L = q.shape[0], q.shape[1]
    C = GDN_CHUNK
    N = L // C

    def blk(t):
        return jnp.moveaxis(t.reshape((B, N, C) + t.shape[2:]), 3, 1)

    q = blk(q) * (DK_B ** -0.5)
    k = blk(k)
    v = blk(v)
    gc = jnp.cumsum(blk(g), axis=-1)
    bt = blk(beta)
    incl = jnp.tril(jnp.ones((C, C), dtype=bool))
    strict = jnp.tril(jnp.ones((C, C), dtype=bool), -1)
    decay = jnp.exp(jnp.where(incl, gc[..., :, None] - gc[..., None, :], -jnp.inf))
    kk = jnp.einsum('bhnid,bhnjd->bhnij', k, k)
    a = jnp.eye(C, dtype=jnp.float32) + jnp.where(strict, bt[..., :, None] * kk * decay, 0.0)
    rhs = jnp.concatenate([v * bt[..., None], k * (bt * jnp.exp(gc))[..., None]], axis=-1)
    sol = lax.linalg.triangular_solve(a, rhs, left_side=True, lower=True, unit_diagonal=True)
    u, w = sol[..., :DV_B], sol[..., DV_B:]
    qk = jnp.where(incl, jnp.einsum('bhnid,bhnjd->bhnij', q, k) * decay, 0.0)
    qg = q * jnp.exp(gc)[..., None]
    kg = k * jnp.exp(gc[..., -1:] - gc)[..., None]
    gl = jnp.exp(gc[..., -1])

    def step(S, xs):
        u_n, w_n, qk_n, qg_n, kg_n, gl_n = xs
        v_new = u_n - jnp.einsum('bhcd,bhde->bhce', w_n, S)
        o = jnp.einsum('bhcd,bhde->bhce', qg_n, S) + jnp.einsum('bhcs,bhse->bhce', qk_n, v_new)
        S = S * gl_n[..., None, None] + jnp.einsum('bhcd,bhce->bhde', kg_n, v_new)
        return S, o

    xs = tuple(jnp.moveaxis(t, 2, 0) for t in (u, w, qk, qg, kg, gl))
    s_fin, o = lax.scan(step, s0, xs)
    o = jnp.moveaxis(o, 0, 2)
    return jnp.moveaxis(o, 1, 3).reshape(B, L, H_B, DV_B), s_fin

def gdn_recurrent(q, k, v, g, beta, s0):
    q = q * (DK_B ** -0.5)

    def step(S, xs):
        q_t, k_t, v_t, g_t, b_t = xs
        S = S * jnp.exp(g_t)[..., None, None]
        delta = (v_t - jnp.einsum('bhd,bhde->bhe', k_t, S)) * b_t[..., None]
        S = S + jnp.einsum('bhd,bhe->bhde', k_t, delta)
        return S, jnp.einsum('bhd,bhde->bhe', q_t, S)

    xs = tuple(jnp.swapaxes(t, 0, 1) for t in (q, k, v, g, beta))
    s_fin, o = lax.scan(step, s0, xs)
    return jnp.swapaxes(o, 0, 1), s_fin

def layer_output(x, fo, go, z, w_gnorm, w_o, ln2, w_up, w_down):
    B, L = x.shape[0], x.shape[1]
    gz = z.reshape(B, L, H_B, DV_B).astype(jnp.float32)
    go = rmsnorm(go, w_gnorm) * jax.nn.silu(gz)
    mix = jnp.concatenate([fo.reshape(B, L, MIX_A).astype(x.dtype),
                           go.reshape(B, L, MIX_B).astype(x.dtype)], axis=-1)
    h = x + mix @ w_o
    u = jax.nn.relu(rmsnorm(h, ln2) @ w_up)
    return h + (u * u) @ w_down

def prompt_layer(x, ln1, w_in, b_f, w_conv, a_log, dt_bias, w_gnorm, w_o, ln2, w_up, w_down):
    B = x.shape[0]
    q, k, v, lf, qkv_b, z, beta, g = mixer_inputs(x, ln1, w_in, b_f, a_log, dt_bias)
    dcum = jnp.cumsum(lf, axis=1)
    fo = fox_prompt(q, k, v, dcum)
    conv_in = jnp.concatenate([jnp.zeros((B, CONV_W - 1, CONV_DIM), qkv_b.dtype), qkv_b], axis=1)
    qg, kg, vg = gdn_qkv(conv_in, w_conv)
    s0 = jnp.zeros((B, H_B, DK_B, DV_B), jnp.float32)
    go, s_fin = gdn_chunked(qg, kg, vg, g, beta, s0)
    y = layer_output(x, fo, go, z, w_gnorm, w_o, ln2, w_up, w_down)
    return y, k, v, lf.astype(x.dtype), conv_in[:, -(CONV_W - 1):], s_fin.astype(x.dtype)

def sample_layer(x, ck, cv, clf, page_table, conv_state, ssm_state,
                 ln1, w_in, b_f, w_conv, a_log, dt_bias, w_gnorm, w_o, ln2, w_up, w_down):
    DB, T = x.shape[0], x.shape[1]
    P = page_table.shape[1] * ck.shape[1]
    q, k, v, lf, qkv_b, z, beta, g = mixer_inputs(x, ln1, w_in, b_f, a_log, dt_bias)
    k_all = jnp.concatenate([ck[page_table].reshape(DB, P, H_A, HD_A).astype(k.dtype), k], axis=1)
    v_all = jnp.concatenate([cv[page_table].reshape(DB, P, H_A, HD_A).astype(v.dtype), v], axis=1)
    lf_all = jnp.concatenate([clf[page_table].reshape(DB, P, H_A).astype(jnp.float32), lf], axis=1)
    d_all = jnp.cumsum(lf_all, axis=1)
    q_pos = P + jnp.arange(T, dtype=jnp.int32)
    k_pos = jnp.arange(P + T, dtype=jnp.int32)
    fo = fox_attend(q, k_all, v_all, d_all[:, P:], d_all, q_pos, k_pos)
    conv_in = jnp.concatenate([conv_state.astype(qkv_b.dtype), qkv_b], axis=1)
    qg, kg, vg = gdn_qkv(conv_in, w_conv)
    go, s_fin = gdn_recurrent(qg, kg, vg, g, beta, ssm_state.astype(jnp.float32))
    y = layer_output(x, fo, go, z, w_gnorm, w_o, ln2, w_up, w_down)
    return (y, k.astype(ck.dtype), v.astype(cv.dtype), lf.astype(clf.dtype),
            conv_in[:, -(CONV_W - 1):].astype(conv_state.dtype), s_fin.astype(ssm_state.dtype))

def setup_inputs(seed: int = 0) -> dict:
    key = jax.random.key(seed)
    ks = jax.random.split(key, 24)
    f32 = jnp.float32
    n_pages = PAST_LEN // PAGE_SIZE
    used = DEC_BATCH * n_pages
    n_phys = used + max(1, used // 4)

    def nrm(k, shape, scale=1.0):
        return jax.random.normal(k, shape, f32) * scale

    x_prompt = nrm(ks[0], (BATCH, SEQ, D_MODEL))
    x_sample = nrm(ks[1], (DEC_BATCH, DEC_SEQ, D_MODEL))
    cache_k = nrm(ks[2], (DEPTH, n_phys, PAGE_SIZE, H_A, HD_A))
    cache_v = nrm(ks[3], (DEPTH, n_phys, PAGE_SIZE, H_A, HD_A))
    cache_lf = jax.nn.log_sigmoid(nrm(ks[4], (DEPTH, n_phys, PAGE_SIZE, H_A)) + FGATE_BIAS_MEAN)
    page_table = jax.random.permutation(ks[5], n_phys)[:used].reshape(DEC_BATCH, n_pages).astype(jnp.int32)
    state_conv = nrm(ks[6], (DEPTH, DEC_BATCH, CONV_W - 1, CONV_DIM))
    state_ssm = nrm(ks[7], (DEPTH, DEC_BATCH, H_B, DK_B, DV_B), 0.1)
    ln1 = 1.0 + nrm(ks[8], (DEPTH, D_MODEL), 0.02)
    w_in = nrm(ks[9], (DEPTH, D_MODEL, IN_DIM), D_MODEL ** -0.5)
    b_f = FGATE_BIAS_MEAN + nrm(ks[10], (DEPTH, H_A), 0.1)
    w_conv = nrm(ks[11], (DEPTH, CONV_W, CONV_DIM), CONV_W ** -0.5)
    a_log = jnp.log(jax.random.uniform(ks[12], (DEPTH, H_B), f32, 1.0, 16.0))
    dt = jnp.exp(jax.random.uniform(ks[13], (DEPTH, H_B), f32, math.log(1e-3), math.log(1e-1)))
    dt_bias = dt + jnp.log(-jnp.expm1(-dt))
    w_gnorm = 1.0 + nrm(ks[14], (DEPTH, DV_B), 0.02)
    w_o = nrm(ks[15], (DEPTH, MIX_W, D_MODEL), MIX_W ** -0.5)
    ln2 = 1.0 + nrm(ks[16], (DEPTH, D_MODEL), 0.02)
    w_up = nrm(ks[17], (DEPTH, D_MODEL, D_FF), D_MODEL ** -0.5)
    w_down = nrm(ks[18], (DEPTH, D_FF, D_MODEL), D_FF ** -0.5)
    ln_f = 1.0 + nrm(ks[19], (D_MODEL,), 0.02)
    return {'x_prompt': x_prompt, 'x_sample': x_sample, 'cache_k': cache_k, 'cache_v': cache_v,
            'cache_lf': cache_lf, 'page_table': page_table, 'state_conv': state_conv,
            'state_ssm': state_ssm, 'ln1': ln1, 'w_in': w_in, 'b_f': b_f, 'w_conv': w_conv,
            'a_log': a_log, 'dt_bias': dt_bias, 'w_gnorm': w_gnorm, 'w_o': w_o, 'ln2': ln2,
            'w_up': w_up, 'w_down': w_down, 'ln_f': ln_f}

def reference(x_prompt, x_sample, cache_k, cache_v, cache_lf, page_table, state_conv, state_ssm,
              ln1, w_in, b_f, w_conv, a_log, dt_bias, w_gnorm, w_o, ln2, w_up, w_down, ln_f):
    yp, ys = x_prompt, x_sample
    pk, pv, plf, pconv, pssm = [], [], [], [], []
    sk, sv, slf, sconv, sssm = [], [], [], [], []
    for l in range(DEPTH):
        lw = (ln1[l], w_in[l], b_f[l], w_conv[l], a_log[l], dt_bias[l], w_gnorm[l],
              w_o[l], ln2[l], w_up[l], w_down[l])
        yp, k1, v1, lf1, c1, s1 = prompt_layer(yp, *lw)
        ys, k2, v2, lf2, c2, s2 = sample_layer(ys, cache_k[l], cache_v[l], cache_lf[l], page_table,
                                               state_conv[l], state_ssm[l], *lw)
        pk.append(k1); pv.append(v1); plf.append(lf1); pconv.append(c1); pssm.append(s1)
        sk.append(k2); sv.append(v2); slf.append(lf2); sconv.append(c2); sssm.append(s2)
    y_prompt = rmsnorm(yp, ln_f)
    y_sample = rmsnorm(ys, ln_f)
    return (y_prompt, y_sample,
            jnp.stack(pk), jnp.stack(pv), jnp.stack(plf), jnp.stack(pconv), jnp.stack(pssm),
            jnp.stack(sk), jnp.stack(sv), jnp.stack(slf), jnp.stack(sconv), jnp.stack(sssm))


_drawn_inputs = setup_inputs


def setup_inputs(seed=0):
    import zlib

    import numpy as np

    out = dict(_drawn_inputs(seed))
    spreads = {}
    factors = {'w_gnorm': 6.428, 'ln2': 3.361, 'ln_f': 8.119, 'cache_lf': 2.705}
    for name, (base, spread) in spreads.items():
        noise = np.random.default_rng([zlib.crc32(name.encode()), seed]).standard_normal(out[name].shape)
        drawn = base * np.exp(spread * noise) if base else spread * noise
        out[name] = __import__('jax').numpy.asarray(drawn.astype(out[name].dtype))
    for name, factor in factors.items():
        out[name] = (out[name] * factor).astype(out[name].dtype)
    return out
```

```python
from contextlib import ExitStack

import concourse.bass as bass
from concourse import mybir

F32 = mybir.dt.float32
F32R = mybir.dt.float32r
I32 = mybir.dt.int32
ALU = mybir.AluOpType
ACT = mybir.ActivationFunctionType
AX = mybir.AxisListType

P = 128
SEQ = 1024
NB = 8
D = 1024
KT = D // P
NT = SEQ // P
TOK = SEQ + NB
G3 = TOK // 3
H = 4
HD = 128
MIX = 512
CONV = 3 * MIX
CW = 4
IN_DIM = 3596
FF = 4096
PAGE = 128
NPG = 8
EPS = 1e-6
SCALE = float(HD) ** -0.5
NEG = -1e30
LEVELS = 7
SBUF0 = 16640

C_QA, C_KA, C_VA, C_FA = 0, MIX, 2 * MIX, 3 * MIX
C_CV = 3 * MIX + H
C_Z = C_CV + CONV
C_BB = C_Z + MIX
C_AA = C_BB + H


def hymba_step(nc, x_prompt, x_sample, cache_k, cache_v, cache_lf, page_table, state_conv, state_ssm,
               ln1, w_in, b_f, w_conv, a_log, dt_bias, w_gnorm, w_o, ln2, w_up, w_down, ln_f,
               y_prompt, y_sample, k_prompt, v_prompt, lf_prompt, conv_prompt, ssm_prompt,
               k_sample, v_sample, lf_sample, conv_sample, ssm_sample):
    z_rows = nc.dram_tensor("z_rows", [SEQ, MIX], F32).ap()

    ctx = ExitStack()
    with ctx:
        def sem(name):
            return ctx.enter_context(nc.semaphore(name))

        def place(name, shape, at, dt=F32):
            return nc.alloc_sbuf_tensor_at(name, shape, dt, offset=SBUF0 + at)

        ctx.enter_context(nc.sbuf_tensor("fence", [P, 53000], F32))
        PS = ctx.enter_context(nc.psum_tensor("PS", [P, 8, 512], F32))

        ident = place("ident", [P, P], 0)
        ones = place("ones", [P, P], 512)
        incl = place("incl", [P, P], 1024)
        strict = place("strict", [P, P], 1536)
        stat = place("stat", [P, 64], 2048)
        gN = place("gN", [P, NT + 1, 72], 2304)
        act_hi = place("act_hi", [P, KT, TOK], 5120, F32R)
        act_lo = place("act_lo", [P, KT, TOK], 38144, F32R)

        w_raw = place("w_raw", [P, 2, KT, P], 71168)
        w_hi = place("w_hi", [P, 2, KT, P], 79360, F32R)
        w_lo = place("w_lo", [P, 2, KT, P], 87552, F32R)
        kT = place("kT", [P, H, TOK], 95744)
        qT = place("qT", [P, H, TOK], 112256)
        cT = place("cT", [P, 12, TOK], 128768)
        gateT = place("gateT", [P, TOK], 178304)
        cb = place("cb", [P, 2, 1040], 182432)
        acc = place("acc", [P, TOK], 190752)
        nat = place("nat", [P, 2, NT, P], 194880)
        tail = place("tail", [P, 12, 11], 203072)
        vzS = place("vzS", [P, 8, NB], 203616)
        hw = place("hw", [P, 12, 28], 203872)
        hrows = place("hrows", [28, CONV], 194880)
        x_t = place("x_t", [P, 3, D], 128768)
        xn = place("xn", [P, 2, D], 141056)
        lnb = place("lnb", [P, D], 149248)
        junk = place("junk", [P, D], 153344)

        pe_once = sem("pe_once")
        (HW_T, CT_T, GN_T, SN_T, CLF_T, BIAS_T, DN_T, A_SPREAD, PRED_READY, SO_READY, SMT_READY, MX_T,
        M_SPREAD, SUM_SPREAD, DVT_READY) = range(1, 16)
        dve_once = sem("dve_once")
        (CT_READY, GATE_MIN, GATE_ABS, T1_READY, SN_READY, CLF_READY, BEK_READY, DN_READY, SM_READY,
        SMLO_READY, MX_READY, MD_READY, SJ_READY, PD_READY, DOLO_READY) = range(1, 16)
        act_once = sem("act_once")
        (EN_READY, A_READY, A_ALL_READY, SORS_READY, SMHI_READY, DOHI_READY) = range(1, 7)
        pool_once = sem("pool_once")
        (EPS_READY, GATE_ZERO, PAD_ZERO, BIAS_ZERO, AD_READY) = range(1, 6)

        consts = sem("consts")
        ln_in = sem("ln_in")
        std_ready = sem("std_ready")
        x_in = [sem(f"x_in{i}") for i in range(3)]
        xn_ready = sem("xn_ready")
        xt_ready = sem("xt_ready")
        act_hi_ready = sem("act_hi_ready")
        act_lo_ready = sem("act_lo_ready")
        hist_in = sem("hist_in")
        w_in_sem = [sem(f"w_raw{i}") for i in range(2)]
        w_hi_ready = sem("w_hi_ready")
        w_lo_ready = sem("w_lo_ready")
        block_done = sem("block_done")
        evacuated = sem("evacuated")
        dve_step = sem("dve_step")
        act_step = sem("act_step")
        conv_ready = sem("conv_ready")
        silu_done = sem("silu_done")
        cb_free = sem("cb_free")
        nat_t = sem("nat_t")
        nat_ready = sem("nat_ready")
        nat_out = [sem(f"nat_out{i}") for i in range(2)]
        out_done = sem("out_done")


        lm = place("lm", [P, LEVELS + 1, P], 205216)
        T1 = place("T1", [P, TOK], 71168)
        ge = place("ge", [P, TOK], 75296)
        gs = place("gs", [P, TOK], 79424)
        cm = place("cm", [P, SEQ], 83552)
        sq = place("sq", [P, 2, TOK], 182432)
        rn = place("rn", [P, 2, TOK], 190688)
        small = place("small", [P, 320], 211360)
        wgn = place("wgn", [P, P], 203872)

        def tiles(name, slots):
            return [place(f"{name}{i}", [P, H, P], at) for i, at in enumerate(slots)]

        low = [75296 + 2048 * i for i in range(9)]
        high = [178304 + 2048 * i for i in range(12)]
        DEC = tiles("DEC", low[0:2])
        LL = tiles("LL", low[2:4])
        LT = tiles("LT", low[4:6])
        QKD = tiles("QKD", low[6:8])
        QKT = tiles("QKT", [low[8], high[0]])
        XX = tiles("XX", high[1:3])
        XT = tiles("XT", high[3:5])
        RK = tiles("RK", high[5:7])
        KG = tiles("KG", high[7:9])
        QG = tiles("QG", high[9:11])
        SG, ST = tiles("SG", [high[11]])[0], tiles("ST", [209312])[0]
        BV, WT, VN = QKD, XX, DEC
        E_N, B_EK = small[:, 0:32].rearrange("p (c h) -> p c h", h=H), small[:, 32:64].rearrange("p (c h) -> p c h", h=H)

        def sm(s, i):
            return small[:, 64 + 32 * s + 4 * i:68 + 32 * s + 4 * i]
        GLC, KGS, EL, OSS, OLN, ORS = range(6)

        bias_in = sem("bias_in")
        wgn_in = sem("wgn_in")
        masks = sem("masks")
        t1_zero = sem("t1_zero")
        gate_act = sem("gate_act")
        gn_ready = sem("gn_ready")
        sq_ready = sem("sq_ready")
        ss_ready = sem("ss_ready")
        sd_ready = sem("sd_ready")
        normed = sem("normed")

        gb_ready = sem("gb_ready")
        kk_ready = sem("kk_ready")
        dif_ready = sem("dif_ready")
        eg_ready = sem("eg_ready")
        dmax_ready = sem("dmax_ready")
        dexp_ready = sem("dexp_ready")
        dec_ready = sem("dec_ready")
        kks_ready = sem("kks_ready")
        l_ready = sem("l_ready")
        qkd_ready = sem("qkd_ready")
        lt_t = sem("lt_t")
        lt_ready = sem("lt_ready")
        qkt_ready = sem("qkt_ready")
        x_step = sem("x_step")
        x0_ready = sem("x0_ready")
        bv_ready = sem("bv_ready")
        kn_ready = sem("kn_ready")
        rk_ready = sem("rk_ready")
        y_ready = sem("y_ready")
        ym_ready = sem("ym_ready")
        z_ready = sem("z_ready")
        x_ready = sem("x_ready")
        wt_t = sem("wt_t")
        wt_ready = sem("wt_ready")
        qg_ready = sem("qg_ready")
        sg_ready = sem("sg_ready")
        u_ready = sem("u_ready")
        vn_ready = sem("vn_ready")
        o_ready = sem("o_ready")
        s_add = sem("s_add")
        s_ready = sem("s_ready")
        ors_ready = sem("ors_ready")
        og_ready = sem("og_ready")
        z_in = [sem(f"z_in{i}") for i in range(2)]
        m_ready = sem("m_ready")
        mt_ready = sem("mt_ready")
        mhi_ready = sem("mhi_ready")
        mlo_ready = sem("mlo_ready")

        def chunk(c):
            return slice(c * P, (c + 1) * P)

        def heads(b):
            return PS[:, b, :].rearrange("p (h d) -> p h d", h=H)

        def per_head(ap):
            return ap.unsqueeze(2).to_broadcast([ap.shape[0], H, P])

        def over_heads(ap):
            return ap.unsqueeze(1).to_broadcast([P, H, P])

        def level_seq(c, l):
            return (c // 2) * 12 + (l - 1) * 2 + c % 2 + 1

        ct = place("ct", [11, 12, P], 87680)
        S_s = place("S_s", [P, NB * H, P], 75296)
        dlt = place("dlt", [NB, H, P], 91680)
        msk = place("msk", [P, H, NB, NB], 93728)
        dmk = place("dmk", [NB, H, NB, P], 178304)
        dN = place("dN", [NB, 16, P], 194688)
        m8 = small[:, 200:264].rearrange("p (a b) -> p a b", b=NB)
        a_row = small[0:NB, 264:268]
        a_diag = small[0:NB, 128:160].rearrange("p (b h) -> p b h", h=H)
        a_all = small[:, 160:192]
        s_oss, s_oln, s_ors = small[0:NB, 268:272], small[0:NB, 272:276], small[0:NB, 276:280]

        ct_out = sem("ct_out")
        m8_ready = sem("m8_ready")
        st_in = sem("st_in")
        msk_ready = sem("msk_ready")
        dmk_ready = sem("dmk_ready")
        outer_ready = sem("outer_ready")
        st_ready = sem("st_ready")

        Db = place("Db", [P, H, SEQ], 128768)
        vN = place("vN", [P, NT, MIX], 145152)
        sc = place("sc", [P, 2, SEQ], 161536)
        pT = place("pT", [P, 2, NT, P], 169728)
        oN = place("oN", [P, 2, H, P], 178304)
        arow = place("arow", [P, 3, NT * H], 182400)
        neg = lm[:, 0, :]

        v_in = sem("v_in")
        d_spread = sem("d_spread")
        db_ready = sem("db_ready")
        qk_ready = sem("qk_ready")
        sc_step = sem("sc_step")
        max_ready = sem("max_ready")
        p_ready = sem("p_ready")
        pt_t = sem("pt_t")
        pt_ready = sem("pt_ready")
        pv_ready = sem("pv_ready")
        on_ready = sem("on_ready")
        ot_ready = sem("ot_ready")
        othi_ready = sem("othi_ready")
        otlo_ready = sem("otlo_ready")
        NAI = NT * H

        NR, NV = 7, 16
        kpages = place("kpages", [P, NR, MIX], 38144)
        qb = place("qb", [P, NB, MIX], 5120)
        sfx = place("sfx", [P, NB, NPG, H], 52480)
        s9 = place("s9", [P, NB, H, NPG], 53504)
        lf_rows = place("lf_rows", [NB * NPG, PAGE * H], 209312)
        clf = place("clf", [P, NB, NPG, H], 75296)
        pre = place("pre", [P, 256], 76320)
        sN = place("sN", [NB, 12, P], 196736)
        run_ = pre[:, 0:32].rearrange("p (b h) -> p b h", h=H)
        lf_diag = pre[0:NB, 32:64].rearrange("p (b h) -> p b h", h=H)
        self_diag = pre[0:NB, 64:96].rearrange("p (b h) -> p b h", h=H)
        self_s = pre[0:NB, 96:100]
        self_sc = small[:, 280:312]
        prod = place("prod", [NB, P], 77344)

        vpages = [place(f"vpages{i}", [P, 8, MIX], at) for i, at in enumerate((75296, 184320))]
        av = [place(f"av{i}", [P, MIX], at) for i, at in enumerate((71168, 73216, 205728))]
        dv = place("dv", [NB, MIX], 200704)
        pp = place("pp", [P, NB, H, NPG], 91680)
        dm_ = place("dm_", [P, 512], 92704)
        mx = dm_[:, 32:64]
        m_all = dm_[:, 64:96]
        self_e = dm_[:, 96:128]
        sj = dm_[:, 128:160]
        inv = dm_[:, 160:192]
        p_diag = dm_[0:NB, 256:288].rearrange("p (h b) -> p h b", b=NB)
        self_p = dm_[0:NB, 296:300]
        mcol = dm_[0:32, 292:293]
        mdiag = dm_[0:32, 320:352]

        table = place("table", [NB, NPG], 4896, I32)

        table_in = sem("table_in")
        kpage_in = [sem(f"kpage_in{i}") for i in range(NR)]
        vpage_in = [sem(f"vpage_in{i}") for i in range(2)]
        clf_in = sem("clf_in")
        sn_out = sem("sn_out")
        qb_t = sem("qb_t")
        qb_ready = sem("qb_ready")
        k_used = sem("k_used")
        v_used = sem("v_used")
        pv_made = sem("pv_made")
        dv_t = sem("dv_t")
        dv_ready = sem("dv_ready")
        diag_ready = sem("diag_ready")
        pre_read = sem("pre_read")
        sh_ready = sem("sh_ready")
        e_ready = sem("e_ready")

        def burst_of(b):
            return min(b, NT - 2)

        def vpage(n):
            return vpages[n % NV // 8][:, n % 8, :]

        wo_hi = place("wo_hi", [P, KT, D], 71168, F32R)
        wo_lo = place("wo_lo", [P, KT, D], 103936, F32R)
        x_r = place("x_r", [P, 2, D], 136704)
        xm = place("xm", [P, 2, D], 144896)
        ln2b = place("ln2b", [P, D], 206592)
        NG, GB = 8, 4
        u_hi = place("u_hi", [P, GB, TOK], 71168, F32R)
        u_lo = place("u_lo", [P, GB, TOK], 87680, F32R)
        wu_hi = place("wu_hi", [P, 2, KT, P], 104192, F32R)
        wu_lo = place("wu_lo", [P, 2, KT, P], 112384, F32R)
        wd_hi = place("wd_hi", [P, GB, D], 120576, F32R)
        wd_lo = place("wd_lo", [P, GB, D], 136960, F32R)
        raw = place("raw", [P, 4, D], 153344)
        y = place("y", [P, NT + 1, D], 169728)
        r_sq = place("r_sq", [P, TOK], 206592)
        lnfb = place("lnfb", [P, D], 104192)
        junk2 = place("junk2", [P, D], 112384)

        ln2_in = sem("ln2_in")
        raw_in = [sem(f"raw_in{i}") for i in range(4)]
        wo_hi_ready = sem("wo_hi_ready")
        wo_lo_ready = sem("wo_lo_ready")
        xr_in = [sem(f"xr_in{i}") for i in range(2)]
        h_t = sem("h_t")
        h_ready = sem("h_ready")
        std2_ready = sem("std2_ready")
        xm_ready = sem("xm_ready")
        xmt_ready = sem("xmt_ready")
        a2hi_ready = sem("a2hi_ready")
        a2lo_ready = sem("a2lo_ready")
        hi_done = sem("hi_done")
        lo_done = sem("lo_done")
        up_done = sem("up_done")
        relu_done = sem("relu_done")
        sq_done = sem("sq_done")
        u_hi_done = sem("u_hi_done")
        u_lo_done = sem("u_lo_done")
        dn_tile = sem("dn_tile")
        y_add = sem("y_add")
        lnf_in = sem("lnf_in")
        std3_ready = sem("std3_ready")
        out_ready = sem("out_ready")
        y_out = [sem(f"y_out{i}") for i in range(4)]
        NT9 = NT + 1
        up_v = w_up[0].rearrange("(kt p) (q c) -> q p kt c", p=P, c=P)
        dn_v = w_down[0].rearrange("(q p) n -> q p n", p=P)

        GATE, CV0, NAT0, Q0, NBLK = 0, 1, 13, 25, 29
        cols = [None] + [C_CV + i * P for i in range(12)] + [C_KA + i * P for i in range(4)] \
            + [C_VA + i * P for i in range(4)] + [C_Z + i * P for i in range(4)] + [C_QA + i * P for i in range(4)]

        def raw_count(n):
            return 48 + 16 * (n // 2) if n % 2 == 0 else 16 * (n // 2 + 1)

        def cb_use(n):
            return n - CV0 if CV0 <= n < NAT0 else n - 17 + 12 if 17 <= n < Q0 else None

        def nat_dst(i):
            h = i % 4
            rows = [k_prompt[0, 0, :, h, :], v_prompt[0, 0, :, h, :], z_rows[:, h * P:(h + 1) * P]][i // 4]
            return rows.rearrange("(t p) d -> p t d", p=P)

        def rows_of(t):
            return P if t < NT else NB

        block = ctx.enter_context(nc.Block())

        @block.sync
        def _(sp):
            def load_page(src, n):
                page = sp.value_load(table[n // NPG:n // NPG + 1, n % NPG:n % NPG + 1], min_val=0, max_val=cache_k.shape[1] - 1)
                return src[0, bass.ds(page, 1)]

            sp.dma_start(table[:, :], page_table[:, :]).then_inc(table_in, 16)

            sp.dma_start(lnb[:, :], ln1[0:1, :].to_broadcast([P, D])).then_inc(ln_in, 16)
            for t in range(NT + 1):
                if t >= 3:
                    sp.wait_ge(xn_ready, t - 2)
                src = x_prompt[0, t * P:(t + 1) * P, :] if t < NT else x_sample[:, 0, :]
                sp.dma_start(x_t[0:rows_of(t), t % 3, :], src).then_inc(x_in[t % 3], 16)
                if t == 0:
                    sp.dma_start(hrows[0:24, :], state_conv[0].rearrange("b i c -> (b i) c")).then_inc(hist_in, 16)
                    sp.dma_start(hrows[24:28, :], w_conv[0]).then_inc(hist_in, 16)
                if t == 2:
                    sp.wait_ge(pool_once, GATE_ZERO)
                    for row, c in ((0, C_FA), (32, C_BB), (64, C_AA)):
                        sp.dma_start(w_raw[:, 0, :, row:row + H],
                                     w_in[0, :, c:c + H].rearrange("(kt p) c -> p kt c", p=P)).then_inc(w_in_sem[0], 16)
            sp.dma_start(conv_sample[0, :, 0:2, :], state_conv[0, :, 1:3, :]).then_inc(out_done, 16)
            for n in range(1, NBLK):
                if n >= 2:
                    sp.wait_ge(w_lo_ready, n - 1)
                sp.dma_start(w_raw[:, n % 2, :, :],
                             w_in[0, :, cols[n]:cols[n] + P].rearrange("(kt p) c -> p kt c", p=P)).then_inc(w_in_sem[n % 2], 16)
                if n >= 4:
                    sp.wait_ge(table_in, 16)
                    for j in range(3 * (n - 4), min(3 * (n - 3), NB * NPG)):
                        sp.dma_start(lf_rows[j:j + 1, :], load_page(cache_lf, j).rearrange("a p h -> a (p h)")).then_inc(clf_in, 16)
                i = n - 3 - NAT0
                if 0 <= i < 12:
                    sp.wait_ge(nat_ready, i + 1)
                    sp.dma_start(nat_dst(i), nat[:, i % 2, :, :]).then_inc(nat_out[i % 2], 16)


            sp.wait_ge(dve_once, CT_READY)
            sp.dma_start(conv_prompt[0, 0, :, :], ct[0:3, :, :].rearrange("i c d -> i (c d)")).then_inc(ct_out, 16)
            sp.dma_start(conv_sample[0, :, 2, :], ct[3:11, :, :].rearrange("i c d -> i (c d)")).then_inc(ct_out, 16)
            sp.wait_ge(pool_once, BIAS_ZERO)
            sp.dma_start(stat[0:H, 50:51], b_f[0:1, :].rearrange("a h -> h a")).then_inc(bias_in, 16)
            sp.dma_start(stat[64:64 + H, 50:51], dt_bias[0:1, :].rearrange("a h -> h a")).then_inc(bias_in, 16)
            sp.dma_start(stat[64:64 + H, 51:52], a_log[0:1, :].rearrange("a h -> h a")).then_inc(bias_in, 16)
            sp.wait_ge(conv_ready, 12)
            sp.dma_start(wgn[:, :], w_gnorm[0:1, :].to_broadcast([P, P])).then_inc(wgn_in, 16)
            sp.wait_ge(gn_ready, 6)
            sp.dma_start(lf_prompt[0, 0, :, :].rearrange("(t p) h -> p t h", p=P), gN[:, 0:NT, 0:H]).then_inc(out_done, 16)
            sp.dma_start(lf_sample[0, :, 0, :], gN[0:NB, NT, 0:H]).then_inc(out_done, 16)
            sp.wait_ge(nat_out[0], 96)
            sp.wait_ge(nat_out[1], 96)
            sp.wait_ge(block_done, NBLK)
            for n in range(NR):
                sp.dma_start(kpages[:, n, :], load_page(cache_k, n).rearrange("a p h d -> (a p) (h d)")).then_inc(kpage_in[n], 16)
            sp.wait_ge(dve_once, SN_READY)
            sp.dma_start(k_sample[0, :, 0, :, :], sN[:, 4:8, :]).then_inc(sn_out, 16)
            sp.dma_start(v_sample[0, :, 0, :, :], sN[:, 8:12, :]).then_inc(sn_out, 16)
            for c in range(NT):
                if c % 2 == 0:
                    for n in range(max(NR, 16 * (c // 2)), 16 * (c // 2 + 1)):
                        sp.wait_ge(k_used, n - NR + 1)
                        sp.dma_start(kpages[:, n % NR, :], load_page(cache_k, n).rearrange("a p h d -> (a p) (h d)"))\
                            .then_inc(kpage_in[n % NR], 16)
                sp.wait_ge(x_ready, level_seq(c, 6))
                sp.dma_start(LT[c % 2][:, :, :], z_rows[chunk(c), :].rearrange("p (h d) -> p h d", h=H)).then_inc(z_in[c % 2], 16)
            sp.wait_ge(s_ready, NT)
            sp.dma_start(ssm_prompt[0, 0].rearrange("h d e -> d h e"), ST[:, :, :]).then_inc(out_done, 16)

            sp.wait_ge(m_ready, NT)
            sp.wait_ge(s_add, NT)
            sp.dma_start(S_s[:, :, :], state_ssm[0].rearrange("b h d e -> d (b h) e")).then_inc(st_in, 16)
            sp.wait_ge(st_ready, 8)
            sp.dma_start(ssm_sample[0].rearrange("b h d e -> d (b h) e"), S_s[:, :, :]).then_inc(out_done, 16)

            sp.wait_ge(pe_once, SO_READY)
            sp.wait_ge(msk_ready, 2 * H)
            sp.dma_start(vN[:, :, :], v_prompt[0, 0].rearrange("(t p) h d -> p t (h d)", p=P)).then_inc(v_in, 16)
            sp.wait_ge(pe_once, SMT_READY)
            for n in range(NB * NPG):
                if n >= NV:
                    sp.wait_ge(v_used, n - NV + 1)
                sp.dma_start(vpage(n), load_page(cache_v, n).rearrange("a p h d -> (a p) (h d)")).then_inc(vpage_in[n // NPG % 2], 16)

            sp.wait_ge(v_used, NB * NPG)
            sp.wait_ge(dve_once, DOLO_READY)
            sp.wait_ge(otlo_ready, NT)
            for k in range(KT):
                if k >= 4:
                    sp.wait_ge(wo_lo_ready, k - 3)
                sp.dma_start(raw[:, k % 4, :], w_o[0, k * P:(k + 1) * P, :]).then_inc(raw_in[k % 4], 16)
                if k == 0:
                    sp.dma_start(ln2b[:, :], ln2[0:1, :].to_broadcast([P, D])).then_inc(ln2_in, 16)
            for t in range(NT9):
                if t >= 2:
                    sp.wait_ge(h_ready, t - 1)
                src = x_prompt[0, t * P:(t + 1) * P, :] if t < NT else x_sample[:, 0, :]
                sp.dma_start(x_r[0:rows_of(t), t % 2, :], src).then_inc(xr_in[t % 2], 16)

            def load_up(q, slot):
                sp.dma_start(raw[:, slot, :].rearrange("p (kt c) -> p kt c", c=P),
                             up_v[bass.ds(q, 1), :, :, :].rearrange("a p kt c -> (a p) kt c")).then_inc(raw_in[slot], 16)

            def load_dn(q, slot):
                sp.dma_start(raw[:, slot, :], dn_v[bass.ds(q, 1), :, :].rearrange("a p n -> (a p) n")).then_inc(raw_in[slot], 16)

            sp.wait_ge(wo_lo_ready, KT)
            load_up(0, 0)
            load_up(1, 1)

            def sync_group(g, last):
                for k in range(GB):
                    sp.wait_ge(lo_done, 8 * g + 2 * k + 3)
                    load_dn(GB * g + k, (2 * k + 2) % 4)
                    if not (last and k >= 2):
                        sp.wait_ge(lo_done, 8 * g + 2 * k + 4)
                        load_up(GB * g + k + 2, (2 * k + 3) % 4)

            with sp.Fori(0, NG - 1) as g:
                sync_group(g, False)
            sync_group(NG - 1, True)
            sp.wait_ge(up_done, GB * NG + 2)
            sp.dma_start(lnfb[:, :], ln_f.rearrange("(a n) -> a n", a=1).to_broadcast([P, D])).then_inc(lnf_in, 16)
            for t in range(NT9):
                sp.wait_ge(out_ready, t + 1)
                dst = y_prompt[0, t * P:(t + 1) * P, :] if t < NT else y_sample[:, 0, :]
                sp.dma_start(dst, raw[0:rows_of(t), t % 4, :]).then_inc(y_out[t % 4], 16)
            for i in range(4):
                sp.wait_ge(y_out[i], 16 * len(range(i, NT9, 4)))
            sp.wait_ge(out_done, 5 * 16)
            sp.wait_ge(sn_out, 32)
            sp.wait_ge(ct_out, 32)

        @block.gpsimd
        def _(pool):
            pool.memset(ones[:, :], 1.0).then_inc(consts, 1)
            pool.memset(stat[:, 42:43], EPS).then_inc(pool_once, 1)
            pool.memset(w_raw[:, 0, :, :], 0.0).then_inc(pool_once, 1)
            pool.wait_ge(consts, 1)
            for m, op, fill in ((ident, ALU.is_equal, 0.0), (incl, ALU.is_ge, 0.0), (strict, ALU.is_gt, 0.0)):
                pool.affine_select(out=m[:, :], in_=ones[:, :], compare_op=op, fill=fill, base=0,
                                   pattern=[[-1, P]], channel_multiplier=1).then_inc(consts, 1)
            pool.memset(cb[:, :, 0:3], 0.0).then_inc(pool_once, 1)

            pool.memset(stat[:, 50:52], 0.0).then_inc(pool_once, 1)
            step = 0
            for l in range(LEVELS):
                b, v = 1 << l, -1.0 if l == 0 else 1.0
                m = lm[:, l, :].rearrange("p (j u w) -> p j u w", u=2, w=b)
                pool.memset(m[:, :, 0, :], v)
                pool.memset(m[:, :, 1, :], 0.0).then_inc(masks, 1)
                m = lm[:, l, :].rearrange("p (j w) -> p j w", w=2 * b)
                for base, k in ((-b, 1), (2 * b - 1, -1)):
                    step += 1
                    pool.wait_ge(masks, step)
                    pool.affine_select(out=m, in_=m, compare_op=ALU.is_ge, fill=0.0, base=base,
                                       pattern=[[-2 * b * k, P // (2 * b)], [0, 2 * b]],
                                       channel_multiplier=k).then_inc(masks, 1)
                step += 1
            m = lm[:, LEVELS, :].rearrange("p (j u) -> p j u", u=2)
            pool.memset(m[:, :, 0:1], 0.0)
            pool.memset(m[:, :, 1:2], -1.0).then_inc(masks, 1)
            pool.wait_ge(masks, step + 1)
            pool.affine_select(out=m, in_=m, compare_op=ALU.is_equal, fill=0.0, base=0,
                               pattern=[[-2, P // 2], [0, 2]], channel_multiplier=1).then_inc(masks, 1)
            NMASK = step + 2

            pool.memset(m8, 1.0).then_inc(m8_ready, 1)
            pool.wait_ge(m8_ready, 1)
            pool.affine_select(out=m8, in_=m8, compare_op=ALU.is_equal, fill=0.0, base=0, pattern=[[1, NB], [-1, NB]],
                               channel_multiplier=0).then_inc(m8_ready, 1)
            for n in range(NBLK):
                pool.wait_ge(w_hi_ready, n + 1)
                if n >= 2:
                    pool.wait_ge(block_done, n - 1)
                pool.tensor_tensor(w_lo[:, n % 2, :, :], w_raw[:, n % 2, :, :],
                                   w_hi[:, n % 2, :, :].bitcast(F32), ALU.subtract).then_inc(w_lo_ready, 1)

            pool.wait_ge(block_done, NBLK)
            pool.memset(T1[64:128, :], 0.0).then_inc(t1_zero, 1)
            pool.memset(cm[64:64 + H, :], 1.0).then_inc(t1_zero, 1)
            pool.wait_ge(t1_zero, 2)
            pool.memset(cm[64:64 + H, :].rearrange("h (c i) -> h c i", i=P)[:, :, 0:1], 0.0).then_inc(t1_zero, 1)
            xs = [0]

            def xlink(ins):
                xs[0] += 1
                ins.then_inc(x_step, 1)
                pool.wait_ge(x_step, xs[0])

            for c0 in range(0, NT, 2):
                for c in (c0, c0 + 1):
                    s = c % 2
                    pool.wait_ge(dif_ready, c + 1)
                    pool.tensor_scalar(DEC[s][:, :, :], DEC[s][:, :, :], 0.0, None, ALU.max).then_inc(dmax_ready, 1)
                for c in (c0, c0 + 1):
                    s = c % 2
                    pool.wait_ge(dexp_ready, c + 1)
                    pool.tensor_tensor(DEC[s][:, :, :], DEC[s][:, :, :], over_heads(incl[:, :]), ALU.mult).then_inc(dec_ready, 1)
                for c in (c0, c0 + 1):
                    s = c % 2
                    pool.wait_ge(kks_ready, c + 1)
                    pool.tensor_tensor(LL[s][:, :, :], LL[s][:, :, :], per_head(gN[:, c, 32:36]), ALU.mult).then_inc(l_ready, 1)
                for c in (c0, c0 + 1):
                    s = c % 2
                    pool.wait_ge(l_ready, c + 1)
                    if c >= 2:
                        pool.wait_ge(u_ready, c - 1)
                    xlink(pool.tensor_tensor(XX[s][:, :, :], LL[s][:, :, :], over_heads(lm[:, 0, :]), ALU.mult))
                    pool.tensor_tensor(XX[s][:, :, :], XX[s][:, :, :], over_heads(ident[:, :]), ALU.add).then_inc(x0_ready, 1)
                    pool.wait_ge(lt_ready, c + 1)
                    xlink(pool.tensor_tensor(XT[s][:, :, :], LT[s][:, :, :], over_heads(lm[:, LEVELS, :]), ALU.mult))
                    pool.tensor_tensor(XT[s][:, :, :], XT[s][:, :, :], over_heads(ident[:, :]), ALU.add).then_inc(x0_ready, 1)
                for c in (c0, c0 + 1):
                    s = c % 2
                    pool.wait_ge(eg_ready, c + 1)
                    pool.tensor_tensor(QG[s][:, :, :], QG[s][:, :, :], cT[:, 0:H, chunk(c)], ALU.mult).then_inc(qg_ready, 1)
                for c in (c0, c0 + 1):
                    s = c % 2
                    if c >= 1:
                        pool.wait_ge(s_ready, c)
                        pool.tensor_tensor(SG[:, :, :], ST[:, :, :], per_head(sm(s, EL)), ALU.mult).then_inc(sg_ready, 1)
                for c in (c0, c0 + 1):
                    s = c % 2
                    pool.wait_ge(og_ready, c + 1)
                    pool.wait_ge(z_in[s], 16 * (c // 2 + 1))
                    pool.tensor_tensor(RK[s][:, :, :], RK[s][:, :, :], LT[s][:, :, :], ALU.mult).then_inc(m_ready, 1)

            pool.wait_ge(act_once, A_READY)
            pool.tensor_tensor(a_diag, ident[0:NB, 0:NB].unsqueeze(2).to_broadcast([NB, NB, H]),
                               a_row.unsqueeze(1).to_broadcast([NB, NB, H]), ALU.mult).then_inc(pool_once, 1)
            for half in range(2):
                if half:
                    pool.wait_ge(pe_once, PRED_READY)
                for h in range(H):
                    src = cT[:, H * (1 - half) + h, SEQ:TOK]
                    pool.tensor_tensor(msk[:, h, :, :], src.unsqueeze(2).to_broadcast([P, NB, NB]), m8, ALU.mult)\
                        .then_inc(msk_ready, 1)

            pool.wait_ge(dve_once, PD_READY)
            for n in range(NB * NPG):
                b, j = n // NPG, n % NPG
                if j == 0:
                    pool.wait_ge(vpage_in[b % 2], 16 * NPG * (b // 2 + 1))
                pool.tensor_tensor(vpage(n).rearrange("p (h d) -> p h d", h=H), vpage(n).rearrange("p (h d) -> p h d", h=H),
                                   per_head(pp[:, b, :, j]), ALU.mult).then_inc(pv_made, 1)

        @block.scalar
        def _(act):
            achain = [0]

            def alink(ins):
                achain[0] += 1
                ins.then_inc(act_step, 1)
                act.wait_ge(act_step, achain[0])

            for t in range(NT + 2):
                if t <= NT:
                    r = rows_of(t)
                    act.wait_ge(x_in[t % 3], 16 * (t // 3 + 1))
                    alink(act.activation(junk[0:r, :], x_t[0:r, t % 3, :], ACT.Square, accum_out=stat[0:r, t:t + 1]))
                    act.wait_ge(pool_once, EPS_READY)
                    act.activation(stat[0:r, 16 + t:17 + t], stat[0:r, t:t + 1], ACT.Sqrt, scale=1.0 / D,
                                   bias=stat[0:r, 42:43]).then_inc(std_ready, 1)
                if t >= 1:
                    u, r = t - 1, rows_of(t - 1)
                    act.wait_ge(xt_ready, u + 1)
                    b = 2 * (u % 2)
                    act.activation(act_hi[:, :, u * P:u * P + r],
                                   PS[:, b:b + 2, :].rearrange("p b (k c) -> p (b k) c", c=P)[:, :, 0:r],
                                   ACT.Copy).then_inc(act_hi_ready, 1)

            def split_w(n):
                act.wait_ge(w_in_sem[n % 2], raw_count(n))
                if n >= 2:
                    act.wait_ge(block_done, n - 1)
                act.activation(w_hi[:, n % 2, :, :], w_raw[:, n % 2, :, :], ACT.Copy).then_inc(w_hi_ready, 1)

            split_w(0)
            for n in range(NBLK + 1):
                if n + 1 < NBLK:
                    split_w(n + 1)
                if CV0 <= n - 1 < NAT0:
                    c = n - 1 - CV0
                    act.wait_ge(conv_ready, c + 1)
                    act.activation(cT[:, c, :], acc[:, :], ACT.Silu).then_inc(silu_done, 1)
                if n == NBLK:
                    break
                act.wait_ge(block_done, n + 1)
                b, m, scale = 3 * (n % 2), cb_use(n), 1.0
                src = PS[:, b:b + 3, 0:G3]
                if n == GATE:
                    dst, src = gateT[0:96, :], PS[0:96, b:b + 3, 0:G3]
                elif m is not None:
                    if m == 0:
                        act.wait_ge(pool_once, PAD_ZERO)
                    if m >= 2:
                        act.wait_ge(cb_free, m - 1)
                    dst = cb[:, m % 2, 3:3 + TOK]
                elif n < 17:
                    dst = kT[:, n - NAT0, :]
                else:
                    dst, scale = qT[:, n - Q0, :], SCALE
                act.activation(dst.rearrange("p (g c) -> p g c", g=3), src, ACT.Silu if 21 <= n < Q0 else ACT.Copy, scale=scale).then_inc(evacuated, 1)

            act.wait_ge(dve_once, GATE_ABS)
            act.activation(ge[0:96, :], ge[0:96, :], ACT.Exp, scale=-1.0).then_inc(gate_act, 1)
            act.wait_ge(gate_act, 1)
            act.activation(gs[0:96, :], ge[0:96, :], ACT.Ln, bias=ones[0:96, 0:1]).then_inc(gate_act, 1)
            act.wait_ge(dve_once, GATE_MIN)
            act.activation(T1[32:64, :], T1[32:64, :], ACT.Exp).then_inc(gate_act, 1)
            act.activation(stat[64:68, 52:53], stat[64:68, 51:52], ACT.Exp).then_inc(gate_act, 1)
            for b in range(9):
                if b < 8:
                    if b >= 2:
                        act.wait_ge(ss_ready, b - 1)
                    act.activation(sq[:, b % 2, :], cT[:, b, :], ACT.Square).then_inc(sq_ready, 1)
                if b >= 1:
                    u = b - 1
                    act.wait_ge(ss_ready, b)
                    if u >= 2:
                        act.wait_ge(normed, u - 1)
                    act.activation(rn[:, u % 2, :].rearrange("p (g c) -> p g c", g=3), PS[:, 3 * (u % 2):3 * (u % 2) + 3, 0:G3],
                                   ACT.Sqrt, bias=stat[:, 42:43]).then_inc(sd_ready, 1)
            for b in range(NB):
                act.wait_ge(qb_t, b + 1)
                act.activation(qb[:, b, :], PS[:, 4 + b % 2, :], ACT.Copy).then_inc(qb_ready, 1)
            act.wait_ge(sn_out, 32)
            act.wait_ge(gn_ready, 6)
            act.activation(E_N, gN[:, 0:NT, 64:68], ACT.Exp).then_inc(act_once, 1)
            for c0 in range(0, NT, 2):
                for c in (c0, c0 + 1):
                    s, A = c % 2, 4 * (c % 2)
                    act.wait_ge(dif_ready, c + 1)
                    if c >= 2:
                        act.wait_ge(o_ready, c - 1)
                        act.wait_ge(s_ready, c - 1)
                    act.activation(QG[s][:, :, :], heads(A), ACT.Exp)
                    act.activation(sm(s, EL), heads(A)[:, :, P - 1], ACT.Exp)
                    act.activation(sm(s, KGS), sm(s, GLC), ACT.Exp).then_inc(eg_ready, 1)
                for c in (c0, c0 + 1):
                    s = c % 2
                    act.wait_ge(dmax_ready, c + 1)
                    act.activation(DEC[s][:, :, :], DEC[s][:, :, :], ACT.Exp, scale=-1.0).then_inc(dexp_ready, 1)
                for c in (c0, c0 + 1):
                    s, A = c % 2, 4 * (c % 2)
                    act.wait_ge(lt_t, c + 1)
                    if c >= 2:
                        act.wait_ge(m_ready, c - 1)
                    act.activation(LT[s][:, :, :], heads(A + 1), ACT.Copy).then_inc(lt_ready, 1)
                    act.activation(QKT[s][:, :, :], heads(A + 2), ACT.Copy).then_inc(qkt_ready, 1)
                for c in (c0, c0 + 1):
                    s, A = c % 2, 4 * (c % 2)
                    act.wait_ge(wt_t, c + 1)
                    act.activation(WT[s][:, :, :], heads(A + 1), ACT.Copy, scale=-1.0).then_inc(wt_ready, 1)
                for c in (c0, c0 + 1):
                    s, A = c % 2, 4 * (c % 2)
                    act.wait_ge(o_ready, c + 1)
                    for h in range(H):
                        last = act.activation(QG[s][:, h, :], heads(A + 2)[:, h, :], ACT.Square, accum_out=sm(s, OSS)[:, h:h + 1])
                    alink(last)
                    alink(act.activation(sm(s, OLN), sm(s, OSS), ACT.Ln, scale=1.0 / HD, bias=stat[:, 42:43]))
                    act.activation(sm(s, ORS), sm(s, OLN), ACT.Exp, scale=-0.5).then_inc(ors_ready, 1)
                for c in (c0, c0 + 1):
                    s, A = c % 2, 4 * (c % 2)
                    act.wait_ge(mt_ready, c + 1)
                    act.activation(act_hi[:, H:2 * H, chunk(c)], heads(A + 1), ACT.Copy).then_inc(mhi_ready, 1)

            act.activation(a_row, gN[0:NB, NT, 64:68], ACT.Exp).then_inc(act_once, 1)
            act.wait_ge(pe_once, A_SPREAD)
            act.activation(a_all, PS[:, 4, 0:32], ACT.Copy).then_inc(act_once, 1)
            act.wait_ge(pe_once, SO_READY)
            for h in range(H):
                alink(act.activation(dmk[:, 0, 0, :], PS[0:NB, 4, h * P:(h + 1) * P], ACT.Square, accum_out=s_oss[:, h:h + 1]))
            alink(act.activation(s_oln, s_oss, ACT.Ln, scale=1.0 / HD, bias=stat[0:NB, 42:43]))
            act.activation(s_ors, s_oln, ACT.Exp, scale=-0.5).then_inc(act_once, 1)
            act.wait_ge(pe_once, SMT_READY)
            act.activation(act_hi[:, H:2 * H, SEQ:TOK], PS[:, 5, 0:H * NB].rearrange("p (h b) -> p h b", h=H), ACT.Copy)\
               .then_inc(act_once, 1)

            for h in range(H):
                act.wait_ge(d_spread, h + 1)
                b = 2 * (h % 2)
                act.activation(Db[:, h, :], PS[:, b:b + 2, :].rearrange("p b n -> p (b n)"), ACT.Copy).then_inc(db_ready, 1)
            act.wait_ge(sh_ready, 2)
            act.activation(pp[:, :, :, :], pp[:, :, :, :], ACT.Exp).then_inc(e_ready, 1)
            act.activation(self_e, self_e, ACT.Exp).then_inc(e_ready, 1)
            for n in range(NAI + 2):
                if n < NAI:
                    i, h, w = n // H, n % H, P * (n // H + 1)
                    act.wait_ge(max_ready, n + 1)
                    act.activation(sc[:, n % 2, 0:w], sc[:, n % 2, 0:w], ACT.Exp, bias=arow[:, 0, n:n + 1],
                                   accum_out=arow[:, 1, n:n + 1]).then_inc(p_ready, 1)
                m = n - 1
                if 0 <= m < NAI:
                    w = P * (m // H + 1)
                    act.wait_ge(pt_t, m + 1)
                    if m >= 2:
                        act.wait_ge(pv_ready, m - 1)
                    act.activation(pT[:, m % 2, :, :].rearrange("p k q -> p (k q)")[:, 0:w],
                                   PS[:, 4:6, :].rearrange("p b n -> p (b n)")[:, 0:w], ACT.Copy).then_inc(pt_ready, 1)
                if n >= H + 1 and (n - 1) % H == 0:
                    i = (n - 1) // H - 1
                    act.wait_ge(ot_ready, i + 1)
                    act.activation(act_hi[:, 0:H, chunk(i)], heads(6 + i % 2), ACT.Copy).then_inc(othi_ready, 1)
            act.wait_ge(pe_once, DVT_READY)
            act.activation(act_hi[:, 0:H, SEQ:TOK], PS[:, 4, 0:H * NB].rearrange("p (h b) -> p h b", h=H), ACT.Copy).then_inc(act_once, 1)

            for k in range(KT):
                act.wait_ge(raw_in[k % 4], 16 * (k // 4 + 1))
                if k == 0:
                    act.wait_ge(dve_once, DOLO_READY)
                act.activation(wo_hi[:, k, :], raw[:, k % 4, :], ACT.Copy).then_inc(wo_hi_ready, 1)
            for t in range(NT9 + 1):
                if t < NT9:
                    r = rows_of(t)
                    act.wait_ge(h_ready, t + 1)
                    if t >= 2:
                        act.wait_ge(xmt_ready, t - 1)
                    alink(act.activation(xm[0:r, t % 2, :], y[0:r, t, :], ACT.Square, accum_out=stat[0:r, t:t + 1]))
                    act.activation(stat[0:r, 16 + t:17 + t], stat[0:r, t:t + 1], ACT.Sqrt, scale=1.0 / D,
                                   bias=stat[0:r, 42:43]).then_inc(std2_ready, 1)
                if t >= 1:
                    u, r = t - 1, rows_of(t - 1)
                    b = 4 + 2 * (u % 2)
                    act.wait_ge(xmt_ready, u + 1)
                    act.activation(act_hi[:, :, u * P:u * P + r],
                                   PS[:, b:b + 2, :].rearrange("p b (k c) -> p (b k) c", c=P)[:, :, 0:r], ACT.Copy).then_inc(a2hi_ready, 1)

            RW = 32
            act.wait_ge(h_t, NT9)
            for q in range(2):
                act.wait_ge(raw_in[q], RW + 16)
                act.activation(wu_hi[:, q, :, :], raw[:, q, :].rearrange("p (kt c) -> p kt c", c=P), ACT.Copy).then_inc(hi_done, 1)

            def act_group(g, last):
                for k in range(GB):
                    b = 3 * (k % 2)
                    act.wait_ge(up_done, GB * g + k + 3)
                    act.wait_ge(u_lo_done, GB * g + k + 1)
                    act.activation(r_sq[:, :].rearrange("p (g c) -> p g c", g=3), PS[:, b:b + 3, 0:G3], ACT.Relu).then_inc(relu_done, 1)
                    slot = (2 * k + 2) % 4
                    act.wait_ge(raw_in[slot], RW + 16 * ((2 * k + 2) // 4 + 1) + 32 * g)
                    act.wait_ge(dn_tile, NT9 * g + 1)
                    act.activation(wd_hi[:, k, :], raw[:, slot, :], ACT.Copy).then_inc(hi_done, 1)
                    act.wait_ge(sq_done, GB * g + k + 1)
                    act.activation(u_hi[:, k, :], r_sq[:, :], ACT.Copy).then_inc(u_hi_done, 1)
                    if not (last and k >= 2):
                        slot = (2 * k + 3) % 4
                        act.wait_ge(raw_in[slot], RW + 16 * ((2 * k + 3) // 4 + 1) + 32 * g)
                        act.activation(wu_hi[:, k % 2, :, :], raw[:, slot, :].rearrange("p (kt c) -> p kt c", c=P), ACT.Copy)\
                           .then_inc(hi_done, 1)

            with act.Fori(0, NG - 1) as g:
                act_group(g, False)
            act_group(NG - 1, True)
            for t in range(NT9):
                r = rows_of(t)
                act.wait_ge(y_add, NT9 * (NG - 1) + t + 2)
                alink(act.activation(junk2[0:r, :], y[0:r, t, :], ACT.Square, accum_out=stat[0:r, t:t + 1]))
                act.activation(stat[0:r, 16 + t:17 + t], stat[0:r, t:t + 1], ACT.Sqrt, scale=1.0 / D,
                               bias=stat[0:r, 42:43]).then_inc(std3_ready, 1)

        @block.vector
        def _(dve):
            chain = [0]

            def link(ins):
                chain[0] += 1
                ins.then_inc(dve_step, 1)
                dve.wait_ge(dve_step, chain[0])

            dve.wait_ge(ln_in, 16)
            for t in range(NT + 2):
                if t <= NT:
                    r = rows_of(t)
                    dve.wait_ge(std_ready, t + 1)
                    link(dve.reciprocal(stat[0:r, 28 + t:29 + t], stat[0:r, 16 + t:17 + t]))
                    if t >= 2:
                        dve.wait_ge(xt_ready, t - 1)
                    dve.scalar_tensor_tensor(xn[0:r, t % 2, :], x_t[0:r, t % 3, :], stat[0:r, 28 + t:29 + t],
                                             lnb[0:r, :], ALU.mult, ALU.mult).then_inc(xn_ready, 1)
                if t >= 1:
                    u, r = t - 1, rows_of(t - 1)
                    dve.wait_ge(act_hi_ready, u + 1)
                    b, cs = 2 * (u % 2), slice(u * P, u * P + r)
                    dve.tensor_tensor(act_lo[:, :, cs],
                                      PS[:, b:b + 2, :].rearrange("p b (k c) -> p (b k) c", c=P)[:, :, 0:r],
                                      act_hi[:, :, cs].bitcast(F32), ALU.subtract).then_inc(act_lo_ready, 1)
            dve.wait_ge(pe_once, HW_T)
            link(dve.tensor_copy(hw[:, :, :], PS[:, 6, 0:12 * 28].rearrange("p (c i) -> p c i", c=12)))
            for n in range(CV0, NBLK + 1):
                if n < NAT0:
                    c = n - CV0
                    s = cb[:, c % 2, :]
                    hist = hw[:, c, 0:24].rearrange("p (b i) -> p b i", i=3)
                    dve.wait_ge(evacuated, n + 1)
                    if c >= 1:
                        dve.wait_ge(silu_done, c)
                    dve.tensor_copy(tail[:, c, :], s[:, SEQ:SEQ + 11])
                    dve.tensor_scalar(acc[:, SEQ:TOK], hist[:, :, 0], hw[:, c, 24:25], None, ALU.mult)
                    link(dve.tensor_scalar(acc[:, 0:SEQ], s[:, 0:SEQ], hw[:, c, 24:25], None, ALU.mult))
                    for i in (1, 2):
                        dve.scalar_tensor_tensor(acc[:, SEQ:TOK], hist[:, :, i], hw[:, c, 24 + i:25 + i],
                                                 acc[:, SEQ:TOK], ALU.mult, ALU.add)
                        link(dve.scalar_tensor_tensor(acc[:, 0:SEQ], s[:, i:SEQ + i], hw[:, c, 24 + i:25 + i],
                                                      acc[:, 0:SEQ], ALU.mult, ALU.add))
                    dve.scalar_tensor_tensor(acc[:, :], s[:, 3:3 + TOK], hw[:, c, 27:28], acc[:, :],
                                             ALU.mult, ALU.add).then_inc(conv_ready, 1)
                    dve.wait_ge(conv_ready, c + 1)
                    dve.tensor_copy(stat[:, 40:41], s[:, 0:1]).then_inc(cb_free, 1)
                i = n - 1 - NAT0
                if 0 <= i < 12:
                    dve.wait_ge(nat_t, i + 1)
                    if i >= 2:
                        dve.wait_ge(nat_out[i % 2], 16 * (i // 2))
                    if i >= 4:
                        m = cb_use(NAT0 + i)
                        dve.tensor_copy(vzS[:, i - 4, :], cb[:, m % 2, 3 + SEQ:3 + TOK]).then_inc(cb_free, 1)
                    dve.tensor_copy(nat[:, i % 2, :, :], PS[:, 6:8, :].rearrange("p b (k c) -> p (b k) c", c=P))\
                       .then_inc(nat_ready, 1)


            dve.wait_ge(pe_once, CT_T)
            dve.tensor_copy(ct[:, :, :], PS[0:11, 0:3, :].rearrange("p b (k c) -> p (b k) c", c=P)).then_inc(dve_once, 1)
            dve.wait_ge(bias_in, 48)
            dve.wait_ge(t1_zero, 3)
            link(dve.tensor_scalar(gateT[0:96, :], gateT[0:96, :], stat[0:96, 50:51], None, ALU.add))
            dve.tensor_scalar(T1[32:64, :], gateT[32:64, :], 0.0, None, ALU.min).then_inc(dve_once, 1)
            dve.scalar_tensor_tensor(ge[0:96, :], gateT[0:96, :], -1.0, gateT[0:96, :], ALU.mult, ALU.max).then_inc(dve_once, 1)
            dve.wait_ge(gate_act, 4)
            dve.scalar_tensor_tensor(T1[0:32, :], gateT[0:32, :], 0.0, gs[0:32, :], ALU.min, ALU.subtract)
            link(dve.tensor_scalar(ge[32:64, :], ge[32:64, :], 1.0, None, ALU.add))
            link(dve.reciprocal(ge[32:64, :], ge[32:64, :]))
            dve.tensor_tensor(T1[32:64, :], T1[32:64, :], ge[32:64, :], ALU.mult)
            link(dve.scalar_tensor_tensor(ge[64:96, :], gateT[64:96, :], 0.0, gs[64:96, :], ALU.max, ALU.add))
            link(dve.tensor_scalar(ge[64:68, :], ge[64:68, :], stat[64:68, 52:53], -1.0, ALU.mult, ALU.mult))
            dve.tensor_copy(T1[64:68, SEQ:TOK], ge[64:68, SEQ:TOK])
            dve.tensor_tensor_scan(T1[64:68, 0:SEQ], cm[64:68, :], ge[64:68, 0:SEQ], 0.0, ALU.mult, ALU.add)
            dve.tensor_tensor_scan(T1[96:100, 0:SEQ], ones[0:4, 0:1].to_broadcast([4, SEQ]), T1[0:4, 0:SEQ], 0.0,
                                   ALU.mult, ALU.add).then_inc(dve_once, 1)
            dve.wait_ge(pe_once, GN_T)
            for (t0, n, r, off) in ((0, 5, P, 6), (5, 3, P, 7), (8, 1, NB, 7)):
                src = PS[0:r, off, 0:500].rearrange("p (t c) -> p t c", c=100)
                k = 3 if t0 == 8 else 0
                dve.tensor_copy(gN[0:r, t0:t0 + n, 0:68], src[:, k:k + n, 0:68]).then_inc(gn_ready, 1)
                dve.tensor_copy(gN[0:r, t0:t0 + n, 68:72], src[:, k:k + n, 96:100]).then_inc(gn_ready, 1)
            for b in range(8):
                dve.wait_ge(sd_ready, b + 1)
                link(dve.reciprocal(rn[:, b % 2, :], rn[:, b % 2, :]))
                dve.scalar_tensor_tensor(cT[:, b, :], cT[:, b, :], SCALE if b < 4 else 1.0, rn[:, b % 2, :],
                                         ALU.mult, ALU.mult).then_inc(normed, 1)
            dve.wait_ge(pe_once, SN_T)
            dve.wait_ge(normed, 8)
            dve.tensor_copy(sN[:, :, :], PS[0:NB, 0:3, :].rearrange("p b (k c) -> p (b k) c", c=P)).then_inc(dve_once, 1)
            dve.wait_ge(pe_once, CLF_T)
            dve.tensor_copy(clf[:, :, :, :].rearrange("p b j h -> p (b j) h"), PS[:, 3, 0:256].rearrange("p (h n) -> p n h", h=H))\
               .then_inc(dve_once, 1)
            dve.wait_ge(dve_once, SN_READY)
            for h in range(H):
                link(dve.tensor_tensor_reduce(prod[:, :], sN[:, h, :], sN[:, H + h, :], 1.0, 0.0, ALU.mult, ALU.add,
                                               self_s[:, h:h + 1]))
            eye8 = ident[0:NB, 0:NB].unsqueeze(2).to_broadcast([NB, NB, H])
            dve.tensor_tensor(lf_diag, eye8, gN[0:NB, NT, 0:H].unsqueeze(1).to_broadcast([NB, NB, H]), ALU.mult).then_inc(diag_ready, 1)
            dve.tensor_tensor(self_diag, eye8, self_s.unsqueeze(1).to_broadcast([NB, NB, H]), ALU.mult).then_inc(diag_ready, 1)
            dve.wait_ge(pe_once, BIAS_T)
            dve.tensor_copy(self_sc, PS[:, 7, 32:64])
            suf = PS[:, 6, 0:256].rearrange("p (b j h) -> p b j h", j=NPG, h=H)
            tot = PS[:, 6, 256:512].rearrange("p (b j h) -> p b j h", j=NPG, h=H)
            link(dve.tensor_copy(run_, PS[:, 7, 0:32].rearrange("p (b h) -> p b h", h=H)))
            for j in range(NPG - 1, -1, -1):
                dve.tensor_tensor(sfx[:, :, j, :], suf[:, :, j, :], run_, ALU.add).then_inc(pre_read, 1)
                dve.wait_ge(pre_read, NPG - j)
                if j:
                    link(dve.tensor_tensor(run_, run_, tot[:, :, j, :], ALU.add))

            kp = [0]

            def score_pages(count):
                for _ in range(count):
                    n = kp[0]
                    kp[0] += 1
                    b, j, k = n // NPG, n % NPG, kpages[:, n % NR, :]
                    dve.wait_ge(kpage_in[n % NR], 16 * (n // NR + 1))
                    if n < NPG or j == 0:
                        dve.wait_ge(qb_ready, b + 1)
                    for h in range(H):
                        cs = slice(h * P, (h + 1) * P)
                        last = dve.tensor_tensor_reduce(k[:, cs], k[:, cs], qb[:, b, cs], 1.0, 0.0, ALU.mult, ALU.add, s9[:, b, h, j:j + 1])
                    last.then_inc(k_used, 1)

            dve.wait_ge(act_once, EN_READY)
            dve.tensor_tensor(B_EK, E_N, gN[:, 0:NT, 32:36], ALU.mult).then_inc(dve_once, 1)
            dve.wait_ge(wgn_in, 16)
            for c0 in range(0, NT, 2):
                for c in (c0, c0 + 1):
                    s, A = c % 2, 4 * (c % 2)
                    dve.wait_ge(gb_ready, c + 1)
                    dve.tensor_tensor(sm(s, GLC), heads(A)[:, :, P - 1], gN[:, c, 64:68], ALU.subtract)
                    dve.tensor_tensor(DEC[s][:, :, :], heads(A), per_head(gN[:, c, 64:68]), ALU.subtract).then_inc(dif_ready, 1)
                for c in (c0, c0 + 1):
                    s, A = c % 2, 4 * (c % 2)
                    dve.wait_ge(dec_ready, c + 1)
                    dve.wait_ge(kk_ready, c + 1)
                    dve.tensor_tensor(LL[s][:, :, :], heads(A + 1), DEC[s][:, :, :], ALU.mult).then_inc(kks_ready, 1)
                    if c < 2:
                        dve.wait_ge(ct_out, 32)
                    dve.tensor_tensor(QKD[s][:, :, :], heads(A + 2), DEC[s][:, :, :], ALU.mult).then_inc(qkd_ready, 1)
                for c in (c0, c0 + 1):
                    s, A = c % 2, 4 * (c % 2)
                    dve.wait_ge(lt_t, c + 1)
                    dve.tensor_tensor(BV[s][:, :, :], heads(A + 3), per_head(gN[:, c, 32:36]), ALU.mult).then_inc(bv_ready, 1)
                score_pages(2)
                for c in (c0, c0 + 1):
                    s, A = c % 2, 4 * (c % 2)
                    dve.wait_ge(kn_ready, c + 1)
                    dve.wait_ge(eg_ready, c + 1)
                    if c == 0:
                        dve.wait_ge(dve_once, BEK_READY)
                    dve.tensor_tensor(RK[s][:, :, :], heads(A + 3), per_head(B_EK[:, c, :]), ALU.mult)
                    dve.tensor_tensor(KG[s][:, :, :], heads(A + 3), per_head(sm(s, KGS)), ALU.mult).then_inc(rk_ready, 1)
                score_pages(2)
                for l in range(1, LEVELS):
                    for c in (c0, c0 + 1):
                        s, A = c % 2, 4 * (c % 2)
                        dve.wait_ge(y_ready, level_seq(c, l))
                        dve.tensor_tensor(LL[s][:, :, :], heads(A), over_heads(lm[:, l, :]), ALU.mult).then_inc(ym_ready, 1)
                    score_pages(2)
                    for c in (c0, c0 + 1):
                        s, A = c % 2, 4 * (c % 2)
                        dve.wait_ge(z_ready, level_seq(c, l))
                        if l < LEVELS - 1:
                            dve.tensor_tensor(XX[s][:, :, :], XX[s][:, :, :], heads(A + 1), ALU.subtract)
                        dve.tensor_tensor(XT[s][:, :, :], XT[s][:, :, :], heads(A + 2), ALU.subtract).then_inc(x_ready, 1)
                for c in (c0, c0 + 1):
                    s, A = c % 2, 4 * (c % 2)
                    dve.wait_ge(u_ready, c + 1)
                    dve.tensor_copy(VN[s][:, :, :], heads(A)).then_inc(vn_ready, 1)
                    dve.wait_ge(s_add, c + 1)
                    if c == 0:
                        dve.tensor_copy(ST[:, :, :], heads(A + 3)).then_inc(s_ready, 1)
                    else:
                        dve.wait_ge(sg_ready, c)
                        dve.tensor_tensor(ST[:, :, :], SG[:, :, :], heads(A + 3), ALU.add).then_inc(s_ready, 1)
                for c in (c0, c0 + 1):
                    s, A = c % 2, 4 * (c % 2)
                    dve.wait_ge(ors_ready, c + 1)
                    for h in range(H):
                        last = dve.scalar_tensor_tensor(RK[s][:, h, :], heads(A + 2)[:, h, :], sm(s, ORS)[:, h:h + 1], wgn[:, :],
                                                        ALU.mult, ALU.mult)
                    last.then_inc(og_ready, 1)
                for c in (c0, c0 + 1):
                    s, A = c % 2, 4 * (c % 2)
                    dve.wait_ge(mhi_ready, c + 1)
                    dve.tensor_tensor(act_lo[:, H:2 * H, chunk(c)], heads(A + 1), act_hi[:, H:2 * H, chunk(c)].bitcast(F32),
                                      ALU.subtract).then_inc(mlo_ready, 1)

            dve.wait_ge(pe_once, DN_T)
            dve.tensor_copy(dN[:, :, :], PS[0:NB, 0:4, :].rearrange("p b (k c) -> p (b k) c", c=P)).then_inc(dve_once, 1)
            dve.wait_ge(dve_once, DN_READY)
            dve.wait_ge(pe_once, PRED_READY)
            for h in range(H):
                last = dve.scalar_tensor_tensor(dlt[:, h, :], PS[0:NB, 5, h * P:(h + 1) * P], a_row[:, h:h + 1], dN[:, 8 + h, :],
                                                ALU.mult, ALU.subtract)
            link(last)
            for h in range(H):
                last = dve.tensor_scalar(dlt[:, h, :], dlt[:, h, :], gN[0:NB, NT, 32 + h:33 + h], -1.0, ALU.mult, ALU.mult)
            link(last)
            for h in range(H):
                dve.tensor_tensor(dmk[:, h, :, :], dlt[:, h, :].unsqueeze(1).to_broadcast([NB, NB, P]),
                                  ident[0:NB, 0:NB].unsqueeze(2).to_broadcast([NB, NB, P]), ALU.mult).then_inc(dmk_ready, 1)
            dve.wait_ge(act_once, A_ALL_READY)
            dve.wait_ge(st_in, 16)
            for g in range(8):
                h, half = g // 2, g % 2
                dve.wait_ge(outer_ready, g + 1)
                for b in range(4):
                    j = (4 * half + b) * H + h
                    last = dve.scalar_tensor_tensor(S_s[:, j, :], S_s[:, j, :], a_all[:, j:j + 1], PS[:, g % 4, b * P:(b + 1) * P],
                                                    ALU.mult, ALU.add)
                last.then_inc(st_ready, 1)
            dve.wait_ge(act_once, SORS_READY)
            for h in range(H):
                last = dve.scalar_tensor_tensor(dlt[:, h, :], PS[0:NB, 4, h * P:(h + 1) * P], s_ors[:, h:h + 1], wgn[0:NB, :],
                                                ALU.mult, ALU.mult)
            link(last)
            dve.tensor_tensor(dlt[:, :, :], dlt[:, :, :], dN[:, 12:16, :], ALU.mult).then_inc(dve_once, 1)
            dve.wait_ge(act_once, SMHI_READY)
            dve.tensor_tensor(act_lo[:, H:2 * H, SEQ:TOK], PS[:, 5, 0:H * NB].rearrange("p (h b) -> p h b", h=H),
                              act_hi[:, H:2 * H, SEQ:TOK].bitcast(F32), ALU.subtract).then_inc(dve_once, 1)

            dve.wait_ge(k_used, NB * NPG)
            dve.wait_ge(st_ready, 8)
            dve.wait_ge(pe_once, SO_READY)
            dve.wait_ge(pe_once, SMT_READY)
            for b in range(NB):
                last = dve.tensor_tensor(pp[:, b, :, :], s9[:, b, :, :], sfx[:, b, :, :].rearrange("p j h -> p h j"), ALU.add)
            link(last)
            pv_ = pp[:, :, :, :].rearrange("p b h j -> p (b h) j")
            link(dve.tensor_reduce(mx, pv_, AX.X, ALU.max))
            dve.tensor_tensor(mx, mx, self_sc, ALU.max).then_inc(dve_once, 1)
            dve.wait_ge(pe_once, MX_T)
            link(dve.tensor_reduce(mcol, PS[0:32, 4, 0:P], AX.X, ALU.max))
            dve.tensor_scalar(mdiag, ident[0:32, 0:32], mcol, None, ALU.mult).then_inc(dve_once, 1)
            dve.wait_ge(pe_once, M_SPREAD)
            link(dve.tensor_copy(m_all, PS[:, 5, 0:32]))
            dve.tensor_tensor(pv_, pv_, m_all.unsqueeze(2).to_broadcast([P, 32, NPG]), ALU.subtract).then_inc(sh_ready, 1)
            dve.tensor_tensor(self_e, self_sc, m_all, ALU.subtract).then_inc(sh_ready, 1)
            dve.wait_ge(e_ready, 2)
            dve.tensor_reduce(sj, pv_, AX.X, ALU.add).then_inc(dve_once, 1)
            dve.wait_ge(pe_once, SUM_SPREAD)
            link(dve.tensor_tensor(inv, PS[:, 5, 32:64], self_e, ALU.add))
            link(dve.reciprocal(inv, inv))
            dve.tensor_tensor(pv_, pv_, inv.unsqueeze(2).to_broadcast([P, 32, NPG]), ALU.mult)
            link(dve.tensor_tensor(self_e, self_e, inv, ALU.mult))
            dve.tensor_tensor(p_diag, self_e[0:NB, :].rearrange("p (b h) -> p h b", h=H),
                              ident[0:NB, 0:NB].unsqueeze(1).to_broadcast([NB, H, NB]), ALU.mult).then_inc(dve_once, 1)
            dve.wait_ge(dve_once, PD_READY)
            link(dve.tensor_reduce(self_p, p_diag, AX.X, ALU.add))
            for h in range(H):
                last = dve.tensor_scalar(dv[:, h * P:(h + 1) * P], PS[0:NB, 4, h * P:(h + 1) * P], self_p[:, h:h + 1], None, ALU.mult)
            last.then_inc(dv_ready, 1)
            dve.wait_ge(x0_ready, 2 * NT)
            link(dve.tensor_scalar(neg, incl[:, :], -NEG, NEG, ALU.mult, ALU.add))
            dve.wait_ge(db_ready, H)
            for n in range(NAI + 2):
                if n < NAI:
                    i, h, w = n // H, n % H, P * (n // H + 1)
                    dve.wait_ge(qk_ready, n + 1)
                    if n >= 2:
                        dve.wait_ge(pt_t, n - 1)
                    b = 2 * (n % 2)
                    dve.scalar_tensor_tensor(sc[:, n % 2, 0:w], PS[:, b:b + 2, :].rearrange("p b n -> p (b n)")[:, 0:w],
                                             gN[:, i, 68 + h:69 + h], Db[:, h, 0:w], ALU.add, ALU.subtract).then_inc(sc_step, 1)
                    dve.wait_ge(sc_step, 2 * n + 1)
                    dve.tensor_tensor(sc[:, n % 2, w - P:w], sc[:, n % 2, w - P:w], neg, ALU.add).then_inc(sc_step, 1)
                    dve.wait_ge(sc_step, 2 * n + 2)
                    dve.tensor_reduce(arow[:, 0, n:n + 1], sc[:, n % 2, 0:w], AX.X, ALU.max, negate=True).then_inc(max_ready, 1)
                if n >= H + 1 and (n - 1) % H == 0:
                    i = (n - 1) // H - 1
                    its = slice(i * H, i * H + H)
                    dve.wait_ge(p_ready, H * i + H)
                    link(dve.reciprocal(arow[:, 2, its], arow[:, 1, its]))
                    dve.wait_ge(pv_ready, H * i + H)
                    if i >= 2:
                        dve.wait_ge(ot_ready, i - 1)
                    dve.tensor_tensor(oN[:, i % 2, :, :], heads(6 + i % 2), per_head(arow[:, 2, its]), ALU.mult).then_inc(on_ready, 1)
                    dve.wait_ge(othi_ready, i + 1)
                    dve.tensor_tensor(act_lo[:, 0:H, chunk(i)], heads(6 + i % 2), act_hi[:, 0:H, chunk(i)].bitcast(F32),
                                      ALU.subtract).then_inc(otlo_ready, 1)
                if n < NAI:
                    for m in (2 * n, 2 * n + 1):
                        b = m // NPG
                        if m % NPG == 0 and b >= 3:
                            dve.wait_ge(dv_t, b - 2)
                        dve.wait_ge(pv_made, m + 1)
                        if m % NPG == 0:
                            dve.tensor_copy(av[b % 3][:, :], vpage(m)).then_inc(v_used, 1)
                        else:
                            dve.wait_ge(v_used, m)
                            dve.tensor_tensor(av[b % 3][:, :], av[b % 3][:, :], vpage(m), ALU.add).then_inc(v_used, 1)
                if n % H == 0 and n > H:
                    r = n // H - 1
                    dve.wait_ge(dv_t, r)
                    dve.wait_ge(dv_ready, r)
                    dve.tensor_tensor(dv[:, :], dv[:, :], PS[0:NB, 7 - r % 2, :], ALU.add).then_inc(dv_ready, 1)
            dve.wait_ge(act_once, DOHI_READY)
            dve.tensor_tensor(act_lo[:, 0:H, SEQ:TOK], PS[:, 4, 0:H * NB].rearrange("p (h b) -> p h b", h=H),
                              act_hi[:, 0:H, SEQ:TOK].bitcast(F32), ALU.subtract).then_inc(dve_once, 1)

            for k in range(KT):
                dve.wait_ge(wo_hi_ready, k + 1)
                dve.tensor_tensor(wo_lo[:, k, :], raw[:, k % 4, :], wo_hi[:, k, :].bitcast(F32), ALU.subtract).then_inc(wo_lo_ready, 1)
            dve.wait_ge(ln2_in, 16)
            for t in range(NT9 + 1):
                if t < NT9:
                    r, b = rows_of(t), 2 * (t % 2)
                    dve.wait_ge(h_t, t + 1)
                    dve.wait_ge(xr_in[t % 2], 16 * (t // 2 + 1))
                    dve.tensor_tensor(y[0:r, t, :], PS[0:r, b:b + 2, :].rearrange("p b n -> p (b n)"), x_r[0:r, t % 2, :],
                                      ALU.add).then_inc(h_ready, 1)
                    dve.wait_ge(std2_ready, t + 1)
                    link(dve.reciprocal(stat[0:r, 28 + t:29 + t], stat[0:r, 16 + t:17 + t]))
                    dve.scalar_tensor_tensor(xm[0:r, t % 2, :], y[0:r, t, :], stat[0:r, 28 + t:29 + t], ln2b[0:r, :],
                                             ALU.mult, ALU.mult).then_inc(xm_ready, 1)
                if t >= 1:
                    u, r = t - 1, rows_of(t - 1)
                    b, cs = 4 + 2 * (u % 2), slice(u * P, u * P + rows_of(u))
                    dve.wait_ge(a2hi_ready, u + 1)
                    dve.tensor_tensor(act_lo[:, :, cs], PS[:, b:b + 2, :].rearrange("p b (k c) -> p (b k) c", c=P)[:, :, 0:r],
                                      act_hi[:, :, cs].bitcast(F32), ALU.subtract).then_inc(a2lo_ready, 1)
            for i, (s_, n) in enumerate(((lo_done, 4), (up_done, 2), (relu_done, 2), (u_lo_done, 1), (dn_tile, 1), (y_add, 1))):
                dve.tensor_copy(stat[:, 44 + i:45 + i], stat[:, 42:43]).then_inc(s_, n)
            for q in range(2):
                dve.wait_ge(hi_done, q + 1)
                dve.tensor_tensor(wu_lo[:, q, :, :], raw[:, q, :].rearrange("p (kt c) -> p kt c", c=P), wu_hi[:, q, :, :].bitcast(F32),
                                  ALU.subtract).then_inc(lo_done, 1)

            def dve_group(g, last):
                for k in range(GB):
                    dve.wait_ge(relu_done, GB * g + k + 3)
                    dve.tensor_tensor(r_sq[:, :], r_sq[:, :], r_sq[:, :], ALU.mult).then_inc(sq_done, 1)
                    dve.wait_ge(hi_done, 8 * g + 2 * k + 3 - (last and k == 3))
                    dve.tensor_tensor(wd_lo[:, k, :], raw[:, (2 * k + 2) % 4, :], wd_hi[:, k, :].bitcast(F32), ALU.subtract).then_inc(lo_done, 1)
                    dve.wait_ge(u_hi_done, GB * g + k + 1)
                    dve.tensor_tensor(u_lo[:, k, :], r_sq[:, :], u_hi[:, k, :].bitcast(F32), ALU.subtract).then_inc(u_lo_done, 1)
                    if not (last and k >= 2):
                        dve.wait_ge(hi_done, 8 * g + 2 * k + 4)
                        dve.tensor_tensor(wu_lo[:, k % 2, :, :], raw[:, (2 * k + 3) % 4, :].rearrange("p (kt c) -> p kt c", c=P),
                                          wu_hi[:, k % 2, :, :].bitcast(F32), ALU.subtract).then_inc(lo_done, 1)
                for t in range(NT9):
                    r, b = rows_of(t), 0 if t % 2 else 6
                    dve.wait_ge(dn_tile, NT9 * g + t + 2)
                    dve.tensor_tensor(y[0:r, t, :], y[0:r, t, :], PS[0:r, b:b + 2, :].rearrange("p b n -> p (b n)"), ALU.add).then_inc(y_add, 1)

            with dve.Fori(0, NG - 1) as g:
                dve_group(g, False)
            dve_group(NG - 1, True)
            dve.wait_ge(lnf_in, 16)
            for t in range(NT9):
                r = rows_of(t)
                dve.wait_ge(std3_ready, t + 1)
                link(dve.reciprocal(stat[0:r, 28 + t:29 + t], stat[0:r, 16 + t:17 + t]))
                if t >= 4:
                    dve.wait_ge(y_out[t % 4], 16 * (t // 4))
                dve.scalar_tensor_tensor(raw[0:r, t % 4, :], y[0:r, t, :], stat[0:r, 28 + t:29 + t], lnfb[0:r, :],
                                         ALU.mult, ALU.mult).then_inc(out_ready, 1)

        @block.tensor
        def _(pe):
            pe.wait_ge(consts, 4)
            for t in range(NT + 1):
                r = rows_of(t)
                pe.wait_ge(xn_ready, t + 1)
                if t >= 2:
                    pe.wait_ge(act_lo_ready, t - 1)
                for k in range(KT):
                    last = pe.transpose(PS[:, 2 * (t % 2) + k // 4, (k % 4) * P:(k % 4) * P + r],
                                        xn[0:r, t % 2, k * P:(k + 1) * P], ident[0:r, 0:r])
                last.then_inc(xt_ready, 1)
            pe.wait_ge(hist_in, 32)
            for c in range(12):
                last = pe.transpose(PS[:, 6, c * 28:(c + 1) * 28], hrows[0:28, c * P:(c + 1) * P], ident[0:28, 0:28])
            last.then_inc(pe_once, 1)
            pe.wait_ge(act_lo_ready, NT + 1)
            for n in range(NBLK + 1):
                if n < NBLK:
                    if n >= 2:
                        pe.wait_ge(evacuated, n - 1)
                    m, b = (P if n else 96), 3 * (n % 2)
                    for half, ready, operands in ((0, w_hi_ready, (act_hi, act_lo)), (1, w_lo_ready, (act_hi,))):
                        pe.wait_ge(ready, n + 1)
                        w = (w_hi, w_lo)[half]
                        for k in range(KT):
                            for g in range(3):
                                for a in operands:
                                    last = pe.matmul(PS[0:m, b + g, 0:G3], w[:, n % 2, k, 0:m],
                                                     a[:, k, g * G3:(g + 1) * G3],
                                                     start=(half == 0 and k == 0 and a is act_hi),
                                                     stop=(half == 1 and k == KT - 1))
                    last.then_inc(block_done, 1)
                i = n - 1 - NAT0
                if 0 <= i < 12:
                    pe.wait_ge(evacuated, n)
                    if i >= 1:
                        pe.wait_ge(nat_ready, i)
                    src = kT[:, i, :] if i < 4 else cb[:, cb_use(n - 1) % 2, 3:3 + TOK]
                    for t in range(NT):
                        last = pe.transpose(PS[:, 6 + t // 4, (t % 4) * P:(t % 4 + 1) * P],
                                            src[:, t * P:(t + 1) * P], ident[:, :])
                    last.then_inc(nat_t, 1)


            pe.wait_ge(evacuated, NBLK)
            pe.wait_ge(conv_ready, 12)
            for c in range(12):
                last = pe.transpose(PS[0:11, c // 4, (c % 4) * P:(c % 4 + 1) * P], tail[:, c, :], ident[:, :])
            last.then_inc(pe_once, 1)
            pe.wait_ge(dve_once, CT_READY)
            pe.wait_ge(dve_once, T1_READY)
            pe.wait_ge(nat_ready, 12)
            for t in range(NT + 1):
                r, b, o = rows_of(t), 6 + t // 5, 100 * (t % 5)
                last = pe.transpose(PS[0:r, b, o:o + 100], T1[0:100, t * P:t * P + r], ident[0:100, 0:100])
            last.then_inc(pe_once, 1)
            for b in range(8):
                pe.wait_ge(sq_ready, b + 1)
                if b >= 2:
                    pe.wait_ge(sd_ready, b - 1)
                for g in range(3):
                    last = pe.matmul(PS[:, 3 * (b % 2) + g, 0:G3], ones[:, :], sq[:, b % 2, g * G3:(g + 1) * G3], start=True, stop=True)
                last.then_inc(ss_ready, 1)
            pe.wait_ge(evacuated, NBLK)
            pe.wait_ge(sd_ready, 8)
            for i in range(12):
                src = (qT[:, i, SEQ:TOK] if i < 4 else kT[:, i - 4, SEQ:TOK] if i < 8 else vzS[:, i - 8, :])
                last = pe.transpose(PS[0:NB, i // 4, (i % 4) * P:(i % 4 + 1) * P], src, ident[:, :])
            last.then_inc(pe_once, 1)
            pe.wait_ge(clf_in, 16 * NB * NPG)
            for h in range(H):
                last = pe.transpose(PS[:, 3, 64 * h:64 * h + 64], lf_rows[:, :].rearrange("n (p h) -> n p h", h=H)[:, :, h],
                                    ident[0:NB * NPG, 0:NB * NPG])
            last.then_inc(pe_once, 1)
            pe.wait_ge(dve_once, SN_READY)
            for b in range(NB):
                if b >= 2:
                    pe.wait_ge(qb_ready, b - 1)
                pe.matmul(PS[:, 4 + b % 2, :], ident[0:NB, b:b + 1].to_broadcast([NB, P]),
                          sN[:, 0:H, :].rearrange("p h d -> p (h d)"), start=True, stop=True).then_inc(qb_t, 1)
            pe.wait_ge(dve_once, CLF_READY)
            pe.wait_ge(gn_ready, 6)
            lfs = clf[:, :, :, :].rearrange("p b j h -> p (b j h)")
            pe.matmul(PS[:, 6, 0:256], strict[:, :], lfs, start=True, stop=True)
            pe.matmul(PS[:, 6, 256:512], ones[:, :], lfs, start=True, stop=True)
            pe.wait_ge(diag_ready, 2)
            pe.matmul(PS[:, 7, 0:32], ones[0:NB, :], lf_diag.rearrange("p b h -> p (b h)"), start=True, stop=True)
            pe.matmul(PS[:, 7, 32:64], ones[0:NB, :], self_diag.rearrange("p b h -> p (b h)"), start=True, stop=True).then_inc(pe_once, 1)
            pe.wait_ge(qb_ready, NB)
            pe.wait_ge(pre_read, NPG)
            pe.wait_ge(normed, 8)
            pe.wait_ge(gn_ready, 6)
            for c0 in range(0, NT, 2):
                for c in (c0, c0 + 1):
                    s, A = c % 2, 4 * (c % 2)
                    if c >= 2:
                        pe.wait_ge(vn_ready, c - 1)
                        pe.wait_ge(mlo_ready, c - 1)
                        pe.wait_ge(s_ready, c - 1)
                    for h in range(H):
                        last = pe.matmul(heads(A)[:, h, :], ident[64:68, 64 + h:65 + h].to_broadcast([4, P]), T1[64:68, chunk(c)],
                                         start=True, stop=True)
                    last.then_inc(gb_ready, 1)
                    for h in range(H):
                        pe.matmul(heads(A + 1)[:, h, :], cT[:, H + h, chunk(c)], cT[:, H + h, chunk(c)], start=True, stop=True)
                    for h in range(H):
                        pe.matmul(heads(A + 2)[:, h, :], cT[:, h, chunk(c)], cT[:, H + h, chunk(c)], start=True, stop=True)
                    for h in range(H):
                        last = pe.transpose(heads(A + 3)[:, h, :], cT[:, 2 * H + h, chunk(c)], ident[:, :])
                    last.then_inc(kk_ready, 1)
                for c in (c0, c0 + 1):
                    s, A = c % 2, 4 * (c % 2)
                    pe.wait_ge(l_ready, c + 1)
                    pe.wait_ge(qkd_ready, c + 1)
                    for h in range(H):
                        pe.transpose(heads(A + 1)[:, h, :], LL[s][:, h, :], ident[:, :])
                    for h in range(H):
                        last = pe.transpose(heads(A + 2)[:, h, :], QKD[s][:, h, :], ident[:, :])
                    last.then_inc(lt_t, 1)
                for c in (c0, c0 + 1):
                    s, A = c % 2, 4 * (c % 2)
                    pe.wait_ge(bv_ready, c + 1)
                    for h in range(H):
                        last = pe.transpose(heads(A + 3)[:, h, :], cT[:, H + h, chunk(c)], ident[:, :])
                    last.then_inc(kn_ready, 1)
                for l in range(1, LEVELS):
                    for c in (c0, c0 + 1):
                        s, A = c % 2, 4 * (c % 2)
                        if l == 1:
                            pe.wait_ge(x0_ready, 2 * (c + 1))
                            pe.wait_ge(qkt_ready, c + 1)
                            pe.wait_ge(eg_ready, c + 1)
                        else:
                            pe.wait_ge(x_ready, level_seq(c, l - 1))
                        for h in range(H):
                            last = pe.matmul(heads(A)[:, h, :], LT[s][:, h, :], XX[s][:, h, :], start=True, stop=True)
                        last.then_inc(y_ready, 1)
                    for c in (c0, c0 + 1):
                        s, A = c % 2, 4 * (c % 2)
                        pe.wait_ge(ym_ready, level_seq(c, l))
                        if l < LEVELS - 1:
                            for h in range(H):
                                pe.matmul(heads(A + 1)[:, h, :], XT[s][:, h, :], LL[s][:, h, :], start=True, stop=True)
                        for h in range(H):
                            last = pe.matmul(heads(A + 2)[:, h, :], LL[s][:, h, :], XT[s][:, h, :], start=True, stop=True)
                        last.then_inc(z_ready, 1)
                for c in (c0, c0 + 1):
                    s, A = c % 2, 4 * (c % 2)
                    pe.wait_ge(x_ready, level_seq(c, LEVELS - 1))
                    pe.wait_ge(rk_ready, c + 1)
                    for h in range(H):
                        last = pe.matmul(heads(A + 1)[:, h, :], RK[s][:, h, :], XT[s][:, h, :], start=True, stop=True)
                    last.then_inc(wt_t, 1)
                for c in (c0, c0 + 1):
                    s, A = c % 2, 4 * (c % 2)
                    pe.wait_ge(wt_ready, c + 1)
                    if c:
                        pe.wait_ge(s_ready, c)
                    for h in range(H):
                        last = pe.matmul(heads(A)[:, h, :], XT[s][:, h, :], BV[s][:, h, :], start=True, stop=(c == 0))
                        if c:
                            last = pe.matmul(heads(A)[:, h, :], WT[s][:, h, :], ST[:, h, :], start=False, stop=True)
                    last.then_inc(u_ready, 1)
                    pe.wait_ge(vn_ready, c + 1)
                    pe.wait_ge(qg_ready, c + 1)
                    for h in range(H):
                        if c:
                            pe.matmul(heads(A + 2)[:, h, :], QG[s][:, h, :], ST[:, h, :], start=True, stop=False)
                        last = pe.matmul(heads(A + 2)[:, h, :], QKT[s][:, h, :], VN[s][:, h, :], start=(c == 0), stop=True)
                    last.then_inc(o_ready, 1)
                    for h in range(H):
                        last = pe.matmul(heads(A + 3)[:, h, :], KG[s][:, h, :], VN[s][:, h, :], start=True, stop=True)
                    last.then_inc(s_add, 1)
                for c in (c0, c0 + 1):
                    s, A = c % 2, 4 * (c % 2)
                    pe.wait_ge(m_ready, c + 1)
                    for h in range(H):
                        last = pe.transpose(heads(A + 1)[:, h, :], RK[s][:, h, :], ident[:, :])
                    last.then_inc(mt_ready, 1)

            pe.wait_ge(mlo_ready, NT)
            pe.wait_ge(m8_ready, 2)
            for i in range(16):
                src = cT[:, i, SEQ:TOK] if i < 12 else vzS[:, i - 8, :]
                last = pe.transpose(PS[0:NB, i // 4, (i % 4) * P:(i % 4 + 1) * P], src, ident[:, :])
            last.then_inc(pe_once, 1)
            pe.wait_ge(pool_once, AD_READY)
            pe.matmul(PS[:, 4, 0:32], ones[0:NB, :], a_diag.rearrange("p b h -> p (b h)"), start=True, stop=True).then_inc(pe_once, 1)
            pe.wait_ge(st_in, 16)
            pe.wait_ge(msk_ready, H)
            for h in range(H):
                for b in range(NB):
                    last = pe.matmul(PS[0:NB, 5, h * P:(h + 1) * P], msk[:, h, b, :], S_s[:, b * H + h, :], start=(b == 0),
                                     stop=(b == NB - 1))
            last.then_inc(pe_once, 1)
            pe.wait_ge(dve_once, DN_READY)
            for g in range(8):
                h, half = g // 2, g % 2
                pe.wait_ge(dmk_ready, h + 1)
                if g >= 4:
                    pe.wait_ge(st_ready, g - 3)
                pe.matmul(PS[:, g % 4, :], dN[:, H + h, :], dmk[:, h, 4 * half:4 * half + 4, :].rearrange("p b e -> p (b e)"),
                          start=True, stop=True).then_inc(outer_ready, 1)
            pe.wait_ge(st_ready, 8)
            pe.wait_ge(msk_ready, 2 * H)
            for h in range(H):
                for b in range(NB):
                    last = pe.matmul(PS[0:NB, 4, h * P:(h + 1) * P], msk[:, h, b, :], S_s[:, b * H + h, :], start=(b == 0),
                                     stop=(b == NB - 1))
            last.then_inc(pe_once, 1)
            pe.wait_ge(dve_once, SM_READY)
            for h in range(H):
                last = pe.transpose(PS[:, 5, h * NB:(h + 1) * NB], dlt[:, h, :], ident[0:NB, 0:NB])
            last.then_inc(pe_once, 1)

            pe.wait_ge(dve_once, SMLO_READY)
            for h in range(H):
                if h >= 2:
                    pe.wait_ge(db_ready, h - 1)
                for g in range(2):
                    last = pe.matmul(PS[:, 2 * (h % 2) + g, :], ident[96:100, 96 + h:97 + h].to_broadcast([4, P]),
                                     T1[96:100, g * 512:(g + 1) * 512], start=True, stop=True)
                last.then_inc(d_spread, 1)
            pe.wait_ge(dve_once, MX_READY)
            pe.transpose(PS[0:32, 4, 0:P], mx, ident[:, :]).then_inc(pe_once, 1)
            pe.wait_ge(dve_once, MD_READY)
            pe.matmul(PS[:, 5, 0:32], ones[0:32, :], mdiag, start=True, stop=True).then_inc(pe_once, 1)
            for h in range(H):
                pe.transpose(PS[0:NB, 4, h * P:(h + 1) * P], vzS[:, h, :], ident[:, :])
            pe.wait_ge(dve_once, SJ_READY)
            pe.matmul(PS[:, 5, 32:64], ones[:, :], sj, start=True, stop=True).then_inc(pe_once, 1)
            pe.wait_ge(v_in, 16)
            pe.wait_ge(db_ready, H)
            pe.wait_ge(dv_ready, 1)
            for n in range(NAI + 3):
                if n < NAI:
                    i, h, w = n // H, n % H, P * (n // H + 1)
                    if n >= 2:
                        pe.wait_ge(sc_step, 2 * (n - 2) + 1)
                    for g in range(0, w, 512):
                        last = pe.matmul(PS[:, 2 * (n % 2) + g // 512, 0:min(512, w - g)], qT[:, h, chunk(i)],
                                         kT[:, h, g:min(g + 512, w)], start=True, stop=True)
                    last.then_inc(qk_ready, 1)
                m = n - 1
                if 0 <= m < NAI:
                    pe.wait_ge(p_ready, m + 1)
                    if m >= 1:
                        pe.wait_ge(pt_ready, m)
                    for k in range(m // H + 1):
                        last = pe.transpose(PS[:, 4 + k // 4, (k % 4) * P:(k % 4 + 1) * P], sc[:, m % 2, k * P:(k + 1) * P], ident[:, :])
                    last.then_inc(pt_t, 1)
                m = n - 2
                if 0 <= m < NAI:
                    i, h = m // H, m % H
                    pe.wait_ge(pt_ready, m + 1)
                    if h == 0 and i >= 2:
                        pe.wait_ge(dv_ready, i)
                    for k in range(i + 1):
                        last = pe.matmul(heads(6 + i % 2)[:, h, :], pT[:, m % 2, k, :], vN[:, k, h * P:(h + 1) * P],
                                         start=(k == 0), stop=(k == i))
                    last.then_inc(pv_ready, 1)
                if n >= H + 2 and (n - 2) % H == 0:
                    i = (n - 2) // H - 1
                    pe.wait_ge(on_ready, i + 1)
                    for h in range(H):
                        last = pe.transpose(heads(6 + i % 2)[:, h, :], oN[:, i % 2, h, :], ident[:, :])
                    last.then_inc(ot_ready, 1)
                if n % H == H - 1 and H < n < NAI:
                    r = n // H
                    pe.wait_ge(otlo_ready, r)
                    samples = [r - 1] if r < NT - 1 else [r - 1, r]
                    for b in samples:
                        pe.wait_ge(v_used, NPG * (b + 1))
                        last = pe.matmul(PS[0:NB, 7 - r % 2, :], m8[:, b, :], av[b % 3][:, :], start=(b == samples[0]), stop=(b == samples[-1]))
                    last.then_inc(dv_t, 1)
            pe.wait_ge(dv_ready, NT)
            for h in range(H):
                last = pe.transpose(PS[:, 4, h * NB:(h + 1) * NB], dv[:, h * P:(h + 1) * P], ident[0:NB, 0:NB])
            last.then_inc(pe_once, 1)

            for t in range(NT9 + 1):
                if t < NT9:
                    r, b = rows_of(t), 2 * (t % 2)
                    cs = slice(t * P, t * P + r)
                    if t == 0:
                        pe.wait_ge(dve_once, DOLO_READY)
                    if t >= 2:
                        pe.wait_ge(h_ready, t - 1)
                    for k in range(KT):
                        if t == 0:
                            pe.wait_ge(wo_lo_ready, k + 1)
                        for a, w in ((act_hi, wo_hi), (act_hi, wo_lo), (act_lo, wo_hi)):
                            for f in range(2):
                                last = pe.matmul(PS[0:r, b + f, :], a[:, k, cs], w[:, k, f * 512:(f + 1) * 512],
                                                 start=(k == 0 and a is act_hi and w is wo_hi), stop=(k == KT - 1 and a is act_lo))
                    last.then_inc(h_t, 1)
                if t >= 1:
                    u, r = t - 1, rows_of(t - 1)
                    pe.wait_ge(xm_ready, u + 1)
                    if u >= 2:
                        pe.wait_ge(a2lo_ready, u - 1)
                    for k in range(KT):
                        last = pe.transpose(PS[:, 4 + 2 * (u % 2) + k // 4, (k % 4) * P:(k % 4) * P + r],
                                            xm[0:r, u % 2, k * P:(k + 1) * P], ident[0:r, 0:r])
                    last.then_inc(xmt_ready, 1)
            pe.wait_ge(a2lo_ready, NT9)
            pe.wait_ge(lo_done, 5)

            def pe_group(g, last_group):
                for k in range(GB):
                    b = 3 * (k % 2)
                    pe.wait_ge(lo_done, 8 * g + 2 * k + 4)
                    pe.wait_ge(relu_done, GB * g + k + 1)
                    if k == 0:
                        pe.wait_ge(y_add, NT9 * g + 1)
                    for half, operands in ((0, (act_hi, act_lo)), (1, (act_hi,))):
                        w = (wu_hi, wu_lo)[half]
                        for kt in range(KT):
                            for f in range(3):
                                for a in operands:
                                    last = pe.matmul(PS[:, b + f, 0:G3], w[:, k % 2, kt, :], a[:, kt, f * G3:(f + 1) * G3],
                                                     start=(half == 0 and kt == 0 and a is act_hi), stop=(half == 1 and kt == KT - 1))
                    last.then_inc(up_done, 1)
                for t in range(NT9):
                    r, b = rows_of(t), 0 if t % 2 else 6
                    cs = slice(t * P, t * P + r)
                    if t == 1:
                        pe.wait_ge(relu_done, GB * g + 5)
                    if t >= 2:
                        pe.wait_ge(y_add, NT9 * g + t)
                    for k in range(GB):
                        if t == 0:
                            pe.wait_ge(u_lo_done, GB * g + k + 2)
                            pe.wait_ge(lo_done, 8 * g + 2 * k + 7 - (last_group and k == 3))
                        for a, w in ((u_hi, wd_hi), (u_hi, wd_lo), (u_lo, wd_hi)):
                            for f in range(2):
                                last = pe.matmul(PS[0:r, b + f, :], a[:, k, cs], w[:, k, f * 512:(f + 1) * 512],
                                                 start=(k == 0 and a is u_hi and w is wd_hi), stop=(k == GB - 1 and a is u_lo))
                    last.then_inc(dn_tile, 1)

            with pe.Fori(0, NG - 1) as g:
                pe_group(g, False)
            pe_group(NG - 1, True)


_INS = ("x_prompt", "x_sample", "cache_k", "cache_v", "cache_lf", "page_table", "state_conv", "state_ssm", "ln1", "w_in", "b_f",
        "w_conv", "a_log", "dt_bias", "w_gnorm", "w_o", "ln2", "w_up", "w_down", "ln_f")
_OUTS = ((1, SEQ, D), (NB, 1, D),
         (1, 1, SEQ, H, HD), (1, 1, SEQ, H, HD), (1, 1, SEQ, H), (1, 1, CW - 1, CONV), (1, 1, H, HD, HD),
         (1, NB, 1, H, HD), (1, NB, 1, H, HD), (1, NB, 1, H), (1, NB, CW - 1, CONV), (1, NB, H, HD, HD))


def kernel(**inputs):
    import numpy as _np
    import concourse.bacc as _bacc
    from concourse.bass_utils import run_bass_kernel_spmd as _run

    nc = _bacc.Bacc("TRN2", target_bir_lowering=False, num_devices=1)
    arrays, args = {}, []
    for name in _INS:
        a = _np.ascontiguousarray(inputs[name])
        arrays[f"in_{name}"] = a
        args.append(nc.dram_tensor(f"in_{name}", a.shape, mybir.dt.from_np(a.dtype), kind="ExternalInput").ap())
    for i, shape in enumerate(_OUTS):
        args.append(nc.dram_tensor(f"out_{i}", shape, F32, kind="ExternalOutput").ap())
    hymba_step(nc, *args)
    r = _run(nc, [arrays], core_ids=[0])
    return tuple(r.results[0][f"out_{i}"] for i in range(len(_OUTS)))
```

```python
from contextlib import ExitStack

import concourse.bass as bass
from concourse import mybir

F32 = mybir.dt.float32
F32R = mybir.dt.float32r
I32 = mybir.dt.int32
ALU = mybir.AluOpType
ACT = mybir.ActivationFunctionType
AX = mybir.AxisListType

P = 128
SEQ = 1024
NB = 8
D = 1024
KT = D // P
NT = SEQ // P
TOK = SEQ + NB
G3 = TOK // 3
H = 4
HD = 128
MIX = 512
CONV = 3 * MIX
CW = 4
PAGE = 128
NPG = 8
EPS = 1e-6
SCALE = float(HD) ** -0.5
NEG = -1e30
LEVELS = 7
SBUF0 = 16640

C_QA, C_KA, C_VA, C_FA = 0, MIX, 2 * MIX, 3 * MIX
C_CV = 3 * MIX + H
C_Z = C_CV + CONV
C_BB = C_Z + MIX
C_AA = C_BB + H


def hymba_step(nc, x_prompt, x_sample, cache_k, cache_v, cache_lf, page_table, state_conv, state_ssm,
               ln1, w_in, b_f, w_conv, a_log, dt_bias, w_gnorm, w_o, ln2, w_up, w_down, ln_f,
               y_prompt, y_sample, k_prompt, v_prompt, lf_prompt, conv_prompt, ssm_prompt,
               k_sample, v_sample, lf_sample, conv_sample, ssm_sample):
    z_rows = nc.dram_tensor("z_rows", [SEQ, MIX], F32).ap()

    q_rows = nc.dram_tensor("q_rows", [NB, MIX], F32).ap()

    ctx = ExitStack()
    with ctx:
        def sem(name):
            return ctx.enter_context(nc.semaphore(name))

        def place(name, shape, at, dt=F32):
            return nc.alloc_sbuf_tensor_at(name, shape, dt, offset=SBUF0 + at)

        ctx.enter_context(nc.sbuf_tensor("fence", [P, 53000], F32))
        PS = ctx.enter_context(nc.psum_tensor("PS", [P, 8, 512], F32))

        ident = place("ident", [P, P], 0)
        ones = place("ones", [P, P], 512)
        incl = place("incl", [P, P], 1024)
        strict = place("strict", [P, P], 1536)
        stat = place("stat", [P, 64], 2048)
        gN = place("gN", [P, NT + 1, 72], 2304)
        act_hi = place("act_hi", [P, KT, TOK], 5120, F32R)
        act_lo = place("act_lo", [P, KT, TOK], 38144, F32R)

        w_raw = place("w_raw", [P, 2, KT, P], 71168)
        w_hi = place("w_hi", [P, 2, KT, P], 79360, F32R)
        w_lo = place("w_lo", [P, 2, KT, P], 87552, F32R)
        kT = place("kT", [P, H, TOK], 95744)
        qT = place("qT", [P, H, TOK], 112256)
        cT = place("cT", [P, 12, TOK], 128768)
        gateT = place("gateT", [P, TOK], 178304)
        cb = place("cb", [P, 2, 1040], 182432)
        acc = place("acc", [P, TOK], 190752)
        nat = place("nat", [P, 2, NT, P], 194880)
        tail = place("tail", [P, 12, 11], 203072)
        vzS = place("vzS", [P, 8, NB], 203616)
        hw = place("hw", [P, 12, 28], 203872)
        hrows = place("hrows", [28, CONV], 194880)
        x_t = place("x_t", [P, 3, D], 128768)
        xn = place("xn", [P, 2, D], 141056)
        lnb = place("lnb", [P, D], 149248)
        junk = place("junk", [P, D], 153344)

        pe_once = sem("pe_once")
        (HW_T, GN_T, CLF_T, BIAS_T, CT_T, SN_T, SELF_T, MX_T, M_SPREAD, SUM_SPREAD, DN_T, A_SPREAD,
        PRED_READY, SO_READY, SMT_READY, VS_T, DVT_READY) = range(1, 18)
        dve_once = sem("dve_once")
        (GATE_ABS, GATE_MIN, T1_READY, CLF_READY, CT_READY, SN_READY, BEK_READY, MX_READY, MD_READY,
        SJ_READY, PD_READY, DN_READY, SM_READY, SMLO_READY, DOLO_READY) = range(1, 16)
        act_once = sem("act_once")
        (EN_READY, A_READY, A_ALL_READY, SORS_READY, SMHI_READY, DOHI_READY) = range(1, 7)
        pool_once = sem("pool_once")
        (EPS_READY, GATE_ZERO, PAD_ZERO, BIAS_ZERO, AD_READY) = range(1, 6)

        consts = sem("consts")
        ln_in = sem("ln_in")
        std_ready = sem("std_ready")
        x_in = [sem(f"x_in{i}") for i in range(3)]
        xn_ready = sem("xn_ready")
        xt_ready = sem("xt_ready")
        act_hi_ready = sem("act_hi_ready")
        act_lo_ready = sem("act_lo_ready")
        hist_in = sem("hist_in")
        w_in_sem = [sem(f"w_raw{i}") for i in range(2)]
        w_hi_ready = sem("w_hi_ready")
        w_lo_ready = sem("w_lo_ready")
        block_done = sem("block_done")
        evacuated = sem("evacuated")
        dve_step = sem("dve_step")
        act_step = sem("act_step")
        conv_ready = sem("conv_ready")
        silu_done = sem("silu_done")
        cb_free = sem("cb_free")
        nat_t = sem("nat_t")
        nat_ready = sem("nat_ready")
        nat_out = [sem(f"nat_out{i}") for i in range(2)]
        out_done = sem("out_done")

        lm = place("lm", [P, LEVELS + 1, P], 205216)
        T1 = gateT
        ge = place("ge", [P, TOK], 112256)
        gs = place("gs", [P, TOK], 116384)
        cm = place("cm", [P, SEQ], 120512)
        sq = place("sq", [P, 2, SEQ], 112256)
        rn = place("rn", [P, 2, SEQ], 120512)
        small = place("small", [P, 320], 211360)
        wgn = place("wgn", [P, P], 203872)

        def tiles(name, slots):
            return [place(f"{name}{i}", [P, H, P], at) for i, at in enumerate(slots)]

        low = [71168 + 2048 * i for i in range(12)]
        high = [182432 + 2048 * i for i in range(10)]
        DEC = tiles("DEC", low[0:2])
        LL = tiles("LL", low[2:4])
        LT = tiles("LT", low[4:6])
        QKD = tiles("QKD", low[6:8])
        QKT = tiles("QKT", low[8:10])
        XX = tiles("XX", low[10:12])
        XT = tiles("XT", high[0:2])
        RK = tiles("RK", high[2:4])
        KG = tiles("KG", high[4:6])
        QG = tiles("QG", high[6:8])
        ZZ = tiles("ZZ", [high[9], 50432])
        OO = tiles("OO", [46336, 48384])
        above = place("above", [P, P], 204384)
        SG, ST = tiles("SG", [high[8]])[0], tiles("ST", [209312])[0]
        BV, WT, VN = QKD, XX, DEC
        E_N, B_EK = small[:, 0:32].rearrange("p (c h) -> p c h", h=H), small[:, 32:64].rearrange("p (c h) -> p c h", h=H)

        def sm(s, i):
            return small[:, 64 + 32 * s + 4 * i:68 + 32 * s + 4 * i]
        GLC, KGS, EL, OSS, OLN, ORS = range(6)

        bias_in = sem("bias_in")
        wgn_in = sem("wgn_in")
        masks = sem("masks")
        NMASK = 3 * LEVELS + 2
        t1_zero = sem("t1_zero")
        gate_act = sem("gate_act")
        gn_ready = sem("gn_ready")
        sq_ready = sem("sq_ready")
        ss_ready = sem("ss_ready")
        sd_ready = sem("sd_ready")
        normed = sem("normed")

        gb_ready = sem("gb_ready")
        kk_ready = sem("kk_ready")
        dif_ready = sem("dif_ready")
        eg_ready = sem("eg_ready")
        dexp_ready = sem("dexp_ready")
        oo_ready = sem("oo_ready")
        l_ready = sem("l_ready")
        qkd_ready = sem("qkd_ready")
        lt_t = sem("lt_t")
        lt_ready = sem("lt_ready")
        qkt_ready = sem("qkt_ready")
        x_step = sem("x_step")
        x0_ready = sem("x0_ready")
        xt0_ready = sem("xt0_ready")
        bv_ready = sem("bv_ready")
        kn_ready = sem("kn_ready")
        rk_ready = sem("rk_ready")
        y_ready = sem("y_ready")
        ym_ready = sem("ym_ready")
        z_ready = sem("z_ready")
        x_ready = sem("x_ready")
        wt_t = sem("wt_t")
        wt_ready = sem("wt_ready")
        qg_ready = sem("qg_ready")
        sg_ready = sem("sg_ready")
        u_ready = sem("u_ready")
        vn_ready = sem("vn_ready")
        o_ready = sem("o_ready")
        s_add = sem("s_add")
        s_ready = sem("s_ready")
        ors_ready = sem("ors_ready")
        og_ready = sem("og_ready")
        z_in = [sem(f"z_in{i}") for i in range(2)]
        m_ready = sem("m_ready")
        mt_ready = sem("mt_ready")
        mhi_ready = sem("mhi_ready")
        mlo_ready = sem("mlo_ready")

        def chunk(c):
            return slice(c * P, (c + 1) * P)

        def heads(b):
            return PS[:, b, :].rearrange("p (h d) -> p h d", h=H)

        def per_head(ap):
            return ap.unsqueeze(2).to_broadcast([ap.shape[0], H, P])

        def over_heads(ap):
            return ap.unsqueeze(1).to_broadcast([P, H, P])

        def level_seq(c, l):
            return (c // 2) * 12 + (l - 1) * 2 + c % 2 + 1

        ct = place("ct", [11, 12, P], 87680)
        S_s = place("S_s", [P, NB * H, P], 75296)
        dlt = place("dlt", [NB, H, P], 91680)
        msk = place("msk", [P, H, NB, NB], 93728)
        dmk = place("dmk", [NB, H, NB, P], 178304)
        dN = place("dN", [NB, 16, P], 194688)
        m8 = small[:, 200:264].rearrange("p (a b) -> p a b", b=NB)
        a_row = small[0:NB, 264:268]
        a_diag = small[0:NB, 128:160].rearrange("p (b h) -> p b h", h=H)
        a_all = small[:, 160:192]
        s_oss, s_oln, s_ors = small[0:NB, 268:272], small[0:NB, 272:276], small[0:NB, 276:280]

        ct_out = sem("ct_out")
        m8_ready = sem("m8_ready")
        st_in = sem("st_in")
        msk_ready = sem("msk_ready")
        dmk_ready = sem("dmk_ready")
        outer_ready = sem("outer_ready")
        st_ready = sem("st_ready")

        D_hi = place("D_hi", [P, SEQ], 128768, F32R)
        D_lo = place("D_lo", [P, SEQ], 132864, F32R)
        less = place("less", [P, H, P], 136960, F32R)
        eye = place("eye", [P, P], 139008, F32R)
        neg = place("neg", [P, P], 139520, F32R)
        vN = place("vN", [P, NT, MIX], 145152)
        sc = place("sc", [P, 2, SEQ], 161536)
        pT = place("pT", [P, 2, NT, P], 169728)
        oN = place("oN", [P, 2, H, P], 178304)
        arow = place("arow", [P, 3, NT * H], 182400)

        v_in = sem("v_in")
        bias_ready = sem("bias_ready")
        qk_ready = sem("qk_ready")
        max_ready = sem("max_ready")
        p_ready = sem("p_ready")
        pt_t = sem("pt_t")
        pt_ready = sem("pt_ready")
        pv_ready = sem("pv_ready")
        on_ready = sem("on_ready")
        ot_ready = sem("ot_ready")
        othi_ready = sem("othi_ready")
        otlo_ready = sem("otlo_ready")
        NAI = NT * H

        NR, NV = 4, 16
        kpages = place("kpages", [P, NR, MIX], 38144)
        qb = place("qb", [P, NB, MIX], 5120)
        sfx = place("sfx", [P, NB, NPG, H], 52480)
        s9 = place("s9", [P, NB, H, NPG], 53504)
        lf_rows = place("lf_rows", [NB * NPG, PAGE * H], 209312)
        clf = place("clf", [P, NB, NPG, H], 190752)
        pre = place("pre", [P, 256], 191776)
        sN = place("sN", [NB, 12, P], 196736)
        run_ = pre[:, 0:32].rearrange("p (b h) -> p b h", h=H)
        lf_diag = pre[0:NB, 32:64].rearrange("p (b h) -> p b h", h=H)
        self_diag = small[0:NB, 280:312].rearrange("p (b h) -> p b h", h=H)
        self_s = pre[0:NB, 96:100]
        ssq, srn = pre[:, 128:192], pre[:, 192:256]
        prod = place("prod", [NB, P], 192800)

        vpages = [place(f"vpages{i}", [P, 8, MIX], at) for i, at in enumerate((184320, 75296))]
        av = [place(f"av{i}", [P, MIX], at) for i, at in enumerate((91680, 205216, 207264))]
        dv = place("dv", [NB, MIX], 200704)
        pp = place("pp", [P, NB, H, NPG], 71168)
        dm_ = place("dm_", [P, 352], 72192)
        self_sc = dm_[:, 0:32]
        mx = dm_[:, 32:64]
        m_all = dm_[:, 64:96]
        self_e = dm_[:, 96:128]
        sj = dm_[:, 128:160]
        inv = dm_[:, 160:192]
        p_diag = dm_[0:NB, 256:288].rearrange("p (h b) -> p h b", b=NB)
        self_p = dm_[0:NB, 296:300]
        mcol = dm_[0:32, 292:293]
        mdiag = dm_[0:32, 320:352]

        table = place("table", [NB, NPG], 4896, I32)

        table_in = sem("table_in")
        kpage_in = [sem(f"kpage_in{i}") for i in range(NR)]
        vpage_in = [sem(f"vpage_in{i}") for i in range(2)]
        clf_in = sem("clf_in")
        sn_out = sem("sn_out")
        q_out = sem("q_out")
        qb_in = sem("qb_in")
        k_made = sem("k_made")
        k_used = sem("k_used")
        v_used = sem("v_used")
        pv_made = sem("pv_made")
        dv_t = sem("dv_t")
        dv_ready = sem("dv_ready")
        diag_ready = sem("diag_ready")
        pre_read = sem("pre_read")
        sh_ready = sem("sh_ready")
        e_ready = sem("e_ready")

        def vpage(n):
            return vpages[n % NV // 8][:, n % 8, :]

        wo_hi = place("wo_hi", [P, KT, D], 71168, F32R)
        wo_lo = place("wo_lo", [P, KT, D], 103936, F32R)
        x_r = place("x_r", [P, 2, D], 136704)
        xm = place("xm", [P, 2, D], 144896)
        ln2b = place("ln2b", [P, D], 206592)
        NG, GB = 8, 4
        u_hi = place("u_hi", [P, GB, TOK], 71168, F32R)
        u_lo = place("u_lo", [P, GB, TOK], 87680, F32R)
        wu_hi = place("wu_hi", [P, 2, KT, P], 104192, F32R)
        wu_lo = place("wu_lo", [P, 2, KT, P], 112384, F32R)
        wd_hi = place("wd_hi", [P, GB, D], 120576, F32R)
        wd_lo = place("wd_lo", [P, GB, D], 136960, F32R)
        raw_o = place("raw_o", [P, 4, D], 184320)
        raw = place("raw", [P, 4, D], 153344)
        y = place("y", [P, NT + 1, D], 169728)
        r_sq = place("r_sq", [P, TOK], 206592)
        lnfb = place("lnfb", [P, D], 104192)
        junk2 = place("junk2", [P, D], 112384)

        ln2_in = sem("ln2_in")
        raw_in = [sem(f"raw_in{i}") for i in range(4)]
        wo_hi_ready = sem("wo_hi_ready")
        wo_lo_ready = sem("wo_lo_ready")
        xr_in = [sem(f"xr_in{i}") for i in range(2)]
        h_t = sem("h_t")
        h_ready = sem("h_ready")
        std2_ready = sem("std2_ready")
        xm_ready = sem("xm_ready")
        xmt_ready = sem("xmt_ready")
        a2hi_ready = sem("a2hi_ready")
        a2lo_ready = sem("a2lo_ready")
        hi_done = sem("hi_done")
        lo_done = sem("lo_done")
        up_done = sem("up_done")
        relu_done = sem("relu_done")
        sq_done = sem("sq_done")
        u_hi_done = sem("u_hi_done")
        u_lo_done = sem("u_lo_done")
        dn_tile = sem("dn_tile")
        y_add = sem("y_add")
        lnf_in = sem("lnf_in")
        std3_ready = sem("std3_ready")
        out_ready = sem("out_ready")
        y_out = [sem(f"y_out{i}") for i in range(4)]
        NT9 = NT + 1
        up_v = w_up[0].rearrange("(kt p) (q c) -> q p kt c", p=P, c=P)
        dn_v = w_down[0].rearrange("(q p) n -> q p n", p=P)

        GATE, CV0, NAT0, Q0, NBLK = 0, 1, 13, 25, 29
        cols = [None] + [C_CV + i * P for i in range(12)] + [C_KA + i * P for i in range(4)] \
            + [C_VA + i * P for i in range(4)] + [C_Z + i * P for i in range(4)] + [C_QA + i * P for i in range(4)]

        NS0 = 15

        def raw_count(n):
            return 48 + 16 * (n // 2) if n % 2 == 0 else 16 * (n // 2 + 1)

        def cb_use(n):
            return n - CV0 if CV0 <= n < NAT0 else n - 17 + 12 if 17 <= n < Q0 else None

        def nat_dst(i):
            h = i % 4
            rows = [k_prompt[0, 0, :, h, :], v_prompt[0, 0, :, h, :], z_rows[:, h * P:(h + 1) * P]][i // 4]
            return rows.rearrange("(t p) d -> p t d", p=P)

        def rows_of(t):
            return P if t < NT else NB

        block = ctx.enter_context(nc.Block())

        @block.sync
        def _(sp):
            def load_page(src, n):
                page = sp.value_load(table[n // NPG:n // NPG + 1, n % NPG:n % NPG + 1], min_val=0, max_val=cache_k.shape[1] - 1)
                return src[0, bass.ds(page, 1)]

            sp.dma_start(table[:, :], page_table[:, :]).then_inc(table_in, 16)

            sp.dma_start(lnb[:, :], ln1[0:1, :].to_broadcast([P, D])).then_inc(ln_in, 16)
            for t in range(NT + 1):
                if t >= 3:
                    sp.wait_ge(xn_ready, t - 2)
                src = x_prompt[0, t * P:(t + 1) * P, :] if t < NT else x_sample[:, 0, :]
                sp.dma_start(x_t[0:rows_of(t), t % 3, :], src).then_inc(x_in[t % 3], 16)
                if t == 0:
                    sp.dma_start(hrows[0:24, :], state_conv[0].rearrange("b i c -> (b i) c")).then_inc(hist_in, 16)
                    sp.dma_start(hrows[24:28, :], w_conv[0]).then_inc(hist_in, 16)
                if t == 2:
                    sp.wait_ge(pool_once, GATE_ZERO)
                    for row, c in ((0, C_FA), (32, C_BB), (64, C_AA)):
                        sp.dma_start(w_raw[:, 0, :, row:row + H],
                                     w_in[0, :, c:c + H].rearrange("(kt p) c -> p kt c", p=P)).then_inc(w_in_sem[0], 16)
            sp.dma_start(conv_sample[0, :, 0:2, :], state_conv[0, :, 1:3, :]).then_inc(out_done, 16)
            sp.wait_ge(pool_once, BIAS_ZERO)
            sp.dma_start(stat[0:H, 50:51], b_f[0:1, :].rearrange("a h -> h a")).then_inc(bias_in, 16)
            sp.dma_start(stat[64:64 + H, 50:51], dt_bias[0:1, :].rearrange("a h -> h a")).then_inc(bias_in, 16)
            sp.dma_start(stat[64:64 + H, 51:52], a_log[0:1, :].rearrange("a h -> h a")).then_inc(bias_in, 16)
            for n in range(1, NBLK):
                if n >= 2:
                    sp.wait_ge(w_lo_ready, n - 1)
                sp.dma_start(w_raw[:, n % 2, :, :],
                             w_in[0, :, cols[n]:cols[n] + P].rearrange("(kt p) c -> p kt c", p=P)).then_inc(w_in_sem[n % 2], 16)
                if n >= 4:
                    sp.wait_ge(table_in, 16)
                    for j in range(3 * (n - 4), min(3 * (n - 3), NB * NPG)):
                        sp.dma_start(lf_rows[j:j + 1, :], load_page(cache_lf, j).rearrange("a p h -> a (p h)")).then_inc(clf_in, 16)
                i = n - 3 - NAT0
                if 0 <= i < 12:
                    sp.wait_ge(nat_ready, i + 1)
                    sp.dma_start(nat_dst(i), nat[:, i % 2, :, :]).then_inc(nat_out[i % 2], 16)

            sp.wait_ge(dve_once, CT_READY)
            sp.dma_start(conv_prompt[0, 0, :, :], ct[0:3, :, :].rearrange("i c d -> i (c d)")).then_inc(ct_out, 16)
            sp.dma_start(conv_sample[0, :, 2, :], ct[3:11, :, :].rearrange("i c d -> i (c d)")).then_inc(ct_out, 16)
            sp.wait_ge(conv_ready, 12)
            sp.dma_start(wgn[:, :], w_gnorm[0:1, :].to_broadcast([P, P])).then_inc(wgn_in, 16)
            sp.wait_ge(gn_ready, 6)
            sp.dma_start(lf_prompt[0, 0, :, :].rearrange("(t p) h -> p t h", p=P), gN[:, 0:NT, 0:H]).then_inc(out_done, 16)
            sp.dma_start(lf_sample[0, :, 0, :], gN[0:NB, NT, 0:H]).then_inc(out_done, 16)
            sp.wait_ge(nat_out[0], 96)
            sp.wait_ge(nat_out[1], 96)
            sp.wait_ge(block_done, NBLK)
            for n in range(NR):
                sp.dma_start(kpages[:, n, :], load_page(cache_k, n).rearrange("a p h d -> (a p) (h d)")).then_inc(kpage_in[n], 16)
            sp.wait_ge(dve_once, SN_READY)
            sp.dma_start(q_rows.rearrange("b (h d) -> b h d", h=H), sN[:, 0:4, :]).then_inc(q_out, 16)
            sp.dma_start(k_sample[0, :, 0, :, :], sN[:, 4:8, :]).then_inc(sn_out, 16)
            sp.dma_start(v_sample[0, :, 0, :, :], sN[:, 8:12, :]).then_inc(sn_out, 16)
            sp.wait_ge(q_out, 16)
            sp.dma_start(qb[:, :, :], q_rows.rearrange("(a b) n -> a b n", a=1).to_broadcast([P, NB, MIX])).then_inc(qb_in, 16)
            for c in range(NT):
                if c % 2 == 0:
                    for n in range(max(NR, 16 * (c // 2)), 16 * (c // 2 + 1)):
                        sp.wait_ge(k_used, n - NR + 1)
                        sp.dma_start(kpages[:, n % NR, :], load_page(cache_k, n).rearrange("a p h d -> (a p) (h d)"))\
                            .then_inc(kpage_in[n % NR], 16)
                if c >= 2:
                    sp.wait_ge(m_ready, c - 1)
                sp.dma_start(ZZ[c % 2][:, :, :], z_rows[chunk(c), :].rearrange("p (h d) -> p h d", h=H)).then_inc(z_in[c % 2], 16)
            sp.wait_ge(s_ready, NT)
            sp.dma_start(ssm_prompt[0, 0].rearrange("h d e -> d h e"), ST[:, :, :]).then_inc(out_done, 16)

            sp.wait_ge(m_ready, NT)
            sp.wait_ge(s_add, NT)
            sp.dma_start(S_s[:, :, :], state_ssm[0].rearrange("b h d e -> d (b h) e")).then_inc(st_in, 16)
            sp.wait_ge(st_ready, 8)
            sp.dma_start(ssm_sample[0].rearrange("b h d e -> d (b h) e"), S_s[:, :, :]).then_inc(out_done, 16)

            sp.wait_ge(pe_once, SO_READY)
            sp.wait_ge(msk_ready, 2 * H)
            sp.dma_start(vN[:, :, :], v_prompt[0, 0].rearrange("(t p) h d -> p t (h d)", p=P)).then_inc(v_in, 16)
            sp.wait_ge(dve_once, SM_READY)
            for n in range(NB * NPG):
                if n == NPG:
                    sp.wait_ge(out_done, 5 * 16)
                if n >= NV:
                    sp.wait_ge(v_used, n - NV + 1)
                sp.dma_start(vpage(n), load_page(cache_v, n).rearrange("a p h d -> (a p) (h d)")).then_inc(vpage_in[n // NPG % 2], 16)

            sp.wait_ge(v_used, NB * NPG)
            for k in range(KT):
                if k >= 4:
                    sp.wait_ge(wo_lo_ready, k - 3)
                sp.dma_start(raw_o[:, k % 4, :], w_o[0, k * P:(k + 1) * P, :]).then_inc(raw_in[k % 4], 16)
            sp.wait_ge(dve_once, DOLO_READY)
            sp.wait_ge(otlo_ready, NT)
            sp.dma_start(ln2b[:, :], ln2[0:1, :].to_broadcast([P, D])).then_inc(ln2_in, 16)
            for t in range(NT9):
                if t >= 2:
                    sp.wait_ge(h_ready, t - 1)
                src = x_prompt[0, t * P:(t + 1) * P, :] if t < NT else x_sample[:, 0, :]
                sp.dma_start(x_r[0:rows_of(t), t % 2, :], src).then_inc(xr_in[t % 2], 16)

            def load_up(q, slot):
                sp.dma_start(raw[:, slot, :].rearrange("p (kt c) -> p kt c", c=P),
                             up_v[bass.ds(q, 1), :, :, :].rearrange("a p kt c -> (a p) kt c")).then_inc(raw_in[slot], 16)

            def load_dn(q, slot):
                sp.dma_start(raw[:, slot, :], dn_v[bass.ds(q, 1), :, :].rearrange("a p n -> (a p) n")).then_inc(raw_in[slot], 16)

            sp.wait_ge(wo_lo_ready, KT)
            load_up(0, 0)
            load_up(1, 1)

            def sync_group(g, last):
                for k in range(GB):
                    sp.wait_ge(lo_done, 8 * g + 2 * k + 3)
                    load_dn(GB * g + k, (2 * k + 2) % 4)
                    if not (last and k >= 2):
                        sp.wait_ge(lo_done, 8 * g + 2 * k + 4)
                        load_up(GB * g + k + 2, (2 * k + 3) % 4)

            with sp.Fori(0, NG - 1) as g:
                sync_group(g, False)
            sync_group(NG - 1, True)
            sp.wait_ge(up_done, GB * NG + 2)
            sp.dma_start(lnfb[:, :], ln_f.rearrange("(a n) -> a n", a=1).to_broadcast([P, D])).then_inc(lnf_in, 16)
            for t in range(NT9):
                sp.wait_ge(out_ready, t + 1)
                dst = y_prompt[0, t * P:(t + 1) * P, :] if t < NT else y_sample[:, 0, :]
                sp.dma_start(dst, raw[0:rows_of(t), t % 4, :]).then_inc(y_out[t % 4], 16)
            for i in range(4):
                sp.wait_ge(y_out[i], 16 * len(range(i, NT9, 4)))
            sp.wait_ge(out_done, 5 * 16)
            sp.wait_ge(sn_out, 32)
            sp.wait_ge(ct_out, 32)

        @block.gpsimd
        def _(pool):
            pool.memset(ones[:, :], 1.0).then_inc(consts, 1)
            pool.memset(stat[:, 42:43], EPS).then_inc(pool_once, 1)
            pool.memset(w_raw[:, 0, :, :], 0.0).then_inc(pool_once, 1)
            pool.wait_ge(consts, 1)
            for m, op, fill in ((ident, ALU.is_equal, 0.0), (incl, ALU.is_ge, 0.0), (strict, ALU.is_gt, 0.0)):
                pool.affine_select(out=m[:, :], in_=ones[:, :], compare_op=op, fill=fill, base=0,
                                   pattern=[[-1, P]], channel_multiplier=1).then_inc(consts, 1)
            pool.memset(cb[:, :, 0:3], 0.0).then_inc(pool_once, 1)

            pool.memset(stat[:, 50:52], 0.0).then_inc(pool_once, 1)
            pool.wait_ge(pool_once, BIAS_ZERO)
            pool.memset(T1[96:128, :], 0.0).then_inc(t1_zero, 1)
            pool.wait_ge(t1_zero, 1)
            pool.memset(cm[64:64 + H, :], 1.0).then_inc(t1_zero, 1)
            pool.wait_ge(t1_zero, 2)
            pool.memset(cm[64:64 + H, :].rearrange("h (c i) -> h c i", i=P)[:, :, 0:1], 0.0).then_inc(t1_zero, 1)
            pool.wait_ge(t1_zero, 3)

            pool.memset(m8, 1.0).then_inc(m8_ready, 1)
            pool.wait_ge(m8_ready, 1)
            pool.affine_select(out=m8, in_=m8, compare_op=ALU.is_equal, fill=0.0, base=0, pattern=[[1, NB], [-1, NB]],
                               channel_multiplier=0).then_inc(m8_ready, 1)
            for n in range(NBLK):
                pool.wait_ge(w_hi_ready, n + 1)
                if n >= 2:
                    pool.wait_ge(block_done, n - 1)
                pool.tensor_tensor(w_lo[:, n % 2, :, :], w_raw[:, n % 2, :, :],
                                   w_hi[:, n % 2, :, :].bitcast(F32), ALU.subtract).then_inc(w_lo_ready, 1)
                if n == 2:
                    step = 0
                    for l in range(LEVELS):
                        b, v = 1 << l, -1.0 if l == 0 else 1.0
                        m = lm[:, l, :].rearrange("p (j u w) -> p j u w", u=2, w=b)
                        pool.memset(m[:, :, 0, :], v)
                        pool.memset(m[:, :, 1, :], 0.0).then_inc(masks, 1)
                        m = lm[:, l, :].rearrange("p (j w) -> p j w", w=2 * b)
                        for base, k in ((-b, 1), (2 * b - 1, -1)):
                            step += 1
                            pool.wait_ge(masks, step)
                            pool.affine_select(out=m, in_=m, compare_op=ALU.is_ge, fill=0.0, base=base,
                                               pattern=[[-2 * b * k, P // (2 * b)], [0, 2 * b]],
                                               channel_multiplier=k).then_inc(masks, 1)
                        step += 1
                    m = lm[:, LEVELS, :].rearrange("p (j u) -> p j u", u=2)
                    pool.memset(m[:, :, 0:1], 0.0)
                    pool.memset(m[:, :, 1:2], -1.0).then_inc(masks, 1)
                    pool.wait_ge(masks, step + 1)
                    pool.affine_select(out=m, in_=m, compare_op=ALU.is_equal, fill=0.0, base=0,
                                       pattern=[[-2, P // 2], [0, 2]], channel_multiplier=1).then_inc(masks, 1)

            xs = [0]

            def xlink(ins):
                xs[0] += 1
                ins.then_inc(x_step, 1)
                pool.wait_ge(x_step, xs[0])

            def multiply_pages(first, end):
                for n in range(first, end):
                    k = kpages[:, n % NR, :]
                    if n == 0:
                        pool.wait_ge(qb_in, 16)
                    pool.wait_ge(kpage_in[n % NR], 16 * (n // NR + 1))
                    pool.tensor_tensor(k, k, qb[:, n // NPG, :], ALU.mult).then_inc(k_made, 1)

            def gate_outputs(c):
                pool.wait_ge(og_ready, c + 1)
                pool.wait_ge(z_in[c % 2], 16 * (c // 2 + 1))
                pool.tensor_tensor(OO[c % 2][:, :, :], OO[c % 2][:, :, :], ZZ[c % 2][:, :, :], ALU.mult).then_inc(m_ready, 1)

            for c0 in range(0, NT, 2):
                for c in (c0, c0 + 1):
                    s = c % 2
                    pool.wait_ge(l_ready, c + 1)
                    if c >= 2:
                        pool.wait_ge(u_ready, c - 1)
                    xlink(pool.tensor_tensor(XX[s][:, :, :], LL[s][:, :, :], over_heads(lm[:, 0, :]), ALU.mult))
                    pool.tensor_tensor(XX[s][:, :, :], XX[s][:, :, :], over_heads(ident[:, :]), ALU.add).then_inc(x0_ready, 1)
                for c in (c0, c0 + 1):
                    s = c % 2
                    pool.wait_ge(eg_ready, c + 1)
                    pool.tensor_tensor(QG[s][:, :, :], QG[s][:, :, :], cT[:, 0:H, chunk(c)], ALU.mult).then_inc(qg_ready, 1)
                multiply_pages(8 * c0, 8 * c0 + 8)
                if c0:
                    gate_outputs(c0 - 2)
                    gate_outputs(c0 - 1)
                multiply_pages(8 * c0 + 8, 8 * c0 + 16)
                for c in (c0, c0 + 1):
                    s = c % 2
                    if c >= 1:
                        pool.wait_ge(s_ready, c)
                        pool.tensor_tensor(SG[:, :, :], ST[:, :, :], per_head(sm(s, EL)), ALU.mult).then_inc(sg_ready, 1)
            gate_outputs(NT - 2)
            gate_outputs(NT - 1)

            pool.wait_ge(act_once, A_READY)
            pool.tensor_tensor(a_diag, ident[0:NB, 0:NB].unsqueeze(2).to_broadcast([NB, NB, H]),
                               a_row.unsqueeze(1).to_broadcast([NB, NB, H]), ALU.mult).then_inc(pool_once, 1)
            for half in range(2):
                if half:
                    pool.wait_ge(pe_once, PRED_READY)
                for h in range(H):
                    src = cT[:, H * (1 - half) + h, SEQ:TOK]
                    pool.tensor_tensor(msk[:, h, :, :], src.unsqueeze(2).to_broadcast([P, NB, NB]), m8, ALU.mult)\
                        .then_inc(msk_ready, 1)

            pool.wait_ge(dve_once, PD_READY)
            for n in range(NB * NPG):
                b, j = n // NPG, n % NPG
                if j == 0:
                    pool.wait_ge(vpage_in[b % 2], 16 * NPG * (b // 2 + 1))
                pool.tensor_tensor(vpage(n).rearrange("p (h d) -> p h d", h=H), vpage(n).rearrange("p (h d) -> p h d", h=H),
                                   per_head(pp[:, b, :, j]), ALU.mult).then_inc(pv_made, 1)

        @block.scalar
        def _(act):
            achain = [0]

            def alink(ins):
                achain[0] += 1
                ins.then_inc(act_step, 1)
                act.wait_ge(act_step, achain[0])

            def split_w(n):
                act.wait_ge(w_in_sem[n % 2], raw_count(n))
                if n >= 2:
                    act.wait_ge(block_done, n - 1)
                act.activation(w_hi[:, n % 2, :, :], w_raw[:, n % 2, :, :], ACT.Copy).then_inc(w_hi_ready, 1)

            for t in range(NT + 2):
                if t == 4:
                    split_w(0)
                if t <= NT:
                    r = rows_of(t)
                    act.wait_ge(x_in[t % 3], 16 * (t // 3 + 1))
                    alink(act.activation(junk[0:r, :], x_t[0:r, t % 3, :], ACT.Square, accum_out=stat[0:r, t:t + 1]))
                    act.wait_ge(pool_once, EPS_READY)
                    act.activation(stat[0:r, 16 + t:17 + t], stat[0:r, t:t + 1], ACT.Sqrt, scale=1.0 / D,
                                   bias=stat[0:r, 42:43]).then_inc(std_ready, 1)
                if t >= 1:
                    u, r = t - 1, rows_of(t - 1)
                    act.wait_ge(xt_ready, u + 1)
                    b = 6 * (u % 2)
                    act.activation(act_hi[:, :, u * P:u * P + r],
                                   PS[:, b:b + 2, :].rearrange("p b (k c) -> p (b k) c", c=P)[:, :, 0:r],
                                   ACT.Copy).then_inc(act_hi_ready, 1)

            for n in range(NBLK + 1):
                if n + 1 < NBLK:
                    split_w(n + 1)
                if CV0 <= n - 1 < NAT0:
                    c = n - 1 - CV0
                    act.wait_ge(conv_ready, c + 1)
                    act.activation(cT[:, c, :], acc[:, :], ACT.Silu).then_inc(silu_done, 1)
                if n == 11:
                    act.wait_ge(dve_once, GATE_ABS)
                    act.activation(ge[0:96, :], ge[0:96, :], ACT.Exp, scale=-1.0).then_inc(gate_act, 1)
                    act.wait_ge(gate_act, 1)
                    act.activation(gs[0:96, :], ge[0:96, :], ACT.Ln, bias=ones[0:96, 0:1]).then_inc(gate_act, 1)
                    act.wait_ge(dve_once, GATE_MIN)
                    act.activation(T1[32:64, :], T1[32:64, :], ACT.Exp).then_inc(gate_act, 1)
                    act.activation(stat[64:68, 52:53], stat[64:68, 51:52], ACT.Exp).then_inc(gate_act, 1)
                b = n - NS0
                if -1 <= b < 7:
                    if b == -1:
                        act.wait_ge(dve_once, T1_READY)
                    if b >= 1:
                        act.wait_ge(ss_ready, b)
                    act.activation(sq[:, (b + 1) % 2, :], cT[:, b + 1, 0:SEQ], ACT.Square).then_inc(sq_ready, 1)
                if 0 <= b < 8:
                    act.wait_ge(ss_ready, b + 1)
                    if b >= 2:
                        act.wait_ge(normed, b - 1)
                    act.activation(rn[:, b % 2, :], PS[:, 6:8, :].rearrange("p b n -> p (b n)"),
                                   ACT.Sqrt, bias=stat[:, 42:43]).then_inc(sd_ready, 1)
                if n == 26:
                    act.activation(ssq.rearrange("p (c b) -> p c b", b=NB), cT[:, 0:8, SEQ:TOK], ACT.Square).then_inc(sq_ready, 1)
                if n == 27:
                    act.wait_ge(ss_ready, 9)
                    act.activation(srn, PS[:, 7, 64:128], ACT.Sqrt, bias=stat[:, 42:43]).then_inc(sd_ready, 1)
                if n == NBLK:
                    break
                act.wait_ge(block_done, n + 1)
                b, m, scale = 3 * ((n + 1) % 2), cb_use(n), 1.0
                src = PS[:, b:b + 3, 0:G3]
                if n == GATE:
                    dst, src = gateT[0:96, :], PS[0:96, b:b + 3, 0:G3]
                elif m is not None:
                    if m == 0:
                        act.wait_ge(pool_once, PAD_ZERO)
                    if m >= 2:
                        act.wait_ge(cb_free, m - 1)
                    dst = cb[:, m % 2, 3:3 + TOK]
                elif n < 17:
                    dst = kT[:, n - NAT0, :]
                else:
                    if n == Q0:
                        act.wait_ge(normed, 8)
                    dst, scale = qT[:, n - Q0, :], SCALE
                func = ACT.Silu if NAT0 + 8 <= n < Q0 else ACT.Copy
                act.activation(dst.rearrange("p (g c) -> p g c", g=3), src, func, scale=scale).then_inc(evacuated, 1)

            act.wait_ge(sn_out, 32)
            act.wait_ge(q_out, 16)
            act.wait_ge(gn_ready, 6)
            act.activation(E_N, gN[:, 0:NT, 64:68], ACT.Exp).then_inc(act_once, 1)
            def sum_pages(first, end):
                for n in range(first, end):
                    act.wait_ge(k_made, n + 1)
                    for h in range(H):
                        k = kpages[:, n % NR, h * P:(h + 1) * P]
                        last = act.activation(k, k, ACT.Copy, accum_out=s9[:, n // NPG, h, n % NPG:n % NPG + 1])
                    last.then_inc(k_used, 1)

            def norm_outputs(c0):
                for c in (c0, c0 + 1):
                    s = c % 2
                    act.wait_ge(oo_ready, c + 1)
                    for h in range(H):
                        last = act.activation(heads(4 * s + 3)[:, h, :], OO[s][:, h, :], ACT.Square, accum_out=sm(s, OSS)[:, h:h + 1])
                    alink(last)
                for c in (c0, c0 + 1):
                    last = act.activation(sm(c % 2, OLN), sm(c % 2, OSS), ACT.Ln, scale=1.0 / HD, bias=stat[:, 42:43])
                alink(last)
                for c in (c0, c0 + 1):
                    act.activation(sm(c % 2, ORS), sm(c % 2, OLN), ACT.Exp, scale=-0.5).then_inc(ors_ready, 1)

            def outputs_hi(c0):
                for c in (c0, c0 + 1):
                    act.wait_ge(mt_ready, c + 1)
                    act.activation(act_hi[:, H:2 * H, chunk(c)], heads(4 * (c % 2) + 3), ACT.Copy).then_inc(mhi_ready, 1)

            for c0 in range(0, NT, 2):
                for c in (c0, c0 + 1):
                    s, A = c % 2, 4 * (c % 2)
                    act.wait_ge(dif_ready, c + 1)
                    act.activation(DEC[s][:, :, :], DEC[s][:, :, :], ACT.Exp, scale=-1.0).then_inc(dexp_ready, 1)
                for c in (c0, c0 + 1):
                    s, A = c % 2, 4 * (c % 2)
                    if c >= 2:
                        act.wait_ge(o_ready, c - 1)
                        act.wait_ge(s_ready, c - 1)
                    act.activation(QG[s][:, :, :], heads(A), ACT.Exp)
                    act.activation(sm(s, EL), heads(A)[:, :, P - 1], ACT.Exp)
                    act.activation(sm(s, KGS), sm(s, GLC), ACT.Exp).then_inc(eg_ready, 1)
                for c in (c0, c0 + 1):
                    s, A = c % 2, 4 * (c % 2)
                    act.wait_ge(lt_t, c + 1)
                    act.activation(LT[s][:, :, :], heads(A + 1), ACT.Copy).then_inc(lt_ready, 1)
                    act.activation(QKT[s][:, :, :], heads(A + 2), ACT.Copy).then_inc(qkt_ready, 1)
                if c0:
                    act.wait_ge(rk_ready, c0 + 2)
                    norm_outputs(c0 - 2)
                sum_pages(8 * c0, 8 * c0 + 8)
                if c0:
                    outputs_hi(c0 - 2)
                sum_pages(8 * c0 + 8, 8 * c0 + 16)
                for c in (c0, c0 + 1):
                    s, A = c % 2, 4 * (c % 2)
                    act.wait_ge(wt_t, c + 1)
                    act.activation(WT[s][:, :, :], heads(A + 1), ACT.Copy, scale=-1.0).then_inc(wt_ready, 1)
            act.wait_ge(s_ready, NT)
            norm_outputs(NT - 2)
            act.wait_ge(sh_ready, 2)
            act.activation(pp[:, :, :, :], pp[:, :, :, :], ACT.Exp).then_inc(e_ready, 1)
            act.activation(self_e, self_e, ACT.Exp).then_inc(e_ready, 1)
            outputs_hi(NT - 2)

            act.activation(a_row, gN[0:NB, NT, 64:68], ACT.Exp).then_inc(act_once, 1)
            act.wait_ge(pe_once, A_SPREAD)
            act.activation(a_all, PS[:, 4, 0:32], ACT.Copy).then_inc(act_once, 1)
            act.wait_ge(pe_once, SO_READY)
            for h in range(H):
                alink(act.activation(dmk[:, 0, 0, :], PS[0:NB, 4, h * P:(h + 1) * P], ACT.Square, accum_out=s_oss[:, h:h + 1]))
            alink(act.activation(s_oln, s_oss, ACT.Ln, scale=1.0 / HD, bias=stat[0:NB, 42:43]))
            act.activation(s_ors, s_oln, ACT.Exp, scale=-0.5).then_inc(act_once, 1)

            def wo_part_hi(k):
                act.wait_ge(raw_in[k % 4], 16 * (k // 4 + 1))
                if k == 0:
                    act.wait_ge(qk_ready, NAI)
                    act.wait_ge(v_used, NB * NPG)
                if k == 5:
                    act.wait_ge(dv_t, NT - 1)
                act.activation(wo_hi[:, k, :], raw_o[:, k % 4, :], ACT.Copy).then_inc(wo_hi_ready, 1)

            for n in range(NAI + 4):
                if n == 1:
                    act.wait_ge(pe_once, SMT_READY)
                    act.activation(act_hi[:, H:2 * H, SEQ:TOK], PS[:, 5, 0:H * NB].rearrange("p (h b) -> p h b", h=H), ACT.Copy)\
                       .then_inc(act_once, 1)
                if n < NAI:
                    i, h, w = n // H, n % H, P * (n // H + 1)
                    act.wait_ge(max_ready, n + 1)
                    if n >= 2:
                        act.wait_ge(pt_t, n - 1)
                    scores = PS[:, 2 * (n % 2):2 * (n % 2) + 2, :].rearrange("p b n -> p (b n)")
                    act.activation(sc[:, n % 2, 0:w], scores[:, 0:w], ACT.Exp, bias=arow[:, 0, n:n + 1],
                                   accum_out=arow[:, 1, n:n + 1]).then_inc(p_ready, 1)
                m = n - 1
                if 0 <= m < NAI:
                    w = P * (m // H + 1)
                    act.wait_ge(pt_t, m + 1)
                    if m >= 2:
                        act.wait_ge(pv_ready, m - 1)
                    act.activation(pT[:, m % 2, :, :].rearrange("p k q -> p (k q)")[:, 0:w],
                                   PS[:, 4:6, :].rearrange("p b n -> p (b n)")[:, 0:w], ACT.Copy).then_inc(pt_ready, 1)
                if n == NAI + 3:
                    for k in range(4):
                        wo_part_hi(k)
                if n >= H + 3 and (n - 3) % H == 0:
                    i = (n - 3) // H - 1
                    act.wait_ge(ot_ready, i + 1)
                    act.activation(act_hi[:, 0:H, chunk(i)], heads(6 + i % 2), ACT.Copy).then_inc(othi_ready, 1)
            act.wait_ge(pe_once, DVT_READY)
            act.activation(act_hi[:, 0:H, SEQ:TOK], PS[:, 4, 0:H * NB].rearrange("p (h b) -> p h b", h=H), ACT.Copy).then_inc(act_once, 1)

            RW = 32
            for k in range(4, KT):
                wo_part_hi(k)
            for t in range(NT9 + 1):
                if t < NT9:
                    r = rows_of(t)
                    act.wait_ge(h_ready, t + 1)
                    if t >= 2:
                        act.wait_ge(xmt_ready, t - 1)
                    alink(act.activation(xm[0:r, t % 2, :], y[0:r, t, :], ACT.Square, accum_out=stat[0:r, t:t + 1]))
                    act.activation(stat[0:r, 16 + t:17 + t], stat[0:r, t:t + 1], ACT.Sqrt, scale=1.0 / D,
                                   bias=stat[0:r, 42:43]).then_inc(std2_ready, 1)
                if t == NT9:
                    act.wait_ge(h_t, NT9)
                    for q in range(2):
                        act.wait_ge(raw_in[q], RW + 16)
                        act.activation(wu_hi[:, q, :, :], raw[:, q, :].rearrange("p (kt c) -> p kt c", c=P), ACT.Copy).then_inc(hi_done, 1)
                if t >= 1:
                    u, r = t - 1, rows_of(t - 1)
                    b = 4 + 2 * (u % 2)
                    act.wait_ge(xmt_ready, u + 1)
                    act.activation(act_hi[:, :, u * P:u * P + r],
                                   PS[:, b:b + 2, :].rearrange("p b (k c) -> p (b k) c", c=P)[:, :, 0:r], ACT.Copy).then_inc(a2hi_ready, 1)

            def act_group(g, last):
                for k in range(GB):
                    b = 3 * (k % 2)
                    act.wait_ge(up_done, GB * g + k + 3)
                    act.wait_ge(u_lo_done, GB * g + k + 1)
                    act.activation(r_sq[:, :].rearrange("p (g c) -> p g c", g=3), PS[:, b:b + 3, 0:G3], ACT.Relu).then_inc(relu_done, 1)
                    slot = (2 * k + 2) % 4
                    act.wait_ge(raw_in[slot], RW + 16 * ((2 * k + 2) // 4 + 1) + 32 * g)
                    act.wait_ge(dn_tile, NT9 * g + 1)
                    act.activation(wd_hi[:, k, :], raw[:, slot, :], ACT.Copy).then_inc(hi_done, 1)
                    act.wait_ge(sq_done, GB * g + k + 1)
                    act.activation(u_hi[:, k, :], r_sq[:, :], ACT.Copy).then_inc(u_hi_done, 1)
                    if not (last and k >= 2):
                        slot = (2 * k + 3) % 4
                        act.wait_ge(raw_in[slot], RW + 16 * ((2 * k + 3) // 4 + 1) + 32 * g)
                        act.activation(wu_hi[:, k % 2, :, :], raw[:, slot, :].rearrange("p (kt c) -> p kt c", c=P), ACT.Copy)\
                           .then_inc(hi_done, 1)

            with act.Fori(0, NG - 1) as g:
                act_group(g, False)
            act_group(NG - 1, True)
            for t in range(NT9):
                r = rows_of(t)
                act.wait_ge(y_add, NT9 * (NG - 1) + t + 3)
                alink(act.activation(junk2[0:r, :], y[0:r, t, :], ACT.Square, accum_out=stat[0:r, t:t + 1]))
                act.activation(stat[0:r, 16 + t:17 + t], stat[0:r, t:t + 1], ACT.Sqrt, scale=1.0 / D,
                               bias=stat[0:r, 42:43]).then_inc(std3_ready, 1)

        @block.vector
        def _(dve):
            chain = [0]

            def link(ins):
                chain[0] += 1
                ins.then_inc(dve_step, 1)
                dve.wait_ge(dve_step, chain[0])

            dve.wait_ge(ln_in, 16)
            for t in range(NT + 2):
                if t <= NT:
                    r = rows_of(t)
                    dve.wait_ge(std_ready, t + 1)
                    link(dve.reciprocal(stat[0:r, 28 + t:29 + t], stat[0:r, 16 + t:17 + t]))
                    if t >= 2:
                        dve.wait_ge(xt_ready, t - 1)
                    dve.scalar_tensor_tensor(xn[0:r, t % 2, :], x_t[0:r, t % 3, :], stat[0:r, 28 + t:29 + t],
                                             lnb[0:r, :], ALU.mult, ALU.mult).then_inc(xn_ready, 1)
                if t >= 1:
                    u, r = t - 1, rows_of(t - 1)
                    dve.wait_ge(act_hi_ready, u + 1)
                    b, cs = 6 * (u % 2), slice(u * P, u * P + r)
                    dve.tensor_tensor(act_lo[:, :, cs],
                                      PS[:, b:b + 2, :].rearrange("p b (k c) -> p (b k) c", c=P)[:, :, 0:r],
                                      act_hi[:, :, cs].bitcast(F32), ALU.subtract).then_inc(act_lo_ready, 1)
            dve.wait_ge(pe_once, HW_T)
            link(dve.tensor_copy(hw[:, :, :], PS[:, 6, 0:12 * 28].rearrange("p (c i) -> p c i", c=12)))
            for n in range(CV0, NBLK + 1):
                if n < NAT0:
                    c = n - CV0
                    s = cb[:, c % 2, :]
                    hist = hw[:, c, 0:24].rearrange("p (b i) -> p b i", i=3)
                    dve.wait_ge(evacuated, n + 1)
                    if c >= 1:
                        dve.wait_ge(silu_done, c)
                    dve.tensor_copy(tail[:, c, :], s[:, SEQ:SEQ + 11])
                    dve.tensor_scalar(acc[:, SEQ:TOK], hist[:, :, 0], hw[:, c, 24:25], None, ALU.mult)
                    link(dve.tensor_scalar(acc[:, 0:SEQ], s[:, 0:SEQ], hw[:, c, 24:25], None, ALU.mult))
                    for i in (1, 2):
                        dve.scalar_tensor_tensor(acc[:, SEQ:TOK], hist[:, :, i], hw[:, c, 24 + i:25 + i],
                                                 acc[:, SEQ:TOK], ALU.mult, ALU.add)
                        link(dve.scalar_tensor_tensor(acc[:, 0:SEQ], s[:, i:SEQ + i], hw[:, c, 24 + i:25 + i],
                                                      acc[:, 0:SEQ], ALU.mult, ALU.add))
                    dve.scalar_tensor_tensor(acc[:, :], s[:, 3:3 + TOK], hw[:, c, 27:28], acc[:, :],
                                             ALU.mult, ALU.add).then_inc(conv_ready, 1)
                    dve.wait_ge(conv_ready, c + 1)
                    dve.tensor_copy(stat[:, 40:41], s[:, 0:1]).then_inc(cb_free, 1)
                if n == 9:
                    dve.wait_ge(evacuated, 1)
                    dve.wait_ge(bias_in, 48)
                    dve.wait_ge(t1_zero, 3)
                    link(dve.tensor_scalar(gateT[0:96, :], gateT[0:96, :], stat[0:96, 50:51], None, ALU.add))
                    dve.scalar_tensor_tensor(ge[0:96, :], gateT[0:96, :], -1.0, gateT[0:96, :], ALU.mult, ALU.max).then_inc(dve_once, 1)
                    dve.wait_ge(dve_once, GATE_ABS)
                    dve.tensor_scalar(T1[32:64, :], T1[32:64, :], 0.0, None, ALU.min).then_inc(dve_once, 1)
                if n == NAT0:
                    dve.wait_ge(gate_act, 4)
                    dve.scalar_tensor_tensor(T1[0:32, :], gateT[0:32, :], 0.0, gs[0:32, :], ALU.min, ALU.subtract)
                    link(dve.tensor_scalar(ge[32:64, :], ge[32:64, :], 1.0, None, ALU.add))
                    link(dve.reciprocal(ge[32:64, :], ge[32:64, :]))
                    dve.tensor_tensor(T1[32:64, :], T1[32:64, :], ge[32:64, :], ALU.mult)
                    link(dve.scalar_tensor_tensor(ge[64:96, :], gateT[64:96, :], 0.0, gs[64:96, :], ALU.max, ALU.add))
                    link(dve.tensor_scalar(ge[64:68, :], ge[64:68, :], stat[64:68, 52:53], -1.0, ALU.mult, ALU.mult))
                    dve.tensor_copy(T1[64:68, SEQ:TOK], ge[64:68, SEQ:TOK])
                    dve.tensor_tensor_scan(T1[64:68, 0:SEQ], cm[64:68, :], ge[64:68, 0:SEQ], 0.0, ALU.mult, ALU.add)
                    dve.tensor_tensor_scan(T1[96:100, 0:SEQ], ones[0:4, 0:1].to_broadcast([4, SEQ]), T1[0:4, 0:SEQ], 0.0,
                                           ALU.mult, ALU.add).then_inc(dve_once, 1)
                b = n - NS0
                if 0 <= b < 8:
                    dve.wait_ge(sd_ready, b + 1)
                    link(dve.reciprocal(rn[:, b % 2, :], rn[:, b % 2, :]))
                    dve.scalar_tensor_tensor(cT[:, b, 0:SEQ], cT[:, b, 0:SEQ], SCALE if b < 4 else 1.0, rn[:, b % 2, :],
                                             ALU.mult, ALU.mult).then_inc(normed, 1)
                i = n - 1 - NAT0
                if 0 <= i < 12:
                    dve.wait_ge(nat_t, i + 1)
                    if i >= 2:
                        dve.wait_ge(nat_out[i % 2], 16 * (i // 2))
                    if i >= 4:
                        m = cb_use(NAT0 + i)
                        dve.tensor_copy(vzS[:, i - 4, :], cb[:, m % 2, 3 + SEQ:3 + TOK]).then_inc(cb_free, 1)
                    dve.tensor_copy(nat[:, i % 2, :, :], PS[:, 6:8, :].rearrange("p b (k c) -> p (b k) c", c=P))\
                       .then_inc(nat_ready, 1)
                if n == 26:
                    dve.wait_ge(pe_once, GN_T)
                    for t0, count, r, off in ((0, 5, P, 6), (5, 3, P, 7), (8, 1, NB, 7)):
                        src = PS[0:r, off, 0:500].rearrange("p (t c) -> p t c", c=100)
                        k = 3 if t0 == 8 else 0
                        dve.tensor_copy(gN[0:r, t0:t0 + count, 0:68], src[:, k:k + count, 0:68]).then_inc(gn_ready, 1)
                        dve.tensor_copy(gN[0:r, t0:t0 + count, 68:72], src[:, k:k + count, 96:100]).then_inc(gn_ready, 1)
                if n == 27:
                    eye8 = ident[0:NB, 0:NB].unsqueeze(2).to_broadcast([NB, NB, H])
                    dve.wait_ge(gn_ready, 6)
                    dve.tensor_tensor(lf_diag, eye8, gN[0:NB, NT, 0:H].unsqueeze(1).to_broadcast([NB, NB, H]), ALU.mult)\
                       .then_inc(diag_ready, 1)
                    dve.wait_ge(pe_once, CLF_T)
                    dve.tensor_copy(clf[:, :, :, :].rearrange("p b j h -> p (b j) h"),
                                    PS[:, 6, 0:256].rearrange("p (h n) -> p n h", h=H)).then_inc(dve_once, 1)
                if n == 28:
                    dve.wait_ge(sd_ready, 9)
                    link(dve.reciprocal(srn, srn))
                    for half in range(2):
                        cs = cT[:, 4 * half:4 * half + 4, SEQ:TOK]
                        last = dve.scalar_tensor_tensor(cs, cs, 1.0 if half else SCALE,
                                                        srn[:, 32 * half:32 * half + 32].rearrange("p (c b) -> p c b", b=NB),
                                                        ALU.mult, ALU.mult)
                    last.then_inc(normed, 1)
                    dve.wait_ge(pe_once, BIAS_T)
                    dve.wait_ge(block_done, NBLK)
                    suf = PS[:, 6, 0:256].rearrange("p (b j h) -> p b j h", j=NPG, h=H)
                    tot = PS[:, 6, 256:512].rearrange("p (b j h) -> p b j h", j=NPG, h=H)
                    link(dve.tensor_copy(run_, PS[:, 7, 0:32].rearrange("p (b h) -> p b h", h=H)))
                    for j in range(NPG - 1, -1, -1):
                        dve.tensor_tensor(sfx[:, :, j, :], suf[:, :, j, :], run_, ALU.add).then_inc(pre_read, 1)
                        dve.wait_ge(pre_read, NPG - j)
                        if j:
                            link(dve.tensor_tensor(run_, run_, tot[:, :, j, :], ALU.add))

            dve.wait_ge(pe_once, CT_T)
            dve.tensor_copy(ct[:, :, :], PS[0:11, 0:3, :].rearrange("p b (k c) -> p (b k) c", c=P)).then_inc(dve_once, 1)
            dve.wait_ge(pe_once, SN_T)
            dve.tensor_copy(sN[:, :, :], PS[0:NB, 0:3, :].rearrange("p b (k c) -> p (b k) c", c=P)).then_inc(dve_once, 1)
            dve.wait_ge(dve_once, SN_READY)
            for h in range(H):
                last = dve.tensor_tensor_reduce(prod[:, :], sN[:, h, :], sN[:, H + h, :], 1.0, 0.0, ALU.mult, ALU.add,
                                                self_s[:, h:h + 1])
                link(last)
            dve.tensor_tensor(self_diag, eye8, self_s.unsqueeze(1).to_broadcast([NB, NB, H]), ALU.mult).then_inc(diag_ready, 1)

            dve.wait_ge(act_once, EN_READY)
            dve.tensor_tensor(B_EK, E_N, gN[:, 0:NT, 32:36], ALU.mult).then_inc(dve_once, 1)
            dve.wait_ge(wgn_in, 16)
            dve.wait_ge(masks, NMASK)
            link(dve.tensor_scalar(above[:, :], incl[:, :], NEG, -NEG, ALU.mult, ALU.add))

            def scale_outputs(c0):
                for c in (c0, c0 + 1):
                    s = c % 2
                    dve.wait_ge(ors_ready, c + 1)
                    for h in range(H):
                        last = dve.scalar_tensor_tensor(OO[s][:, h, :], OO[s][:, h, :], sm(s, ORS)[:, h:h + 1], wgn[:, :],
                                                        ALU.mult, ALU.mult)
                    last.then_inc(og_ready, 1)

            def outputs_lo(c0):
                for c in (c0, c0 + 1):
                    dve.wait_ge(mhi_ready, c + 1)
                    dve.tensor_tensor(act_lo[:, H:2 * H, chunk(c)], heads(4 * (c % 2) + 3), act_hi[:, H:2 * H, chunk(c)].bitcast(F32),
                                      ALU.subtract).then_inc(mlo_ready, 1)

            for c0 in range(0, NT, 2):
                for c in (c0, c0 + 1):
                    s, A = c % 2, 4 * (c % 2)
                    dve.wait_ge(gb_ready, c + 1)
                    dve.tensor_tensor(sm(s, GLC), heads(A)[:, :, P - 1], gN[:, c, 64:68], ALU.subtract)
                    for h in range(H):
                        last = dve.scalar_tensor_tensor(DEC[s][:, h, :], heads(A)[:, h, :], gN[:, c, 64 + h:65 + h], above[:, :],
                                                        ALU.subtract, ALU.max)
                    last.then_inc(dif_ready, 1)
                for c in (c0, c0 + 1):
                    s, A = c % 2, 4 * (c % 2)
                    dve.wait_ge(dexp_ready, c + 1)
                    dve.wait_ge(kk_ready, c + 1)
                    for h in range(H):
                        last = dve.scalar_tensor_tensor(LL[s][:, h, :], heads(A + 1)[:, h, :], gN[:, c, 32 + h:33 + h], DEC[s][:, h, :],
                                                        ALU.mult, ALU.mult)
                    last.then_inc(l_ready, 1)
                    if c < 2:
                        dve.wait_ge(ct_out, 32)
                    dve.tensor_tensor(QKD[s][:, :, :], heads(A + 2), DEC[s][:, :, :], ALU.mult).then_inc(qkd_ready, 1)
                for l in range(1, LEVELS):
                    for c in (c0, c0 + 1):
                        s, A = c % 2, 4 * (c % 2)
                        if l == 1:
                            dve.wait_ge(lt_ready, c + 1)
                            link(dve.tensor_tensor(XT[s][:, :, :], LT[s][:, :, :], over_heads(lm[:, LEVELS, :]), ALU.mult))
                            dve.tensor_tensor(XT[s][:, :, :], XT[s][:, :, :], over_heads(ident[:, :]), ALU.add).then_inc(xt0_ready, 1)
                        dve.wait_ge(y_ready, level_seq(c, l))
                        dve.tensor_tensor(LL[s][:, :, :], heads(A), over_heads(lm[:, l, :]), ALU.mult).then_inc(ym_ready, 1)
                    if l == 2:
                        for c in (c0, c0 + 1):
                            s, A = c % 2, 4 * (c % 2)
                            dve.wait_ge(kn_ready, c + 1)
                            dve.wait_ge(eg_ready, c + 1)
                            if c == 0:
                                dve.wait_ge(dve_once, BEK_READY)
                            dve.tensor_tensor(RK[s][:, :, :], heads(A + 3), per_head(B_EK[:, c, :]), ALU.mult)
                            dve.tensor_tensor(KG[s][:, :, :], heads(A + 3), per_head(sm(s, KGS)), ALU.mult).then_inc(rk_ready, 1)
                    for c in (c0, c0 + 1):
                        s, A = c % 2, 4 * (c % 2)
                        dve.wait_ge(z_ready, level_seq(c, l))
                        if l < LEVELS - 1:
                            dve.tensor_tensor(XX[s][:, :, :], XX[s][:, :, :], heads(A + 1), ALU.subtract)
                        dve.tensor_tensor(XT[s][:, :, :], XT[s][:, :, :], heads(A + 2), ALU.subtract).then_inc(x_ready, 1)
                    if l == 1:
                        for c in (c0, c0 + 1):
                            s, A = c % 2, 4 * (c % 2)
                            dve.wait_ge(lt_t, c + 1)
                            dve.tensor_tensor(BV[s][:, :, :], heads(A + 3), per_head(gN[:, c, 32:36]), ALU.mult).then_inc(bv_ready, 1)
                    if c0 and l == 3:
                        scale_outputs(c0 - 2)
                    if c0 and l == 5:
                        outputs_lo(c0 - 2)
                for c in (c0, c0 + 1):
                    s, A = c % 2, 4 * (c % 2)
                    dve.wait_ge(u_ready, c + 1)
                    dve.tensor_copy(VN[s][:, :, :], heads(A)).then_inc(vn_ready, 1)
                    dve.wait_ge(s_add, c + 1)
                    if c == 0:
                        dve.tensor_copy(ST[:, :, :], heads(A + 3)).then_inc(s_ready, 1)
                    else:
                        dve.wait_ge(sg_ready, c)
                        dve.tensor_tensor(ST[:, :, :], SG[:, :, :], heads(A + 3), ALU.add).then_inc(s_ready, 1)
                    if c >= 2:
                        dve.wait_ge(mt_ready, c - 1)
                    dve.wait_ge(o_ready, c + 1)
                    dve.tensor_copy(OO[s][:, :, :], heads(A + 2)).then_inc(oo_ready, 1)
            dve.wait_ge(k_used, NB * NPG)
            dve.wait_ge(s_add, NT)
            for b in range(NB):
                last = dve.tensor_tensor(pp[:, b, :, :], s9[:, b, :, :], sfx[:, b, :, :].rearrange("p j h -> p h j"), ALU.add)
            link(last)
            pv_ = pp[:, :, :, :].rearrange("p b h j -> p (b h) j")
            link(dve.tensor_reduce(mx, pv_, AX.X, ALU.max))
            dve.wait_ge(pe_once, SELF_T)
            link(dve.tensor_copy(self_sc, PS[:, 5, 64:96]))
            dve.tensor_tensor(mx, mx, self_sc, ALU.max).then_inc(dve_once, 1)
            dve.wait_ge(pe_once, MX_T)
            link(dve.tensor_reduce(mcol, PS[0:32, 4, 0:P], AX.X, ALU.max))
            dve.tensor_scalar(mdiag, ident[0:32, 0:32], mcol, None, ALU.mult).then_inc(dve_once, 1)
            dve.wait_ge(pe_once, M_SPREAD)
            link(dve.tensor_copy(m_all, PS[:, 5, 0:32]))
            dve.tensor_tensor(pv_, pv_, m_all.unsqueeze(2).to_broadcast([P, 32, NPG]), ALU.subtract).then_inc(sh_ready, 1)
            dve.tensor_tensor(self_e, self_sc, m_all, ALU.subtract).then_inc(sh_ready, 1)
            scale_outputs(NT - 2)
            dve.wait_ge(e_ready, 2)
            dve.tensor_reduce(sj, pv_, AX.X, ALU.add).then_inc(dve_once, 1)
            dve.wait_ge(pe_once, SUM_SPREAD)
            link(dve.tensor_tensor(inv, PS[:, 5, 32:64], self_e, ALU.add))
            link(dve.reciprocal(inv, inv))
            dve.tensor_tensor(pv_, pv_, inv.unsqueeze(2).to_broadcast([P, 32, NPG]), ALU.mult)
            link(dve.tensor_tensor(self_e, self_e, inv, ALU.mult))
            dve.tensor_tensor(p_diag, self_e[0:NB, :].rearrange("p (b h) -> p h b", h=H),
                              ident[0:NB, 0:NB].unsqueeze(1).to_broadcast([NB, H, NB]), ALU.mult).then_inc(dve_once, 1)
            outputs_lo(NT - 2)

            dve.wait_ge(pe_once, DN_T)
            dve.tensor_copy(dN[:, :, :], PS[0:NB, 0:4, :].rearrange("p b (k c) -> p (b k) c", c=P)).then_inc(dve_once, 1)
            dve.wait_ge(dve_once, DN_READY)
            dve.wait_ge(pe_once, PRED_READY)
            for h in range(H):
                last = dve.scalar_tensor_tensor(dlt[:, h, :], PS[0:NB, 5, h * P:(h + 1) * P], a_row[:, h:h + 1], dN[:, 8 + h, :],
                                                ALU.mult, ALU.subtract)
            link(last)
            for h in range(H):
                last = dve.tensor_scalar(dlt[:, h, :], dlt[:, h, :], gN[0:NB, NT, 32 + h:33 + h], -1.0, ALU.mult, ALU.mult)
            link(last)
            for h in range(H):
                dve.tensor_tensor(dmk[:, h, :, :], dlt[:, h, :].unsqueeze(1).to_broadcast([NB, NB, P]),
                                  ident[0:NB, 0:NB].unsqueeze(2).to_broadcast([NB, NB, P]), ALU.mult).then_inc(dmk_ready, 1)
            dve.wait_ge(act_once, A_ALL_READY)
            dve.wait_ge(st_in, 16)
            for g in range(8):
                h, half = g // 2, g % 2
                dve.wait_ge(outer_ready, g + 1)
                for b in range(4):
                    j = (4 * half + b) * H + h
                    last = dve.scalar_tensor_tensor(S_s[:, j, :], S_s[:, j, :], a_all[:, j:j + 1], PS[:, g % 4, b * P:(b + 1) * P],
                                                    ALU.mult, ALU.add)
                last.then_inc(st_ready, 1)
            dve.wait_ge(msk_ready, 2 * H)
            dve.wait_ge(pe_once, DN_T)
            dve.tensor_scalar(neg[:, :], incl[:, :], -NEG, NEG, ALU.mult, ALU.add)
            dve.tensor_copy(eye[:, :], ident[:, :])
            for h in range(H):
                dve.tensor_scalar(less[96:100, h, :], ident[96:100, 96 + h:97 + h].to_broadcast([4, P]), -1.0, None, ALU.mult)
            link(dve.tensor_copy(D_hi[96:100, :], T1[96:100, 0:SEQ]))
            dve.tensor_tensor(D_lo[96:100, :], T1[96:100, 0:SEQ], D_hi[96:100, :].bitcast(F32), ALU.subtract).then_inc(bias_ready, 1)
            dve.wait_ge(act_once, SORS_READY)
            for h in range(H):
                last = dve.scalar_tensor_tensor(dlt[:, h, :], PS[0:NB, 4, h * P:(h + 1) * P], s_ors[:, h:h + 1], wgn[0:NB, :],
                                                ALU.mult, ALU.mult)
            link(last)
            dve.tensor_tensor(dlt[:, :, :], dlt[:, :, :], dN[:, 12:16, :], ALU.mult).then_inc(dve_once, 1)

            def wo_part_lo(k):
                dve.wait_ge(wo_hi_ready, k + 1)
                dve.tensor_tensor(wo_lo[:, k, :], raw_o[:, k % 4, :], wo_hi[:, k, :].bitcast(F32), ALU.subtract).then_inc(wo_lo_ready, 1)

            for n in range(NAI + 5):
                if n < NAI:
                    i, h, w = n // H, n % H, P * (n // H + 1)
                    dve.wait_ge(qk_ready, n + 1)
                    dve.tensor_reduce(arow[:, 0, n:n + 1], PS[:, 2 * (n % 2):2 * (n % 2) + 2, :].rearrange("p b n -> p (b n)")[:, 0:w],
                                      AX.X, ALU.max, negate=True).then_inc(max_ready, 1)
                if n == 1:
                    dve.wait_ge(act_once, SMHI_READY)
                    dve.tensor_tensor(act_lo[:, H:2 * H, SEQ:TOK], PS[:, 5, 0:H * NB].rearrange("p (h b) -> p h b", h=H),
                                      act_hi[:, H:2 * H, SEQ:TOK].bitcast(F32), ALU.subtract).then_inc(dve_once, 1)
                    dve.wait_ge(pe_once, VS_T)
                    dve.wait_ge(dve_once, PD_READY)
                    link(dve.tensor_reduce(self_p, p_diag, AX.X, ALU.add))
                    for h in range(H):
                        last = dve.tensor_scalar(dv[:, h * P:(h + 1) * P], PS[0:NB, 4, h * P:(h + 1) * P], self_p[:, h:h + 1], None, ALU.mult)
                    last.then_inc(dv_ready, 1)
                if n >= H + 2 and (n - 2) % H == 0:
                    i = (n - 2) // H - 1
                    its = slice(i * H, i * H + H)
                    dve.wait_ge(p_ready, H * i + H)
                    link(dve.reciprocal(arow[:, 2, its], arow[:, 1, its]))
                    dve.wait_ge(pv_ready, H * i + H)
                    if i >= 2:
                        dve.wait_ge(ot_ready, i - 1)
                    dve.tensor_tensor(oN[:, i % 2, :, :], heads(6 + i % 2), per_head(arow[:, 2, its]), ALU.mult).then_inc(on_ready, 1)
                if n == NAI + 3:
                    for k in range(3):
                        wo_part_lo(k)
                if n >= H + 4 and n % H == 0:
                    i = n // H - 2
                    dve.wait_ge(othi_ready, i + 1)
                    dve.tensor_tensor(act_lo[:, 0:H, chunk(i)], heads(6 + i % 2), act_hi[:, 0:H, chunk(i)].bitcast(F32),
                                      ALU.subtract).then_inc(otlo_ready, 1)
                if H <= n < NAI + 2:
                    k = 2 * (n - H) + 2 * max(0, n - NAI)
                    for m in range(k, k + (2 if n < NAI else 4)):
                        b = m // NPG
                        if m % NPG == 0 and b >= 3:
                            dve.wait_ge(dv_t, b - 2)
                        dve.wait_ge(pv_made, m + 1)
                        if m % NPG == 0:
                            dve.tensor_copy(av[b % 3][:, :], vpage(m)).then_inc(v_used, 1)
                        else:
                            dve.wait_ge(v_used, m)
                            dve.tensor_tensor(av[b % 3][:, :], av[b % 3][:, :], vpage(m), ALU.add).then_inc(v_used, 1)
                if n % H == 1 and n > 2 * H:
                    r = n // H - 1
                    dve.wait_ge(dv_t, r)
                    dve.wait_ge(dv_ready, r)
                    dve.tensor_tensor(dv[:, :], dv[:, :], PS[0:NB, 7 - r % 2, :], ALU.add).then_inc(dv_ready, 1)
            wo_part_lo(3)
            dve.wait_ge(act_once, DOHI_READY)
            dve.tensor_tensor(act_lo[:, 0:H, SEQ:TOK], PS[:, 4, 0:H * NB].rearrange("p (h b) -> p h b", h=H),
                              act_hi[:, 0:H, SEQ:TOK].bitcast(F32), ALU.subtract).then_inc(dve_once, 1)

            for k in range(4, KT):
                wo_part_lo(k)

            def first_up_lo(q):
                dve.wait_ge(hi_done, q + 1)
                dve.tensor_tensor(wu_lo[:, q, :, :], raw[:, q, :].rearrange("p (kt c) -> p kt c", c=P), wu_hi[:, q, :, :].bitcast(F32),
                                  ALU.subtract).then_inc(lo_done, 1)

            for i, (s_, n) in enumerate(((lo_done, 4), (up_done, 2), (relu_done, 2), (u_lo_done, 1), (dn_tile, 1), (y_add, 2))):
                dve.tensor_copy(stat[:, 44 + i:45 + i], stat[:, 42:43]).then_inc(s_, n)
            dve.wait_ge(ln2_in, 16)
            for t in range(NT9 + 1):
                if t < NT9:
                    r, b = rows_of(t), 2 * (t % 2)
                    dve.wait_ge(h_t, t + 1)
                    dve.wait_ge(xr_in[t % 2], 16 * (t // 2 + 1))
                    dve.tensor_tensor(y[0:r, t, :], PS[0:r, b:b + 2, :].rearrange("p b n -> p (b n)"), x_r[0:r, t % 2, :],
                                      ALU.add).then_inc(h_ready, 1)
                    dve.wait_ge(std2_ready, t + 1)
                    link(dve.reciprocal(stat[0:r, 28 + t:29 + t], stat[0:r, 16 + t:17 + t]))
                    dve.scalar_tensor_tensor(xm[0:r, t % 2, :], y[0:r, t, :], stat[0:r, 28 + t:29 + t], ln2b[0:r, :],
                                             ALU.mult, ALU.mult).then_inc(xm_ready, 1)
                if t == NT9:
                    first_up_lo(0)
                if t >= 1:
                    u, r = t - 1, rows_of(t - 1)
                    b, cs = 4 + 2 * (u % 2), slice(u * P, u * P + rows_of(u))
                    dve.wait_ge(a2hi_ready, u + 1)
                    dve.tensor_tensor(act_lo[:, :, cs], PS[:, b:b + 2, :].rearrange("p b (k c) -> p (b k) c", c=P)[:, :, 0:r],
                                      act_hi[:, :, cs].bitcast(F32), ALU.subtract).then_inc(a2lo_ready, 1)
            first_up_lo(1)

            def normed_output(t):
                r = rows_of(t)
                dve.wait_ge(std3_ready, t + 1)
                link(dve.reciprocal(stat[0:r, 28 + t:29 + t], stat[0:r, 16 + t:17 + t]))
                if t >= 4:
                    dve.wait_ge(y_out[t % 4], 16 * (t // 4))
                dve.scalar_tensor_tensor(raw[0:r, t % 4, :], y[0:r, t, :], stat[0:r, 28 + t:29 + t], lnfb[0:r, :],
                                         ALU.mult, ALU.mult).then_inc(out_ready, 1)

            def dve_group(g, last):
                for k in range(GB):
                    dve.wait_ge(relu_done, GB * g + k + 3)
                    dve.tensor_tensor(r_sq[:, :], r_sq[:, :], r_sq[:, :], ALU.mult).then_inc(sq_done, 1)
                    dve.wait_ge(hi_done, 8 * g + 2 * k + 3 - (last and k == 3))
                    dve.tensor_tensor(wd_lo[:, k, :], raw[:, (2 * k + 2) % 4, :], wd_hi[:, k, :].bitcast(F32), ALU.subtract).then_inc(lo_done, 1)
                    dve.wait_ge(u_hi_done, GB * g + k + 1)
                    dve.tensor_tensor(u_lo[:, k, :], r_sq[:, :], u_hi[:, k, :].bitcast(F32), ALU.subtract).then_inc(u_lo_done, 1)
                    if not (last and k >= 2):
                        dve.wait_ge(hi_done, 8 * g + 2 * k + 4)
                        dve.tensor_tensor(wu_lo[:, k % 2, :, :], raw[:, (2 * k + 3) % 4, :].rearrange("p (kt c) -> p kt c", c=P),
                                          wu_hi[:, k % 2, :, :].bitcast(F32), ALU.subtract).then_inc(lo_done, 1)
                if last:
                    dve.wait_ge(lnf_in, 16)
                for t in range(NT9 + last):
                    if last and t:
                        normed_output(t - 1)
                    if t == NT9:
                        break
                    r, b = rows_of(t), 0 if t % 2 else 6
                    dve.wait_ge(dn_tile, NT9 * g + t + 2)
                    dve.tensor_tensor(y[0:r, t, :], y[0:r, t, :], PS[0:r, b:b + 2, :].rearrange("p b n -> p (b n)"), ALU.add).then_inc(y_add, 1)

            with dve.Fori(0, NG - 1) as g:
                dve_group(g, False)
            dve_group(NG - 1, True)

        @block.tensor
        def _(pe):
            pe.wait_ge(consts, 4)

            def gate_group(g):
                pe.wait_ge(act_lo_ready, min(NT + 1, ((g + 1) * G3 + P - 1) // P))
                for half, ready, operands in ((0, w_hi_ready, (act_hi, act_lo)), (1, w_lo_ready, (act_hi,))):
                    pe.wait_ge(ready, 1)
                    w = (w_hi, w_lo)[half]
                    for k in range(KT):
                        for a in operands:
                            last = pe.matmul(PS[0:96, 3 + g, 0:G3], w[:, 0, k, 0:96], a[:, k, g * G3:(g + 1) * G3],
                                             start=(half == 0 and k == 0 and a is act_hi), stop=(half == 1 and k == KT - 1))
                if g == 2:
                    last.then_inc(block_done, 1)

            for t in range(NT + 1):
                r = rows_of(t)
                pe.wait_ge(xn_ready, t + 1)
                if t >= 2:
                    pe.wait_ge(act_lo_ready, t - 1)
                for k in range(KT):
                    last = pe.transpose(PS[:, 6 * (t % 2) + k // 4, (k % 4) * P:(k % 4) * P + r],
                                        xn[0:r, t % 2, k * P:(k + 1) * P], ident[0:r, 0:r])
                last.then_inc(xt_ready, 1)
                if t in (4, 7, 8):
                    gate_group((4, 7, 8).index(t))
            pe.wait_ge(hist_in, 32)
            for c in range(12):
                last = pe.transpose(PS[:, 6, c * 28:(c + 1) * 28], hrows[0:28, c * P:(c + 1) * P], ident[0:28, 0:28])
            last.then_inc(pe_once, 1)
            for n in range(1, NBLK + 1):
                if n < NBLK:
                    if n >= 2:
                        pe.wait_ge(evacuated, n - 1)
                    b = 3 * ((n + 1) % 2)
                    for half, ready, operands in ((0, w_hi_ready, (act_hi, act_lo)), (1, w_lo_ready, (act_hi,))):
                        if half and 0 <= n - NS0 < 8:
                            c = n - NS0
                            pe.wait_ge(sq_ready, c + 1)
                            pe.wait_ge(nat_ready, n - NAT0 - 1)
                            for g in range(2):
                                last = pe.matmul(PS[:, 6 + g, :], ones[:, :], sq[:, c % 2, g * 512:(g + 1) * 512],
                                                 start=True, stop=True)
                            last.then_inc(ss_ready, 1)
                        if half and n == 26:
                            pe.wait_ge(dve_once, T1_READY)
                            pe.wait_ge(nat_ready, 12)
                            for t in range(NT + 1):
                                r, bank, o = rows_of(t), 6 + t // 5, 100 * (t % 5)
                                last = pe.transpose(PS[0:r, bank, o:o + 100], T1[0:100, t * P:t * P + r], ident[0:100, 0:100])
                            last.then_inc(pe_once, 1)
                        if half and n == 27:
                            pe.wait_ge(gn_ready, 6)
                            pe.wait_ge(clf_in, 16 * NB * NPG)
                            for h in range(H):
                                last = pe.transpose(PS[:, 6, 64 * h:64 * h + 64], lf_rows[:, :].rearrange("n (p h) -> n p h", h=H)[:, :, h],
                                                    ident[0:NB * NPG, 0:NB * NPG])
                            last.then_inc(pe_once, 1)
                            pe.wait_ge(sq_ready, 9)
                            pe.matmul(PS[:, 7, 64:128], ones[:, :], ssq, start=True, stop=True).then_inc(ss_ready, 1)
                        if half and n == 28:
                            pe.wait_ge(dve_once, CLF_READY)
                            pe.wait_ge(sd_ready, 9)
                            lfs = clf[:, :, :, :].rearrange("p b j h -> p (b j h)")
                            pe.matmul(PS[:, 6, 0:256], strict[:, :], lfs, start=True, stop=True)
                            pe.matmul(PS[:, 6, 256:512], ones[:, :], lfs, start=True, stop=True)
                            pe.wait_ge(diag_ready, 1)
                            pe.matmul(PS[:, 7, 0:32], ones[0:NB, :], lf_diag.rearrange("p b h -> p (b h)"), start=True, stop=True)\
                              .then_inc(pe_once, 1)
                        pe.wait_ge(ready, n + 1)
                        w = (w_hi, w_lo)[half]
                        for k in range(KT):
                            for g in range(3):
                                for a in operands:
                                    last = pe.matmul(PS[:, b + g, 0:G3], w[:, n % 2, k, :],
                                                     a[:, k, g * G3:(g + 1) * G3],
                                                     start=(half == 0 and k == 0 and a is act_hi),
                                                     stop=(half == 1 and k == KT - 1))
                    last.then_inc(block_done, 1)
                i = n - 1 - NAT0
                if 0 <= i < 12:
                    pe.wait_ge(evacuated, n)
                    if i >= 1:
                        pe.wait_ge(nat_ready, i)
                    if 0 <= n - NS0 < 8:
                        pe.wait_ge(sd_ready, n - NS0 + 1)
                    src = kT[:, i, :] if i < 4 else cb[:, cb_use(n - 1) % 2, 3:3 + TOK]
                    for t in range(NT):
                        last = pe.transpose(PS[:, 6 + t // 4, (t % 4) * P:(t % 4 + 1) * P],
                                            src[:, t * P:(t + 1) * P], ident[:, :])
                    last.then_inc(nat_t, 1)

            pe.wait_ge(evacuated, NBLK)
            pe.wait_ge(conv_ready, 12)
            for c in range(12):
                last = pe.transpose(PS[0:11, c // 4, (c % 4) * P:(c % 4 + 1) * P], tail[:, c, :], ident[:, :])
            last.then_inc(pe_once, 1)
            pe.wait_ge(dve_once, CT_READY)
            pe.wait_ge(evacuated, NBLK)
            for i in range(12):
                src = (qT[:, i, SEQ:TOK] if i < 4 else kT[:, i - 4, SEQ:TOK] if i < 8 else vzS[:, i - 8, :])
                last = pe.transpose(PS[0:NB, i // 4, (i % 4) * P:(i % 4 + 1) * P], src, ident[:, :])
            last.then_inc(pe_once, 1)
            pe.wait_ge(dve_once, SN_READY)
            pe.wait_ge(dve_once, SN_READY)
            pe.wait_ge(normed, 9)
            pe.wait_ge(gn_ready, 6)
            def transpose_outputs(c0):
                for c in (c0, c0 + 1):
                    pe.wait_ge(m_ready, c + 1)
                    for h in range(H):
                        last = pe.transpose(heads(4 * (c % 2) + 3)[:, h, :], OO[c % 2][:, h, :], ident[:, :])
                    last.then_inc(mt_ready, 1)

            for c0 in range(0, NT, 2):
                for c in (c0, c0 + 1):
                    s, A = c % 2, 4 * (c % 2)
                    if c >= 2:
                        pe.wait_ge(vn_ready, c - 1)
                        pe.wait_ge(wt_ready, c - 1)
                        pe.wait_ge(s_ready, c - 1)
                        pe.wait_ge(oo_ready, c - 1)
                    for h in range(H):
                        last = pe.matmul(heads(A)[:, h, :], ident[64:68, 64 + h:65 + h].to_broadcast([4, P]), T1[64:68, chunk(c)],
                                         start=True, stop=True)
                    last.then_inc(gb_ready, 1)
                    for h in range(H):
                        pe.matmul(heads(A + 1)[:, h, :], cT[:, H + h, chunk(c)], cT[:, H + h, chunk(c)], start=True, stop=True)
                    for h in range(H):
                        pe.matmul(heads(A + 2)[:, h, :], cT[:, h, chunk(c)], cT[:, H + h, chunk(c)], start=True, stop=True)
                    for h in range(H):
                        last = pe.transpose(heads(A + 3)[:, h, :], cT[:, 2 * H + h, chunk(c)], ident[:, :])
                    last.then_inc(kk_ready, 1)
                for c in (c0, c0 + 1):
                    s, A = c % 2, 4 * (c % 2)
                    pe.wait_ge(l_ready, c + 1)
                    pe.wait_ge(qkd_ready, c + 1)
                    for h in range(H):
                        pe.transpose(heads(A + 1)[:, h, :], LL[s][:, h, :], ident[:, :])
                    for h in range(H):
                        last = pe.transpose(heads(A + 2)[:, h, :], QKD[s][:, h, :], ident[:, :])
                    last.then_inc(lt_t, 1)
                for l in range(1, LEVELS):
                    for c in (c0, c0 + 1):
                        s, A = c % 2, 4 * (c % 2)
                        if l == 1:
                            pe.wait_ge(x0_ready, c + 1)
                            pe.wait_ge(lt_ready, c + 1)
                            pe.wait_ge(eg_ready, c + 1)
                        else:
                            pe.wait_ge(x_ready, level_seq(c, l - 1))
                        for h in range(H):
                            last = pe.matmul(heads(A)[:, h, :], LT[s][:, h, :], XX[s][:, h, :], start=True, stop=True)
                        last.then_inc(y_ready, 1)
                    if l == 2:
                        for c in (c0, c0 + 1):
                            s, A = c % 2, 4 * (c % 2)
                            pe.wait_ge(bv_ready, c + 1)
                            for h in range(H):
                                last = pe.transpose(heads(A + 3)[:, h, :], cT[:, H + h, chunk(c)], ident[:, :])
                            last.then_inc(kn_ready, 1)
                    if c0 and l == 5:
                        transpose_outputs(c0 - 2)
                    for c in (c0, c0 + 1):
                        s, A = c % 2, 4 * (c % 2)
                        pe.wait_ge(ym_ready, level_seq(c, l))
                        if l == 1:
                            pe.wait_ge(xt0_ready, c + 1)
                            pe.wait_ge(qkt_ready, c + 1)
                        if l < LEVELS - 1:
                            for h in range(H):
                                pe.matmul(heads(A + 1)[:, h, :], XT[s][:, h, :], LL[s][:, h, :], start=True, stop=True)
                        for h in range(H):
                            last = pe.matmul(heads(A + 2)[:, h, :], LL[s][:, h, :], XT[s][:, h, :], start=True, stop=True)
                        last.then_inc(z_ready, 1)
                for c in (c0, c0 + 1):
                    s, A = c % 2, 4 * (c % 2)
                    pe.wait_ge(x_ready, level_seq(c, LEVELS - 1))
                    pe.wait_ge(rk_ready, c + 1)
                    for h in range(H):
                        last = pe.matmul(heads(A + 1)[:, h, :], RK[s][:, h, :], XT[s][:, h, :], start=True, stop=True)
                    last.then_inc(wt_t, 1)
                for c in (c0, c0 + 1):
                    s, A = c % 2, 4 * (c % 2)
                    for h in range(H):
                        last = pe.matmul(heads(A)[:, h, :], XT[s][:, h, :], BV[s][:, h, :], start=(h == 0), stop=(c == 0),
                                         skip_group_check=True)
                    pe.wait_ge(wt_ready, c + 1)
                    if c:
                        pe.wait_ge(s_ready, c)
                        for h in range(H):
                            last = pe.matmul(heads(A)[:, h, :], WT[s][:, h, :], ST[:, h, :], start=False, stop=True,
                                             skip_group_check=True)
                    last.then_inc(u_ready, 1)
                    pe.wait_ge(qg_ready, c + 1)
                    if c:
                        for h in range(H):
                            pe.matmul(heads(A + 2)[:, h, :], QG[s][:, h, :], ST[:, h, :], start=(h == 0), stop=False,
                                      skip_group_check=True)
                    pe.wait_ge(vn_ready, c + 1)
                    if c >= 2:
                        pe.wait_ge(mlo_ready, c - 1)
                    for h in range(H):
                        last = pe.matmul(heads(A + 3)[:, h, :], KG[s][:, h, :], VN[s][:, h, :], start=True, stop=True)
                    last.then_inc(s_add, 1)
                    for h in range(H):
                        last = pe.matmul(heads(A + 2)[:, h, :], QKT[s][:, h, :], VN[s][:, h, :], start=(c == 0 and h == 0), stop=True,
                                         skip_group_check=True)
                    last.then_inc(o_ready, 1)
            pe.wait_ge(diag_ready, 2)
            pe.wait_ge(vn_ready, NT)
            pe.wait_ge(wt_ready, NT)
            pe.matmul(PS[:, 5, 64:96], ones[0:NB, :], self_diag.rearrange("p b h -> p (b h)"), start=True, stop=True).then_inc(pe_once, 1)
            pe.wait_ge(dve_once, MX_READY)
            pe.transpose(PS[0:32, 4, 0:P], mx, ident[:, :]).then_inc(pe_once, 1)
            pe.wait_ge(dve_once, MD_READY)
            pe.matmul(PS[:, 5, 0:32], ones[0:32, :], mdiag, start=True, stop=True).then_inc(pe_once, 1)
            pe.wait_ge(dve_once, SJ_READY)
            pe.matmul(PS[:, 5, 32:64], ones[:, :], sj, start=True, stop=True).then_inc(pe_once, 1)
            transpose_outputs(NT - 2)
            pe.wait_ge(dve_once, PD_READY)

            pe.wait_ge(mlo_ready, NT)
            pe.wait_ge(m8_ready, 2)
            for i in range(16):
                src = cT[:, i, SEQ:TOK] if i < 12 else vzS[:, i - 8, :]
                last = pe.transpose(PS[0:NB, i // 4, (i % 4) * P:(i % 4 + 1) * P], src, ident[:, :])
            last.then_inc(pe_once, 1)
            pe.wait_ge(pool_once, AD_READY)
            pe.matmul(PS[:, 4, 0:32], ones[0:NB, :], a_diag.rearrange("p b h -> p (b h)"), start=True, stop=True).then_inc(pe_once, 1)
            pe.wait_ge(st_in, 16)
            pe.wait_ge(msk_ready, H)
            for h in range(H):
                for b in range(NB):
                    last = pe.matmul(PS[0:NB, 5, h * P:(h + 1) * P], msk[:, h, b, :], S_s[:, b * H + h, :], start=(b == 0),
                                     stop=(b == NB - 1))
            last.then_inc(pe_once, 1)
            pe.wait_ge(dve_once, DN_READY)
            for g in range(8):
                h, half = g // 2, g % 2
                pe.wait_ge(dmk_ready, h + 1)
                if g >= 4:
                    pe.wait_ge(st_ready, g - 3)
                pe.matmul(PS[:, g % 4, :], dN[:, H + h, :], dmk[:, h, 4 * half:4 * half + 4, :].rearrange("p b e -> p (b e)"),
                          start=True, stop=True).then_inc(outer_ready, 1)
            pe.wait_ge(st_ready, 8)
            pe.wait_ge(msk_ready, 2 * H)
            for h in range(H):
                for b in range(NB):
                    last = pe.matmul(PS[0:NB, 4, h * P:(h + 1) * P], msk[:, h, b, :], S_s[:, b * H + h, :], start=(b == 0),
                                     stop=(b == NB - 1))
            last.then_inc(pe_once, 1)

            pe.wait_ge(bias_ready, 1)
            for n in range(NAI + 4):
                if n < NAI:
                    i, h, w = n // H, n % H, P * (n // H + 1)
                    if n >= 2:
                        pe.wait_ge(p_ready, n - 1)
                    for g in range(0, w, 512):
                        e = min(g + 512, w)
                        out = PS[:, 2 * (n % 2) + g // 512, :]
                        pe.matmul(out[:, 0:e - g], qT[:, h, chunk(i)], kT[:, h, g:e], start=True, stop=False)
                        pe.matmul(out[:, 0:e - g], less[96:100, h, :], D_lo[96:100, g:e], start=False, stop=False)
                        if e == w:
                            pe.matmul(out[:, w - P - g:w - g], eye[:, :], neg[:, :], start=False, stop=False)
                        last = pe.matmul(out[:, 0:e - g], less[96:100, h, :], D_hi[96:100, g:e], start=False, stop=True)
                    last.then_inc(qk_ready, 1)
                if n == 1:
                    pe.wait_ge(dve_once, SM_READY)
                    for h in range(H):
                        last = pe.transpose(PS[:, 5, h * NB:(h + 1) * NB], dlt[:, h, :], ident[0:NB, 0:NB])
                    last.then_inc(pe_once, 1)
                    for h in range(H):
                        last = pe.transpose(PS[0:NB, 4, h * P:(h + 1) * P], vzS[:, h, :], ident[:, :])
                    last.then_inc(pe_once, 1)
                    pe.wait_ge(v_in, 16)
                    pe.wait_ge(dve_once, SMLO_READY)
                    pe.wait_ge(dv_ready, 1)
                m = n - 1
                if 0 <= m < NAI:
                    pe.wait_ge(p_ready, m + 1)
                    if m >= 1:
                        pe.wait_ge(pt_ready, m)
                    for k in range(m // H + 1):
                        last = pe.transpose(PS[:, 4 + k // 4, (k % 4) * P:(k % 4 + 1) * P], sc[:, m % 2, k * P:(k + 1) * P], ident[:, :])
                    last.then_inc(pt_t, 1)
                m = n - 2
                if 0 <= m < NAI:
                    i, h = m // H, m % H
                    pe.wait_ge(pt_ready, m + 1)
                    if h == 0 and i >= 2:
                        pe.wait_ge(dv_ready, i)
                    for k in range(i + 1):
                        last = pe.matmul(heads(6 + i % 2)[:, h, :], pT[:, m % 2, k, :], vN[:, k, h * P:(h + 1) * P],
                                         start=(k == 0), stop=(k == i))
                    last.then_inc(pv_ready, 1)
                if n >= H + 3 and (n - 3) % H == 0:
                    i = (n - 3) // H - 1
                    pe.wait_ge(on_ready, i + 1)
                    for h in range(H):
                        last = pe.transpose(heads(6 + i % 2)[:, h, :], oN[:, i % 2, h, :], ident[:, :])
                    last.then_inc(ot_ready, 1)
                if n % H == 0 and n >= 2 * H:
                    r = n // H - 1
                    pe.wait_ge(otlo_ready, r)
                    samples = [r - 1] if r < NT - 1 else [r - 1, r]
                    for b in samples:
                        pe.wait_ge(v_used, NPG * (b + 1))
                        last = pe.matmul(PS[0:NB, 7 - r % 2, :], m8[:, b, :], av[b % 3][:, :], start=(b == samples[0]), stop=(b == samples[-1]))
                    last.then_inc(dv_t, 1)
            pe.wait_ge(dv_ready, NT)
            for h in range(H):
                last = pe.transpose(PS[:, 4, h * NB:(h + 1) * NB], dv[:, h * P:(h + 1) * P], ident[0:NB, 0:NB])
            last.then_inc(pe_once, 1)

            for t in range(NT9 + 1):
                if t < NT9:
                    r, b = rows_of(t), 2 * (t % 2)
                    cs = slice(t * P, t * P + r)
                    if t < NT:
                        pe.wait_ge(otlo_ready, t + 1)
                    else:
                        pe.wait_ge(dve_once, DOLO_READY)
                    if t >= 2:
                        pe.wait_ge(h_ready, t - 1)
                    for k in range(KT):
                        if t == 0:
                            pe.wait_ge(wo_lo_ready, k + 1)
                        for a, w in ((act_hi, wo_hi), (act_hi, wo_lo), (act_lo, wo_hi)):
                            for f in range(2):
                                last = pe.matmul(PS[0:r, b + f, :], a[:, k, cs], w[:, k, f * 512:(f + 1) * 512],
                                                 start=(k == 0 and a is act_hi and w is wo_hi), stop=(k == KT - 1 and a is act_lo))
                    last.then_inc(h_t, 1)
                if t >= 1:
                    u, r = t - 1, rows_of(t - 1)
                    pe.wait_ge(xm_ready, u + 1)
                    if u >= 2:
                        pe.wait_ge(a2lo_ready, u - 1)
                    for k in range(KT):
                        last = pe.transpose(PS[:, 4 + 2 * (u % 2) + k // 4, (k % 4) * P:(k % 4) * P + r],
                                            xm[0:r, u % 2, k * P:(k + 1) * P], ident[0:r, 0:r])
                    last.then_inc(xmt_ready, 1)
            pe.wait_ge(lo_done, 5)

            def pe_group(g, last_group):
                for k in range(GB):
                    b = 3 * (k % 2)
                    pe.wait_ge(lo_done, 8 * g + 2 * k + 4)
                    pe.wait_ge(relu_done, GB * g + k + 1)
                    if k == 0:
                        pe.wait_ge(y_add, NT9 * g + 1)
                        for f in range(3):
                            pe.wait_ge(a2lo_ready, min(NT9, ((f + 1) * G3 + P - 1) // P))
                            for w, operands in ((wu_hi, (act_hi, act_lo)), (wu_lo, (act_hi,))):
                                for kt in range(KT):
                                    for a in operands:
                                        last = pe.matmul(PS[:, f, 0:G3], w[:, 0, kt, :], a[:, kt, f * G3:(f + 1) * G3],
                                                         start=(w is wu_hi and kt == 0 and a is act_hi), stop=(w is wu_lo and kt == KT - 1))
                    else:
                        for w, operands in ((wu_hi, (act_hi, act_lo)), (wu_lo, (act_hi,))):
                            for kt in range(KT):
                                for f in range(3):
                                    for a in operands:
                                        last = pe.matmul(PS[:, b + f, 0:G3], w[:, k % 2, kt, :], a[:, kt, f * G3:(f + 1) * G3],
                                                         start=(w is wu_hi and kt == 0 and a is act_hi), stop=(w is wu_lo and kt == KT - 1))
                    last.then_inc(up_done, 1)

                def down(t, ks):
                    r, b = rows_of(t), 0 if t % 2 else 6
                    cs = slice(t * P, t * P + r)
                    for k in ks:
                        if t == 0:
                            pe.wait_ge(u_lo_done, GB * g + k + 2)
                            pe.wait_ge(lo_done, 8 * g + 2 * k + 7 - (last_group and k == 3))
                        for a, w in ((u_hi, wd_hi), (u_hi, wd_lo), (u_lo, wd_hi)):
                            for f in range(2):
                                last = pe.matmul(PS[0:r, b + f, :], a[:, k, cs], w[:, k, f * 512:(f + 1) * 512],
                                                 start=(k == 0 and a is u_hi and w is wd_hi), stop=(k == GB - 1 and a is u_lo))
                    if ks[-1] == GB - 1:
                        last.then_inc(dn_tile, 1)

                pe.wait_ge(y_add, NT9 * g + 2)
                down(0, range(GB - 1))
                pe.wait_ge(relu_done, GB * g + 5)
                down(1, range(GB - 1))
                down(0, (GB - 1,))
                down(1, (GB - 1,))
                for t in range(2, NT9):
                    pe.wait_ge(y_add, NT9 * g + t + 1)
                    down(t, range(GB))

            with pe.Fori(0, NG - 1) as g:
                pe_group(g, False)
            pe_group(NG - 1, True)


_INS = ("x_prompt", "x_sample", "cache_k", "cache_v", "cache_lf", "page_table", "state_conv", "state_ssm", "ln1", "w_in", "b_f",
        "w_conv", "a_log", "dt_bias", "w_gnorm", "w_o", "ln2", "w_up", "w_down", "ln_f")
_OUTS = ((1, SEQ, D), (NB, 1, D),
         (1, 1, SEQ, H, HD), (1, 1, SEQ, H, HD), (1, 1, SEQ, H), (1, 1, CW - 1, CONV), (1, 1, H, HD, HD),
         (1, NB, 1, H, HD), (1, NB, 1, H, HD), (1, NB, 1, H), (1, NB, CW - 1, CONV), (1, NB, H, HD, HD))


def kernel(**inputs):
    import numpy as _np
    import concourse.bacc as _bacc
    from concourse.bass_utils import run_bass_kernel_spmd as _run

    nc = _bacc.Bacc("TRN2", target_bir_lowering=False, num_devices=1)
    arrays, args = {}, []
    for name in _INS:
        a = _np.ascontiguousarray(inputs[name])
        arrays[f"in_{name}"] = a
        args.append(nc.dram_tensor(f"in_{name}", a.shape, mybir.dt.from_np(a.dtype), kind="ExternalInput").ap())
    for i, shape in enumerate(_OUTS):
        args.append(nc.dram_tensor(f"out_{i}", shape, F32, kind="ExternalOutput").ap())
    hymba_step(nc, *args)
    r = _run(nc, [arrays], core_ids=[0])
    return tuple(r.results[0][f"out_{i}"] for i in range(len(_OUTS)))
```
